# Optimizing a Trainium2 kernel written in Bass

```python
import jax, jax.numpy as jnp
from jax import lax
import numpy as np

D_MODEL = 1024
BATCH = 1
SEQ = 256
DEPTH = 2

N_MIXERS = 2
N_POOL_LAYERS = (DEPTH + 1) // 2
N_MLA_LAYERS = DEPTH // 2

POOL_WINDOWS = (2, 4, 8, 16)
N_POOL_GROUPS = len(POOL_WINDOWS)
POOL_GROUP = D_MODEL // N_POOL_GROUPS

N_HEADS = D_MODEL // 128
QK_NOPE_DIM = 128
QK_ROPE_DIM = 64
V_HEAD_DIM = 128
Q_LORA_RANK = 3 * D_MODEL // 8
KV_LORA_RANK = D_MODEL // 8
QK_HEAD_DIM = QK_NOPE_DIM + QK_ROPE_DIM
ROPE_THETA = 10000.0
Q_BLOCK = 128

D_FF = ((8 * D_MODEL // 3 + 255) // 256) * 256

RMS_EPS = 1e-6


def rms_norm(x, g):
    xf = x.astype(jnp.float32)
    y = xf * lax.rsqrt(jnp.mean(xf * xf, axis=-1, keepdims=True) + RMS_EPS)
    return (y * g.astype(jnp.float32)).astype(x.dtype)

def pool_mixer(h, w, scale):
    B, S, D = h.shape
    hf = h.astype(jnp.float32).reshape(B, S, N_POOL_GROUPS, POOL_GROUP)
    cs = jnp.cumsum(hf, axis=1)
    n_avail = jnp.arange(1, S + 1, dtype=jnp.float32)
    outs = []
    for g, win in enumerate(POOL_WINDOWS):
        c = cs[:, :, g]
        lag = jnp.pad(c[:, :-win], ((0, 0), (win, 0), (0, 0)))
        mean = (c - lag) / jnp.minimum(n_avail, float(win))[:, None]
        outs.append(mean - hf[:, :, g])
    p = jnp.stack(outs, axis=2).astype(h.dtype)
    y = jnp.einsum('bsgc,gcd->bsgd', p, w).reshape(B, S, D)
    return y * scale

def rope_tables(positions):
    inv = 1.0 / (ROPE_THETA ** (jnp.arange(0, QK_ROPE_DIM, 2, dtype=jnp.float32) / QK_ROPE_DIM))
    ang = positions.astype(jnp.float32)[..., None] * inv
    return jnp.cos(ang), jnp.sin(ang)

def apply_rope(x, cos, sin):
    xf = x.astype(jnp.float32)
    half = QK_ROPE_DIM // 2
    x1, x2 = xf[..., :half], xf[..., half:]
    return jnp.concatenate([x1 * cos - x2 * sin, x2 * cos + x1 * sin], axis=-1).astype(x.dtype)

def causal_attention(q, k, v):
    B, S, H, Dq = q.shape
    nb = S // Q_BLOCK
    qb = q.reshape(B, nb, Q_BLOCK, H, Dq).transpose(1, 0, 2, 3, 4)
    key_pos = jnp.arange(S)
    sm_scale = Dq ** -0.5

    def one_block(args):
        blk, qi = args
        s = jnp.einsum('bqhd,bkhd->bhqk', qi, k).astype(jnp.float32) * sm_scale
        q_pos = blk * Q_BLOCK + jnp.arange(Q_BLOCK)
        mask = key_pos[None, :] <= q_pos[:, None]
        s = jnp.where(mask, s, -jnp.inf)
        p = jax.nn.softmax(s, axis=-1).astype(v.dtype)
        return jnp.einsum('bhqk,bkhd->bqhd', p, v)

    o = lax.map(one_block, (jnp.arange(nb), qb))
    return o.transpose(1, 0, 2, 3, 4).reshape(B, S, H, v.shape[-1])

def mla(h, cos, sin, w_down, q_norm, w_uq, kv_norm, w_ukv, w_o):
    B, S, _ = h.shape
    d = h @ w_down
    cq = rms_norm(d[..., :Q_LORA_RANK], q_norm)
    ckv = rms_norm(d[..., Q_LORA_RANK:Q_LORA_RANK + KV_LORA_RANK], kv_norm)
    k_rope = apply_rope(d[..., Q_LORA_RANK + KV_LORA_RANK:], cos, sin)
    q = (cq @ w_uq).reshape(B, S, N_HEADS, QK_HEAD_DIM)
    q_rope = apply_rope(q[..., QK_NOPE_DIM:], cos[:, :, None], sin[:, :, None])
    q = jnp.concatenate([q[..., :QK_NOPE_DIM], q_rope], axis=-1)
    kv = (ckv @ w_ukv).reshape(B, S, N_HEADS, QK_NOPE_DIM + V_HEAD_DIM)
    k = jnp.concatenate(
        [kv[..., :QK_NOPE_DIM],
         jnp.broadcast_to(k_rope[:, :, None, :], (B, S, N_HEADS, QK_ROPE_DIM))], axis=-1)
    v = kv[..., QK_NOPE_DIM:]
    o = causal_attention(q, k, v)
    return o.reshape(B, S, N_HEADS * V_HEAD_DIM) @ w_o

def swiglu(h, w_gate, w_up, w_down):
    return (jax.nn.silu(h @ w_gate) * (h @ w_up)) @ w_down

def first_inputs(seed: int = 0) -> dict:
    key = jax.random.key(seed)
    ks = jax.random.split(key, 16)
    f32 = jnp.float32

    def nrm(k, shape, fan_in):
        return jax.random.normal(k, shape, f32) * (fan_in ** -0.5)

    def gain(k, shape):
        return 1.0 + 0.02 * jax.random.normal(k, shape, f32)

    x = jax.random.normal(ks[0], (BATCH, SEQ, D_MODEL), f32)
    positions = jnp.broadcast_to(jnp.arange(SEQ, dtype=jnp.int32)[None, :], (BATCH, SEQ))
    return {
        "x": x,
        "positions": positions,
        "norm_mix": gain(ks[1], (DEPTH, D_MODEL)),
        "norm_ffn": gain(ks[2], (DEPTH, D_MODEL)),
        "norm_final": gain(ks[3], (D_MODEL,)),
        "pool_w": nrm(ks[4], (N_POOL_LAYERS, N_POOL_GROUPS, POOL_GROUP, POOL_GROUP), POOL_GROUP),
        "pool_scale": gain(ks[5], (N_POOL_LAYERS, D_MODEL)),
        "mla_w_down": nrm(ks[6], (N_MLA_LAYERS, D_MODEL, Q_LORA_RANK + KV_LORA_RANK + QK_ROPE_DIM), D_MODEL),
        "mla_q_norm": gain(ks[7], (N_MLA_LAYERS, Q_LORA_RANK)),
        "mla_w_uq": nrm(ks[8], (N_MLA_LAYERS, Q_LORA_RANK, N_HEADS * QK_HEAD_DIM), Q_LORA_RANK),
        "mla_kv_norm": gain(ks[9], (N_MLA_LAYERS, KV_LORA_RANK)),
        "mla_w_ukv": nrm(ks[10], (N_MLA_LAYERS, KV_LORA_RANK, N_HEADS * (QK_NOPE_DIM + V_HEAD_DIM)), KV_LORA_RANK),
        "mla_w_o": nrm(ks[11], (N_MLA_LAYERS, N_HEADS * V_HEAD_DIM, D_MODEL), N_HEADS * V_HEAD_DIM),
        "ffn_w_gate": nrm(ks[12], (DEPTH, D_MODEL, D_FF), D_MODEL),
        "ffn_w_up": nrm(ks[13], (DEPTH, D_MODEL, D_FF), D_MODEL),
        "ffn_w_down": nrm(ks[14], (DEPTH, D_FF, D_MODEL), D_FF),
    }

def first_block(x, positions, norm_mix, norm_ffn, norm_final, pool_w, pool_scale,
              mla_w_down, mla_q_norm, mla_w_uq, mla_kv_norm, mla_w_ukv, mla_w_o,
              ffn_w_gate, ffn_w_up, ffn_w_down):
    cos, sin = rope_tables(positions)
    for i in range(DEPTH):
        h = rms_norm(x, norm_mix[i])
        j = i // N_MIXERS
        if i % N_MIXERS == 0:
            x = x + pool_mixer(h, pool_w[j], pool_scale[j])
        else:
            x = x + mla(h, cos, sin, mla_w_down[j], mla_q_norm[j], mla_w_uq[j],
                        mla_kv_norm[j], mla_w_ukv[j], mla_w_o[j])
        h = rms_norm(x, norm_ffn[i])
        x = x + swiglu(h, ffn_w_gate[i], ffn_w_up[i], ffn_w_down[i])
    return rms_norm(x, norm_final)


DEPTH_2 = 1

MEM_LEN = 256
NSA_HEADS = 8
NSA_KV_HEADS = 2
NSA_HEAD_DIM = 64
NSA_REP = NSA_HEADS // NSA_KV_HEADS
CMP_BLOCK = 32
CMP_STRIDE = 16
SEL_BLOCK = 64
N_SELECT = 16
WINDOW = 512
NSA_WIDTH = NSA_HEADS * NSA_HEAD_DIM
KV_WIDTH = NSA_KV_HEADS * NSA_HEAD_DIM
GMLP_WIDTH = 256
GMLP_GROUPS = 4
GMLP_CHUNK = 128
CONV_WIDTH = 256
CONV_TAPS = 31
MIX_WIDTH = NSA_WIDTH + GMLP_WIDTH + CONV_WIDTH
IN_SPLITS = (NSA_WIDTH, KV_WIDTH, KV_WIDTH, KV_WIDTH, KV_WIDTH, KV_WIDTH, KV_WIDTH,
             NSA_HEADS * 3, 2 * GMLP_WIDTH, 2 * CONV_WIDTH)
IN_WIDTH = sum(IN_SPLITS)
XATTN_HEADS = 4
XATTN_HEAD_DIM = D_MODEL // XATTN_HEADS
D_FF_2 = 2816
FFN_CONV_TAPS = 3

EPS = 1e-6
NEG_INF = -1e30
TINY = 1e-30
FORCE = 1e4


def _split_cols(z, widths):
    outs, off = [], 0
    for w in widths:
        outs.append(z[..., off:off + w])
        off += w
    return outs

def rms_norm_2(x, g):
    xf = x.astype(jnp.float32)
    y = xf * lax.rsqrt(jnp.mean(xf * xf, axis=-1, keepdims=True) + EPS)
    return (y * g.astype(jnp.float32)).astype(x.dtype)

def layer_norm(x, g, b):
    xf = x.astype(jnp.float32)
    mu = jnp.mean(xf, axis=-1, keepdims=True)
    var = jnp.mean(jnp.square(xf - mu), axis=-1, keepdims=True)
    y = (xf - mu) * lax.rsqrt(var + EPS)
    return (y * g.astype(jnp.float32) + b.astype(jnp.float32)).astype(x.dtype)

def masked_softmax(s, mask):
    s = jnp.where(mask, s, NEG_INF)
    m = jnp.max(s, axis=-1, keepdims=True)
    e = jnp.where(mask, jnp.exp(s - m), 0.0)
    return e / jnp.maximum(jnp.sum(e, axis=-1, keepdims=True), TINY)

def causal_depthwise_conv(x, w, b):
    taps = w.shape[0]
    y = lax.conv_general_dilated(x, w[:, None, :], window_strides=(1,), padding=[(taps - 1, 0)],
                                 dimension_numbers=("NWC", "WIO", "NWC"),
                                 feature_group_count=x.shape[-1])
    return y + b

def _to_heads(z, n):
    b, s, _ = z.shape
    return z.reshape(b, s, n, NSA_HEAD_DIM).transpose(0, 2, 1, 3)

def compress_blocks(kv, pe, w1, w2):
    b, g, s, dh = kv.shape
    n_cmp = (s - CMP_BLOCK) // CMP_STRIDE + 1
    idx = jnp.arange(n_cmp)[:, None] * CMP_STRIDE + jnp.arange(CMP_BLOCK)[None, :]
    blocks = kv[:, :, idx, :] + pe
    flat = blocks.reshape(b, g, n_cmp, CMP_BLOCK * dh)
    return jax.nn.gelu(flat @ w1) @ w2

def nsa_mixer(q, k_c_raw, v_c_raw, k_s, v_s, k_w, v_w, gate_logits, cmp_pe, cmp_w1, cmp_w2):
    b, s, _ = q.shape
    dh, G, R = NSA_HEAD_DIM, NSA_KV_HEADS, NSA_REP
    scale = dh ** -0.5
    k_cmp = compress_blocks(_to_heads(k_c_raw, G), cmp_pe[0], cmp_w1[0], cmp_w2[0])
    v_cmp = compress_blocks(_to_heads(v_c_raw, G), cmp_pe[1], cmp_w1[1], cmp_w2[1])
    n_cmp = k_cmp.shape[2]
    cmp_end = jnp.arange(n_cmp) * CMP_STRIDE + CMP_BLOCK - 1
    n_slc = s // SEL_BLOCK
    k_sel = min(N_SELECT, n_slc)
    k_slc_b = _to_heads(k_s, G).reshape(b, G, n_slc, SEL_BLOCK, dh)
    v_slc_b = _to_heads(v_s, G).reshape(b, G, n_slc, SEL_BLOCK, dh)
    ci = jnp.arange(n_cmp)[:, None] * CMP_STRIDE
    sj = jnp.arange(n_slc)[None, :] * SEL_BLOCK
    overlap = ((ci < sj + SEL_BLOCK) & (ci + CMP_BLOCK > sj)).astype(jnp.float32)
    pad = ((0, 0), (0, 0), (WINDOW, 0), (0, 0))
    k_win_p = jnp.pad(_to_heads(k_w, G), pad)
    v_win_p = jnp.pad(_to_heads(v_w, G), pad)
    nb = s // Q_BLOCK
    q_blocks = q.reshape(b, nb, Q_BLOCK, G, R, dh).transpose(1, 0, 3, 4, 2, 5)
    gather = jax.vmap(jax.vmap(lambda kb, ix: kb[ix]))

    def block_fn(args):
        qb, bi = args
        t = bi * Q_BLOCK + jnp.arange(Q_BLOCK)
        s_c = jnp.einsum("bgrtd,bgnd->bgrtn", qb, k_cmp).astype(jnp.float32) * scale
        p_c = masked_softmax(s_c, cmp_end[None, :] <= t[:, None])
        o_c = jnp.einsum("bgrtn,bgnd->bgrtd", p_c.astype(v_cmp.dtype), v_cmp)
        imp = jnp.einsum("bgtn,nj->bgtj", jnp.sum(p_c, axis=2), overlap)
        cur = (t // SEL_BLOCK)[:, None]
        jj = jnp.arange(n_slc)[None, :]
        forced = (jj == 0) | (jj == cur) | (jj == cur - 1)
        imp = jnp.where(forced, FORCE, imp)
        imp = jnp.where(jj <= cur, imp, -FORCE)
        _, sel = lax.top_k(imp, k_sel)
        gk = gather(k_slc_b, sel).reshape(b, G, Q_BLOCK, k_sel * SEL_BLOCK, dh)
        gv = gather(v_slc_b, sel).reshape(b, G, Q_BLOCK, k_sel * SEL_BLOCK, dh)
        kpos = (sel[..., None] * SEL_BLOCK + jnp.arange(SEL_BLOCK)).reshape(b, G, Q_BLOCK, k_sel * SEL_BLOCK)
        mask_s = (kpos <= t[None, None, :, None])[:, :, None]
        s_s = jnp.einsum("bgrtd,bgtmd->bgrtm", qb, gk).astype(jnp.float32) * scale
        p_s = masked_softmax(s_s, mask_s)
        o_s = jnp.einsum("bgrtm,bgtmd->bgrtd", p_s.astype(gv.dtype), gv)
        kw = lax.dynamic_slice_in_dim(k_win_p, bi * Q_BLOCK, Q_BLOCK + WINDOW, axis=2)
        vw = lax.dynamic_slice_in_dim(v_win_p, bi * Q_BLOCK, Q_BLOCK + WINDOW, axis=2)
        kp = (bi * Q_BLOCK - WINDOW + jnp.arange(Q_BLOCK + WINDOW))[None, :]
        mask_w = (kp <= t[:, None]) & (kp > t[:, None] - WINDOW) & (kp >= 0)
        s_w = jnp.einsum("bgrtd,bgkd->bgrtk", qb, kw).astype(jnp.float32) * scale
        p_w = masked_softmax(s_w, mask_w)
        o_w = jnp.einsum("bgrtk,bgkd->bgrtd", p_w.astype(vw.dtype), vw)
        return o_c, o_s, o_w

    o_c, o_s, o_w = lax.map(block_fn, (q_blocks, jnp.arange(nb)))
    def unblock(o):
        return o.transpose(1, 0, 4, 2, 3, 5).reshape(b, s, NSA_HEADS, dh)
    gates = jax.nn.sigmoid(gate_logits.reshape(b, s, NSA_HEADS, 3))
    o = (gates[..., 0:1] * unblock(o_c) + gates[..., 1:2] * unblock(o_s)
         + gates[..., 2:3] * unblock(o_w))
    return o.reshape(b, s, NSA_WIDTH)

def gmlp_mixer(z, ln_g, ln_b, w_s, b_s):
    b, s, _ = z.shape
    z = jax.nn.gelu(z)
    u, v = z[..., :GMLP_WIDTH], z[..., GMLP_WIDTH:]
    v = layer_norm(v, ln_g, ln_b)
    nc = s // GMLP_CHUNK
    v = v.reshape(b, nc, GMLP_CHUNK, GMLP_GROUPS, GMLP_WIDTH // GMLP_GROUPS)
    causal = jnp.tril(jnp.ones((GMLP_CHUNK, GMLP_CHUNK), dtype=w_s.dtype))
    mixed = jnp.einsum("gts,bcsgd->bctgd", w_s * causal, v) + b_s.T[:, :, None]
    return u * mixed.reshape(b, s, GMLP_WIDTH)

def conformer_conv_mixer(z, dw_w, dw_b, ln_g, ln_b):
    a, gt = z[..., :CONV_WIDTH], z[..., CONV_WIDTH:]
    h = a * jax.nn.sigmoid(gt)
    h = causal_depthwise_conv(h, dw_w, dw_b)
    h = layer_norm(h, ln_g, ln_b)
    return jax.nn.silu(h)

def memory_cross_attention(x, mem, g_x, g_m, wq, wk, wv, wo):
    b, s, _ = x.shape
    h = rms_norm_2(x, g_x)
    m = rms_norm_2(mem, g_m)
    q = (h @ wq).reshape(b, s, XATTN_HEADS, XATTN_HEAD_DIM)
    k = (m @ wk).reshape(b, m.shape[1], XATTN_HEADS, XATTN_HEAD_DIM)
    v = (m @ wv).reshape(b, m.shape[1], XATTN_HEADS, XATTN_HEAD_DIM)
    sc = jnp.einsum("bshd,bmhd->bhsm", q, k).astype(jnp.float32) * (XATTN_HEAD_DIM ** -0.5)
    p = jax.nn.softmax(sc, axis=-1)
    o = jnp.einsum("bhsm,bmhd->bshd", p.astype(v.dtype), v).reshape(b, s, D_MODEL)
    return o @ wo

def conv_ffn(x, g, w_up, dw_w, dw_b, w_down):
    h = causal_depthwise_conv(rms_norm_2(x, g) @ w_up, dw_w, dw_b)
    gate, up = h[..., :D_FF_2], h[..., D_FF_2:]
    return (jax.nn.silu(gate) * up) @ w_down

def second_inputs(seed: int = 0) -> dict:
    key = jax.random.key(seed)
    ks = iter(jax.random.split(key, 40))
    def nrm(shape, scale):
        return jax.random.normal(next(ks), shape, jnp.float32) * scale
    def gain(shape):
        return 1.0 + 0.02 * jax.random.normal(next(ks), shape, jnp.float32)
    L, dh = DEPTH_2, NSA_HEAD_DIM
    return {
        "x": nrm((BATCH, SEQ, D_MODEL), 1.0),
        "mem": nrm((BATCH, MEM_LEN, D_MODEL), 1.0),
        "mix_norm_g": gain((L, D_MODEL)),
        "w_in": nrm((L, D_MODEL, IN_WIDTH), D_MODEL ** -0.5),
        "cmp_pe": nrm((L, 2, CMP_BLOCK, dh), 0.1),
        "cmp_w1": nrm((L, 2, CMP_BLOCK * dh, dh), (CMP_BLOCK * dh) ** -0.5),
        "cmp_w2": nrm((L, 2, dh, dh), dh ** -0.5),
        "gmlp_ln_g": gain((L, GMLP_WIDTH)),
        "gmlp_ln_b": nrm((L, GMLP_WIDTH), 0.02),
        "gmlp_ws": nrm((L, GMLP_GROUPS, GMLP_CHUNK, GMLP_CHUNK), GMLP_CHUNK ** -0.5),
        "gmlp_bs": gain((L, GMLP_GROUPS, GMLP_CHUNK)),
        "conv_dw_w": nrm((L, CONV_TAPS, CONV_WIDTH), CONV_TAPS ** -0.5),
        "conv_dw_b": nrm((L, CONV_WIDTH), 0.02),
        "conv_ln_g": gain((L, CONV_WIDTH)),
        "conv_ln_b": nrm((L, CONV_WIDTH), 0.02),
        "mix_out_g": gain((L, MIX_WIDTH)),
        "w_out": nrm((L, MIX_WIDTH, D_MODEL), MIX_WIDTH ** -0.5),
        "xattn_norm_g": gain((L, D_MODEL)),
        "mem_norm_g": gain((L, D_MODEL)),
        "xattn_wq": nrm((L, D_MODEL, D_MODEL), D_MODEL ** -0.5),
        "xattn_wk": nrm((L, D_MODEL, D_MODEL), D_MODEL ** -0.5),
        "xattn_wv": nrm((L, D_MODEL, D_MODEL), D_MODEL ** -0.5),
        "xattn_wo": nrm((L, D_MODEL, D_MODEL), D_MODEL ** -0.5),
        "ffn_norm_g": gain((L, D_MODEL)),
        "ffn_w_up": nrm((L, D_MODEL, 2 * D_FF_2), D_MODEL ** -0.5),
        "ffn_dw_w": nrm((L, FFN_CONV_TAPS, 2 * D_FF_2), FFN_CONV_TAPS ** -0.5),
        "ffn_dw_b": nrm((L, 2 * D_FF_2), 0.02),
        "ffn_w_down": nrm((L, D_FF_2, D_MODEL), D_FF_2 ** -0.5),
        "final_norm_g": gain((D_MODEL,)),
    }

def second_block(x, mem, mix_norm_g, w_in, cmp_pe, cmp_w1, cmp_w2, gmlp_ln_g, gmlp_ln_b, gmlp_ws,
              gmlp_bs, conv_dw_w, conv_dw_b, conv_ln_g, conv_ln_b, mix_out_g, w_out,
              xattn_norm_g, mem_norm_g, xattn_wq, xattn_wk, xattn_wv, xattn_wo,
              ffn_norm_g, ffn_w_up, ffn_dw_w, ffn_dw_b, ffn_w_down, final_norm_g):
    for l in range(DEPTH_2):
        z = rms_norm_2(x, mix_norm_g[l]) @ w_in[l]
        (q, kc, vc, ks, vs, kw, vw, gl, zg, zc) = _split_cols(z, IN_SPLITS)
        y_nsa = nsa_mixer(q, kc, vc, ks, vs, kw, vw, gl, cmp_pe[l], cmp_w1[l], cmp_w2[l])
        y_gmlp = gmlp_mixer(zg, gmlp_ln_g[l], gmlp_ln_b[l], gmlp_ws[l], gmlp_bs[l])
        y_conv = conformer_conv_mixer(zc, conv_dw_w[l], conv_dw_b[l], conv_ln_g[l], conv_ln_b[l])
        g_nsa, g_gmlp, g_conv = _split_cols(mix_out_g[l], (NSA_WIDTH, GMLP_WIDTH, CONV_WIDTH))
        y = jnp.concatenate([rms_norm_2(y_nsa, g_nsa), rms_norm_2(y_gmlp, g_gmlp),
                             rms_norm_2(y_conv, g_conv)], axis=-1)
        x = x + y @ w_out[l]
        x = x + memory_cross_attention(x, mem, xattn_norm_g[l], mem_norm_g[l], xattn_wq[l],
                                       xattn_wk[l], xattn_wv[l], xattn_wo[l])
        x = x + conv_ffn(x, ffn_norm_g[l], ffn_w_up[l], ffn_dw_w[l], ffn_dw_b[l], ffn_w_down[l])
    return rms_norm_2(x, final_norm_g)


def setup_inputs(seed=0):
    out = dict(first_inputs(seed))
    for name, value in second_inputs(seed + 1).items():
        if name != "x":
            out[name + "_2"] = value
    return out


def reference(
    x, positions, norm_mix, norm_ffn, norm_final, pool_w, pool_scale, mla_w_down, mla_q_norm,
    mla_w_uq, mla_kv_norm, mla_w_ukv, mla_w_o, ffn_w_gate, ffn_w_up, ffn_w_down, mem_2,
    mix_norm_g_2, w_in_2, cmp_pe_2, cmp_w1_2, cmp_w2_2, gmlp_ln_g_2, gmlp_ln_b_2, gmlp_ws_2,
    gmlp_bs_2, conv_dw_w_2, conv_dw_b_2, conv_ln_g_2, conv_ln_b_2, mix_out_g_2, w_out_2,
    xattn_norm_g_2, mem_norm_g_2, xattn_wq_2, xattn_wk_2, xattn_wv_2, xattn_wo_2, ffn_norm_g_2,
    ffn_w_up_2, ffn_dw_w_2, ffn_dw_b_2, ffn_w_down_2, final_norm_g_2,
):
    x = first_block(
        x, positions, norm_mix, norm_ffn, norm_final, pool_w, pool_scale, mla_w_down,
        mla_q_norm, mla_w_uq, mla_kv_norm, mla_w_ukv, mla_w_o, ffn_w_gate, ffn_w_up, ffn_w_down,
    )
    return second_block(
        x, mem_2, mix_norm_g_2, w_in_2, cmp_pe_2, cmp_w1_2, cmp_w2_2, gmlp_ln_g_2, gmlp_ln_b_2,
        gmlp_ws_2, gmlp_bs_2, conv_dw_w_2, conv_dw_b_2, conv_ln_g_2, conv_ln_b_2, mix_out_g_2,
        w_out_2, xattn_norm_g_2, mem_norm_g_2, xattn_wq_2, xattn_wk_2, xattn_wv_2, xattn_wo_2,
        ffn_norm_g_2, ffn_w_up_2, ffn_dw_w_2, ffn_dw_b_2, ffn_w_down_2, final_norm_g_2,
    )


_drawn_inputs = setup_inputs


def setup_inputs(seed=0):
    import zlib

    import numpy as np

    out = dict(_drawn_inputs(seed))
    spreads = {}
    factors = {'norm_mix': 2.823,
     'norm_ffn': 2.699,
     'pool_scale': 2.942,
     'mla_q_norm': 8.0,
     'mla_kv_norm': 8.0,
     'mix_norm_g_2': 3.068,
     'gmlp_ln_g_2': 8.0,
     'gmlp_ln_b_2': 8.0,
     'gmlp_bs_2': 8.0,
     'conv_dw_b_2': 3.306,
     'conv_ln_g_2': 5.937,
     'conv_ln_b_2': 7.751,
     'mix_out_g_2': 3.68,
     'xattn_norm_g_2': 8.0,
     'mem_norm_g_2': 8.0,
     'ffn_norm_g_2': 4.936,
     'ffn_dw_b_2': 5.005,
     'final_norm_g_2': 2.894}
    for name, (base, spread) in spreads.items():
        noise = np.random.default_rng([zlib.crc32(name.encode()), seed]).standard_normal(out[name].shape)
        drawn = base * np.exp(spread * noise) if base else spread * noise
        out[name] = __import__('jax').numpy.asarray(drawn.astype(out[name].dtype))
    for name, factor in factors.items():
        out[name] = (out[name] * factor).astype(out[name].dtype)
    return out
```

```python
from contextlib import ExitStack

import numpy as np

import concourse.bass as bass
from concourse import mybir

F32 = mybir.dt.float32
F32R = mybir.dt.float32r
I32 = mybir.dt.int32
ACT = mybir.ActivationFunctionType
ALU = mybir.AluOpType
AX = mybir.AxisListType

P = 128
SEQ = 256
NT = SEQ // P
D = 1024
KD = D // P
HALF = 512
EPS = 1e-6
NEG = -1e30
TINY = 1e-30

POOL_WINDOWS = (2, 4, 8, 16)
NG = len(POOL_WINDOWS)
EDGE = max(POOL_WINDOWS)

HEADS = 8
NOPE = 128
ROPE = 64
QLR = 384
KVR = 128
MLA_DOWN = QLR + KVR + ROPE
MLA_SCALE = float(NOPE + ROPE) ** -0.5

FF = 2816
STEPS = FF // P
LOOPED = 18

NSA_HEADS = 8
DH = 64
GROUPS = 2
REP = NSA_HEADS // GROUPS
NSA_SCALE = float(DH) ** -0.5
CMP_BLOCK = 32
CMP_STRIDE = 16
NCMP = (SEQ - CMP_BLOCK) // CMP_STRIDE + 1
CMP_KT = CMP_BLOCK * DH // P
GW = 256
GG = 4
CW_ = 256
TAPS = 31
PAD = TAPS - 1
FTAPS = 3
XHEADS = 4
XHD = D // XHEADS
XSCALE = float(XHD) ** -0.5
GELU_C = 0.044715
GELU_S = float(np.sqrt(2.0 / np.pi))

C_MIX0, C_MIX1, C_FFN = 0, 8, 16
C_QN, C_KVN = 32, 35
C_MIXN, C_MOUT, C_XN, C_MEMN, C_FN2 = 36, 44, 52, 60, 68
C_CDB = 76
C_CDW = 78
C_PE = C_CDW + 2 * TAPS
C_DW = C_PE + 2 * CMP_KT
NF2 = 2 * FF // P
NCOLS = C_DW + 4 * NF2

K_ID = 0
K_MASK = K_ID + P
K_CB = K_MASK + 3 * P
K_C01 = K_CB + NT * NCMP
K_INV = K_C01 + NT * NCMP
K_SEL = K_INV + ROPE // 2
NCONST = K_SEL + GW
NPOOL = NG * P + NG * EDGE + NG * P


def constants():
    c = np.zeros((P, NCONST), np.float32)
    c[:, K_ID:K_ID + P] = np.eye(P, dtype=np.float32)
    causal = np.where(np.arange(P)[None, :] <= np.arange(P)[:, None], 0.0, NEG).astype(np.float32)
    c[:, K_MASK:K_MASK + P] = causal
    c[:, K_MASK + 2 * P:K_MASK + 3 * P] = causal
    t = np.arange(SEQ).reshape(NT, P)
    end = np.arange(NCMP) * CMP_STRIDE + CMP_BLOCK - 1
    ok = (end[None, None, :] <= t[:, :, None]).transpose(1, 0, 2).reshape(P, NT * NCMP)
    c[:, K_CB:K_CB + NT * NCMP] = np.where(ok, 0.0, NEG)
    c[:, K_C01:K_C01 + NT * NCMP] = ok
    theta = np.float32(10000.0)
    power = np.arange(0, ROPE, 2, dtype=np.float32) / np.float32(ROPE)
    c[:, K_INV:K_INV + ROPE // 2] = (np.float32(1.0) / (theta ** power).astype(np.float32))[None, :]
    for g in range(GG):
        c[g, K_SEL + g * GW // GG:K_SEL + (g + 1) * GW // GG] = 1.0
    bands = np.zeros((P, NPOOL), np.float32)
    full = np.zeros((NG, SEQ, SEQ), np.float64)
    for g, win in enumerate(POOL_WINDOWS):
        for tok in range(SEQ):
            lo = max(0, tok - win + 1)
            full[g, lo:tok + 1, tok] = 1.0 / min(tok + 1, win)
            full[g, tok, tok] -= 1.0
    a, b = NG * P, NG * P + NG * EDGE
    bands[:, :a] = full[:, :P, :P].transpose(1, 0, 2).reshape(P, -1)
    bands[:, a:b] = full[:, :P, P:P + EDGE].transpose(1, 0, 2).reshape(P, -1)
    bands[:, b:] = full[:, P:, P:].transpose(1, 0, 2).reshape(P, -1)
    return c, bands


def weight_blocks(w):
    out = []

    def view(k, c):
        return lambda slot: slot[:, 0:k * c].rearrange("p (k c) -> p k c", k=k)

    def rows(src):
        return src.rearrange("(k p) n -> p k n", p=P)

    def halves(name, src, k, c):
        v = view(k, c)
        h = (k + 1) // 2
        out.append((name, k * c, [(v, (slice(0, h), slice(0, c)), src[:, 0:h, :]),
                                  (v, (slice(h, k), slice(0, c)), src[:, h:k, :])]))

    def cols(name, src, a, c):
        halves(name, rows(src)[:, :, a:a + c], KD, c)

    def pair(name, src, a, b):
        v = view(KD, 2 * P)
        out.append((name, KD * 2 * P, [(v, (slice(0, KD), slice(0, P)), rows(src)[:, :, a:a + P]),
                                       (v, (slice(0, KD), slice(P, 2 * P)), rows(src)[:, :, b:b + P])]))

    def rowpair(name, src, i):
        halves(name, rows(src)[:, 2 * i:2 * i + 2, :], 2, D)

    def mem(i):
        cols(f"mem{i}", w["xattn_wk_2"][0] if i < 4 else w["xattn_wv_2"][0], (i % 4) * 2 * P, 2 * P)

    def ffn(layer):
        for j in range(STEPS):
            out.append((f"ffn{layer}", KD * 2 * P, None))

    halves("pool", w["pool_w"][0].rearrange("g (c p) d -> p (g c) d", p=P), 2 * NG, 256)
    mem(0)
    ffn(0)
    mem(1)
    for b in range(3):
        cols(f"down{b}", w["mla_w_down"][0], b * MLA_DOWN // 3, MLA_DOWN // 3)
    mem(2)
    hw = NOPE + ROPE
    for b, n in enumerate((3, 3, 2)):
        halves(f"uq{b}", rows(w["mla_w_uq"][0])[:, :, 3 * b * hw:(3 * b + n) * hw], 3, n * hw)
    halves("ukv", w["mla_w_ukv"][0].rearrange("p (k c) -> p k c", k=2), 2, D)
    for i in range(4):
        rowpair(f"wo{i}", w["mla_w_o"][0], i)
    mem(3)
    ffn(1)
    mem(4)
    mem(5)
    win = w["w_in_2"][0]
    z = NSA_HEADS * DH
    zg = z + 6 * P + 24
    zc = zg + 2 * GW
    cols("z_a", win, zc, CW_)
    cols("z_gt", win, zc + CW_, CW_)
    cols("z_kcvc", win, z, 2 * P)
    pair("z_q0", win, 0, REP * DH)
    pair("z_q1", win, P, REP * DH + P)
    pair("z_ksw", win, z + 2 * P, z + 4 * P)
    pair("z_vsw", win, z + 3 * P, z + 5 * P)
    cols("z_gl", win, z + 6 * P, 24)
    cols("z_v", win, zg + GW, GW)
    cols("z_u", win, zg, GW)
    for i in range(4):
        rowpair(f"wout{i}", w["w_out_2"][0], i)
    mem(6)
    mem(7)
    for i in range(4):
        cols(f"xq{i}", w["xattn_wq_2"][0], i * XHD, XHD)
    for i in range(4):
        rowpair(f"xo{i}", w["xattn_wo_2"][0], i)
    ffn(2)
    return out


def build(nc, w, consts, bands, out):
    blocks = weight_blocks(w)
    names = [b[0] for b in blocks]
    at = {name: names.index(name) for name in names}
    used_cols = [b[1] for b in blocks]
    NB = len(blocks)
    x_dram = w["x"].rearrange("b (t p) d -> p (b t) d", p=P)
    mem_dram = w["mem_2"].rearrange("b (t p) d -> p (b t) d", p=P)
    out_dram = out.rearrange("b (t p) d -> p (b t) d", p=P)

    def gate_up(layer):
        if layer < 2:
            return (w["ffn_w_gate"][layer], w["ffn_w_up"][layer])
        return (w["ffn_w_up_2"][0][:, 0:FF], w["ffn_w_up_2"][0][:, FF:2 * FF])

    def down_rows(layer):
        return w["ffn_w_down"][layer] if layer < 2 else w["ffn_w_down_2"][0]

    with ExitStack() as ctx:
        def sb(name, shape, dt=F32):
            return ctx.enter_context(nc.sbuf_tensor(name, shape, dt))

        def sem(name):
            return ctx.enter_context(nc.semaphore(name))

        raw = [sb(f"raw{s}", [P, 2048]) for s in range(3)]
        wh = [sb(f"wh{s}", [P, 2048], F32R) for s in range(3)]
        wl = [sb(f"wl{s}", [P, 2048], F32R) for s in range(3)]
        xt = sb("x_tok", [P, NT, D])
        xh = sb("xh", [P, KD, SEQ], F32R)
        xl = sb("xl", [P, KD, SEQ], F32R)
        mh = sb("mh", [P, KD, SEQ], F32R)
        ml = sb("ml", [P, KD, SEQ], F32R)
        km = sb("k_mem", [P, KD, SEQ])
        vm = sb("v_mem", [P, NT, D])
        hh = [sb(f"hh{s}", [P, SEQ], F32R) for s in range(3)]
        hl = [sb(f"hl{s}", [P, SEQ], F32R) for s in range(3)]
        zero = sb("zero", [P, P], F32R)
        con = sb("con", [P, NCONST])
        col = sb("col", [P, NCOLS])
        gain = sb("gain", [P, D])
        diag = sb("diag", [P, NT, P])
        junk = sb("junk", [P, HALF])
        ss = sb("ss", [P, 16, NT, 2])
        st1 = sb("st1", [P, 16, NT])
        st2 = sb("st2", [P, 16, NT])
        rstd = sb("rstd", [P, 16, NT])
        mhalf = sb("mhalf", [P, 16])
        cs = sb("cs", [P, NT, ROPE])
        sn = sb("sn", [P, NT, ROPE])
        base = nc.sbuf_base
        REGION = 61312
        ctx.enter_context(nc.sbuf_tensor("region", [P, REGION // 4], F32))
        base = (base + 31) // 32 * 32
        cursor = [0]

        def at_(name, shape, dt=F32, off=None):
            if off is not None:
                cursor[0] = off
            n = 4
            for d in shape[1:]:
                n *= d
            t = nc.alloc_sbuf_tensor_at(name, shape, dt, offset=base + cursor[0])
            cursor[0] += (n + 31) // 32 * 32
            assert cursor[0] <= REGION - 32, (name, cursor[0])
            return t

        memt = at_("mem_tok", [P, NT, D], off=0)
        band = at_("band", [P, NPOOL])
        bandr = at_("bandr", [P, NPOOL])
        pscale = at_("pscale", [P, D])
        prow = [at_(f"prow{i}", [P, P]) for i in range(4)]
        posi = at_("posi", [P, NT], I32)
        posf = at_("posf", [P, NT])
        ang = at_("ang", [P, NT, ROPE // 2])
        kk = at_("kk", [P, NT, ROPE // 2])
        r0 = at_("r0", [P, NT, ROPE // 2])
        r1 = at_("r1", [P, NT, ROPE // 2])
        draw = [at_(f"draw{s}", [P, D], off=(0 if s == 0 else None)) for s in range(3)]
        dh = [at_(f"dh{s}", [P, D], F32R) for s in range(3)]
        dl = [at_(f"dl{s}", [P, D], F32R) for s in range(3)]
        th = [at_(f"th{s}", [P, SEQ]) for s in range(3)]
        pr = [at_(f"pr{s}", [P, SEQ]) for s in range(3)]
        ga = at_("ga", [P, SEQ])
        cg = [at_(f"cg{s}", [P, SEQ]) for s in range(3)]
        cu = [at_(f"cu{s}", [P, SEQ]) for s in range(3)]
        ds = at_("ds", [P, NT, MLA_DOWN], off=0)
        dqk = at_("dqk", [P, 2, NT, P])
        qn = at_("qn", [P, HEADS, SEQ])
        qr = at_("qr", [P, NT, HEADS * ROPE])
        qrt = at_("qrt", [P, HEADS // 2, SEQ])
        kn = at_("kn", [P, HEADS, SEQ])
        vv = at_("vv", [P, NT, HEADS * P])
        kr = at_("kr", [P, NT, P])
        krt = at_("krt", [P, SEQ])
        ra = at_("ra", [P, HEADS * ROPE])
        rb = at_("rb", [P, HEADS * ROPE])
        sc = [at_(f"sc{s}", [P, 3 * P]) for s in range(2)]
        pt = [at_(f"pt{s}", [P, 3 * P]) for s in range(2)]
        stat = at_("stat", [P, HEADS, 4, NT])
        mst = at_("mst", [P, 4, 2, NT])
        qt = at_("qt", [P, REP, SEQ], off=0)
        ksw = at_("ksw", [P, 2, SEQ])
        kvc = at_("kvc", [P, 2, SEQ])
        vsw = at_("vsw", [P, NT, 2 * P])
        x4 = at_("x4", [P, 2, GROUPS, SEQ])
        fl = at_("fl", [P, 2, CMP_KT, GROUPS, NCMP])
        yn = at_("yn", [P, NT, D])
        cw1 = at_("cw1", [P, 2, CMP_KT, DH])
        cw2 = at_("cw2", [DH, 2, DH])
        hg = at_("hg", [DH, 4, 2 * GROUPS * NCMP])
        kcm = at_("kcm", [P, NCMP])
        vcs = at_("vcs", [NCMP, GROUPS, DH])
        vbd = at_("vbd", [P, NSA_HEADS * DH])
        hc = at_("hc", [P, 2, PAD + SEQ])
        yc = at_("yc", [P, 2, SEQ])
        gate = at_("gate", [P, NT, 24])
        e1 = at_("e1", [P, HALF])
        e2 = at_("e2", [P, HALF])
        e3 = at_("e3", [P, HALF])
        wst = at_("wst", [P, GG, P])
        bsr = at_("bsr", [GG, P])
        lng = at_("lng", [P, 2, 2, GW])
        s2 = [kvc[:, :, :].rearrange("p a s -> p (a s)")[:, 0:3 * P],
              fl[:, :, :, :, :].rearrange("p a k g n -> p (a k g n)")[:, GG * P:GG * P + 3 * P]]
        p2 = [at_(f"p2_{s}", [P, 3 * P]) for s in range(2)]
        nst = at_("nst", [P, 4, 2 * NSA_HEADS, NT])
        lst = at_("lst", [P, 64])
        uu = x4[:, :, :, :].rearrange("p a g s -> p (a g s)")[:, 0:HALF]
        vg = x4[:, :, :, :].rearrange("p a g s -> p (a g s)")[:, HALF:2 * HALF]
        ws = fl[:, :, :, :, :].rearrange("p a k g n -> p (a k g n)")[:, 0:GG * P]
        cm = [cw1[:, 0, :, :].rearrange("p k d -> p (k d)")[:, 240 * i:240 * i + 240] for i in range(4)]
        dseg = cw1[:, 1, :, :].rearrange("p k d -> p (k d)")[:, 0:768].rearrange("p (a b) -> p a b", a=6)
        qx = at_("qx", [P, KD, SEQ], off=0)
        sx = [at_(f"sx{s}", [P, NT, SEQ]) for s in range(2)]
        px = [at_(f"px{s}", [P, NT, SEQ]) for s in range(2)]
        xst = at_("xst", [P, XHEADS, 4, NT])

        bank = [ctx.enter_context(nc.psum_tensor(f"bank{i}", [P, HALF], F32)) for i in range(8)]

        raw_full = [sem(f"raw_full{s}") for s in range(3)]
        hi_done, lo_done, block_used = sem("hi_done"), sem("lo_done"), sem("block_used")
        d_full = [sem(f"d_full{s}") for s in range(3)]
        d_hi, d_lo, down_done = sem("d_hi"), sem("d_lo"), sem("down_done")
        tanh_done, gated, prod_done = sem("tanh_done"), sem("gated"), sem("prod_done")
        h_hi, h_ready = sem("h_hi"), sem("h_ready")
        conv_in, conv_tap, conv_silu = sem("conv_in"), sem("conv_tap"), sem("conv_silu")
        x_loaded, con_loaded, band_loaded = sem("x_loaded"), sem("con_loaded"), sem("band_loaded")
        mem_loaded, rows_loaded, pscale_loaded = sem("mem_loaded"), sem("rows_loaded"), sem("pscale_loaded")
        gain_loaded, pos_loaded = sem("gain_loaded"), sem("pos_loaded")
        last_gain_loaded = sem("last_gain_loaded")
        zero_set, mhalf_set = sem("zero_set"), sem("mhalf_set")
        cols_t, cols_done, taps_halved = sem("cols_t"), sem("cols_done"), sem("taps_halved")
        pool_scaled = sem("pool_scaled")
        sq_done, rstd_done = sem("sq_done"), sem("rstd_done")
        res_done, diag_done = sem("res_done"), sem("diag_done")
        t_done, t_hi, t_lo = sem("t_done"), sem("t_hi"), sem("t_lo")
        mem_out = sem("mem_out")
        region_free = sem("region_free")
        scaled = sem("scaled")
        rope_a, rope_s = sem("rope_a"), sem("rope_s")
        ds_out, mla_sq, mla_rs, mla_dg = sem("ds_out"), sem("mla_sq"), sem("mla_rs"), sem("mla_dg")
        cq_t, cq_hi, cq_lo = sem("cq_t"), sem("cq_hi"), sem("cq_lo")
        kr_done, kr_t, kr_out = sem("kr_done"), sem("kr_t"), sem("kr_out")
        qk_mm, qk_out = sem("qk_mm"), sem("qk_out")
        v_mm, v_out = sem("v_mm"), sem("v_out")
        qr_done, qr_t, qr_out = sem("qr_done"), sem("qr_t"), sem("qr_out")
        s_mm, s_max, s_exp, s_norm = sem("s_mm"), sem("s_max"), sem("s_exp"), sem("s_norm")
        p_t, p_out, o_mm, o_hi, o_lo = sem("p_t"), sem("p_out"), sem("o_mm"), sem("o_hi"), sem("o_lo")
        z_out = sem("z_out")
        z_params = sem("z_params")
        z_ws, ws_loaded, ws_cut = sem("z_ws"), sem("ws_loaded"), sem("ws_cut")
        hc_done, cv_tap = sem("hc_done"), sem("cv_tap")
        shifted, fl_done, cmp_mm, cmp_a, cmp_d, cmp_out = (sem("shifted"), sem("fl_done"), sem("cmp_mm"),
                                                         sem("cmp_a"), sem("cmp_d"), sem("cmp_out"))
        vbd_zero, vbd_set = sem("vbd_zero"), sem("vbd_set")
        gl_a, gl_done = sem("gl_a"), sem("gl_done")
        gz_a, gz_d = sem("gz_a"), sem("gz_d")
        ws_t, ws_out, ln_rs, vn_done, mix_mm, gy_done = (sem("ws_t"), sem("ws_out"), sem("ln_rs"),
                                                        sem("vn_done"), sem("mix_mm"), sem("gy_done"))
        ycs_t, cvln_done, cv_a, cy_done = sem("ycs_t"), sem("cvln_done"), sem("cv_a"), sem("cy_done")
        sc_mm, cm_e, pc_done, pc_t, pc_out = (sem("sc_mm"), sem("cm_e"), sem("pc_done"), sem("pc_t"),
                                             sem("pc_out"))
        n_mm, n_max, n_exp, n_norm, n_t, n_out = (sem("n_mm"), sem("n_max"), sem("n_exp"), sem("n_norm"),
                                                  sem("n_t"), sem("n_out"))
        o_all, yn_done, y_sq, y_rs, y_dg = sem("o_all"), sem("yn_done"), sem("y_sq"), sem("y_rs"), sem("y_dg")
        y_ms = sem("y_ms")
        q_out = sem("q_out")
        a_mm, a_max, a_exp, a_norm, a_t, a_out, ao_mm, ao_hi, ao_lo = (
            sem("a_mm"), sem("a_max"), sem("a_exp"), sem("a_norm"), sem("a_t"), sem("a_out"),
            sem("ao_mm"), sem("ao_hi"), sem("ao_lo"))
        dve_order, act_order, pool_order = sem("dve_order"), sem("act_order"), sem("pool_order")
        stored = sem("stored")

        ident = con[:, K_ID:K_ID + P]
        mask = con[:, K_MASK:K_MASK + 3 * P]

        def split_views(n, *slots):
            if names[n] not in ("z_q0", "z_q1"):
                return [[t[:, 0:used_cols[n]] for t in slots]]
            by_head = [t[:, :].rearrange("p (k j g d) -> p k j g d", k=KD, j=2, g=GROUPS) for t in slots[1:]]
            by_group = slots[0][:, :].rearrange("p (k g j d) -> p k g j d", k=KD, j=2, g=GROUPS)
            return [[by_group[:, :, g, :, :]] + [v[:, :, :, g, :] for v in by_head] for g in range(GROUPS)]

        def k_view(t, k, c):
            return t[:, 0:k * c].rearrange("p (k c) -> p k c", k=k)

        block = ctx.enter_context(nc.Block())

        @block.sync
        def _(sp):
            def load(n):
                _, _, parts = blocks[n]
                if n >= 3:
                    sp.wait_ge(hi_done, n - 2)
                    sp.wait_ge(lo_done, n - 2)
                for v, (ks, cs_), src in parts:
                    sp.dma_start(v(raw[n % 3])[:, ks, cs_], src).then_inc(raw_full[n % 3], 32 // len(parts))

            def ffn(layer):
                n0, m0 = at[f"ffn{layer}"], STEPS * layer
                gu = gate_up(layer)
                dn = down_rows(layer)

                def load_gu(s, j, n):
                    slot = raw[s][:, :].rearrange("p (k h c) -> p k h c", k=KD, h=2)
                    sp.wait_ge(hi_done, n - 2)
                    sp.wait_ge(lo_done, n - 2)
                    for half in range(2):
                        src = gu[half].rearrange("(k p) n -> p k n", p=P)[:, :, bass.ds(j * P, P)]
                        sp.dma_start(slot[:, :, half, :], src).then_inc(raw_full[s], 16)

                def load_d(s, j, m):
                    if not isinstance(m, int) or m >= 3:
                        sp.wait_ge(d_lo, m - 2)
                    sp.dma_start(draw[s][:, :], dn[bass.ds(j * P, P), :]).then_inc(d_full[s], 16)

                for j in range(3):
                    load_gu((n0 + j) % 3, j, n0 + j)
                sp.wait_ge(region_free, layer + 1)
                for j in range(3):
                    load_d((m0 + j) % 3, j, m0 + j)
                with sp.Fori(0, LOOPED // 3) as i:
                    for s in range(3, 6):
                        load_gu((n0 + s) % 3, 3 * i + s, 3 * i + n0 + s)
                        load_d((m0 + s) % 3, 3 * i + s, 3 * i + m0 + s)
                for j in range(LOOPED + 3, STEPS):
                    load_gu((n0 + j) % 3, j, n0 + j)
                    load_d((m0 + j) % 3, j, m0 + j)

            n = 0
            while n < NB:
                if names[n].startswith("ffn"):
                    ffn(int(names[n][3:]))
                    n += STEPS
                else:
                    load(n)
                    n += 1
            for t in range(NT):
                sp.wait_ge(scaled, 6 + 2 * t)
                sp.dma_start(out_dram[:, t, :], xt[:, t, :]).then_inc(stored, 16)
            sp.wait_ge(stored, 16 * NT)

        @block.scalar
        def _(act):
            junk_writer = [None]

            def junk_for(signal, count, width):
                if junk_writer[0] is not None:
                    act.wait_ge(*junk_writer[0])
                junk_writer[0] = (signal, count)
                return junk[:, 0:width]

            def hi(n):
                if n >= NB:
                    return
                act.wait_ge(raw_full[n % 3], 32 * (n // 3 + 1))
                if n >= 3:
                    act.wait_ge(block_used, n - 2)
                if n == 0:
                    act.wait_ge(pool_scaled, 3)
                for r, h in split_views(n, raw[n % 3], wh[n % 3]):
                    ins = act.activation(h, r, ACT.Copy)
                ins.then_inc(hi_done, 1)

            def squares(q, src, ready, first):
                for t in range(NT):
                    for c in range(2):
                        if ready is not None:
                            act.wait_ge(ready, first + 2 * t + c)
                        act.activation(junk_for(sq_done, 4 * q + 2 * t + c + 1, HALF),
                                       src[:, t, c * HALF:(c + 1) * HALF], ACT.Square,
                                       accum_out=ss[:, q, t, c:c + 1]).then_inc(sq_done, 1)

            def split_t(e, dst, c0, banks):
                for k in range(KD):
                    if k % 2 == 0:
                        act.wait_ge(t_done, (KD * e + k) // 2 + 1)
                    src = bank[banks + k // 2][:, (k % 2) * SEQ:(k % 2 + 1) * SEQ]
                    act.activation(dst[:, k, :], src, ACT.Copy, scale=col[:, c0 + k:c0 + k + 1]) \
                       .then_inc(t_hi, 1)

            def mem_block(i):
                n = at[f"mem{i}"]
                act.wait_ge(block_used, n + 1)
                src = bank[7][:, :].rearrange("p (a s) -> p a s", a=2)
                if i < 4:
                    dst = km[:, 2 * i:2 * i + 2, :]
                else:
                    dst = vm[:, :, (i - 4) * 256:(i - 3) * 256]
                act.activation(dst, src, ACT.Copy).then_inc(mem_out, 1)
                hi(n + 3)

            def ffn(layer):
                n0, m0 = at[f"ffn{layer}"], STEPS * layer

                def d_split(s, m):
                    act.wait_ge(d_full[s], 16 * (m // 3 + 1) if isinstance(m, int) else m)
                    return s

                def dhi(s, m, q):
                    act.wait_ge(d_full[s], q)
                    act.wait_ge(down_done, m + 1)
                    act.activation(dh[s][:, :], draw[s][:, :], ACT.Copy).then_inc(d_hi, 1)

                def step(j, i, jj):
                    s = (m0 + jj) % 3
                    n, m = n0 + j, m0 + j
                    act.wait_ge(block_used, n + 1)
                    b = bank[4 + s]
                    if layer < 2:
                        act.activation(th[s][:, :], b[:, 0:SEQ], ACT.Tanh, scale=0.5).then_inc(tanh_done, 1)
                    else:
                        for half, dst in ((0, cg[s]), (1, cu[s])):
                            c2 = C_DW + 2 * NF2 + half * STEPS
                            cb = C_DW + 3 * NF2 + half * STEPS
                            act.activation(dst[:, :], b[:, half * SEQ:(half + 1) * SEQ], ACT.Identity,
                                           scale=col[:, bass.ds(j + c2, 1)],
                                           bias=col[:, bass.ds(j + cb, 1)]).then_inc(conv_in, 1)
                    if i is not None or jj + 3 < STEPS:
                        ns = (n0 + jj) % 3
                        act.wait_ge(raw_full[ns], 32 * ((n0 + jj) // 3 + 2) + (0 if i is None else 32 * i))
                        act.activation(wh[ns][:, :], raw[ns][:, :], ACT.Copy).then_inc(hi_done, 1)
                    else:
                        hi(n0 + jj + 3)
                    if layer == 2:
                        act.wait_ge(conv_tap, 4 * (j + 1) - 2)
                        act.activation(th[s][:, :], cg[s][:, :], ACT.Tanh, scale=0.5).then_inc(tanh_done, 1)
                    act.wait_ge(prod_done, m + 4)
                    act.wait_ge(down_done, m + 1)
                    act.activation(hh[s][:, :], pr[s][:, :], ACT.Copy).then_inc(h_hi, 1)
                    if i is not None or jj + 2 < STEPS:
                        s2_ = (m0 + jj + 2) % 3
                        q = 16 * ((m0 + jj + 2) // 3 + 1) + (0 if i is None else 16 * i)
                        dhi(s2_, m + 2, q)

                for j in range(2):
                    dhi((m0 + j) % 3, m0 + j, 16 * ((m0 + j) // 3 + 1))
                step(0, None, 0)
                with act.Fori(0, LOOPED // 3) as i:
                    for s in range(1, 4):
                        step(3 * i + s, i, s)
                for j in range(LOOPED + 1, STEPS):
                    step(j, None, j)

            def norm(p, q, e, c0, first):
                squares(q, xt, res_done, first)
                split_t(e, xh, c0, 0)

            for t in range(NT):
                act.dma_start(xt[:, t, :], x_dram[:, t, :]).then_inc(x_loaded, 16)
            act.dma_start(con[:, :], consts).then_inc(con_loaded, 16)
            act.dma_start(band[:, :], bands).then_inc(band_loaded, 16)
            act.dma_start(pscale[:, :], w["pool_scale"][0:1, :].to_broadcast([P, D])).then_inc(pscale_loaded, 16)
            rows = [(0, 0, w["norm_mix"].rearrange("l (k p) -> (l k) p", p=P)),
                    (0, C_FFN, w["norm_ffn"].rearrange("l (k p) -> (l k) p", p=P)),
                    (0, C_QN, w["mla_q_norm"].rearrange("l (k p) -> (l k) p", p=P)),
                    (0, C_KVN, w["mla_kv_norm"].rearrange("l (k p) -> (l k) p", p=P)),
                    (0, C_MIXN, w["mix_norm_g_2"].rearrange("l (k p) -> (l k) p", p=P)),
                    (0, C_MOUT, w["mix_out_g_2"].rearrange("l (k p) -> (l k) p", p=P)),
                    (0, C_XN, w["xattn_norm_g_2"].rearrange("l (k p) -> (l k) p", p=P)),
                    (0, C_MEMN, w["mem_norm_g_2"].rearrange("l (k p) -> (l k) p", p=P)),
                    (0, C_FN2, w["ffn_norm_g_2"].rearrange("l (k p) -> (l k) p", p=P)),
                    (0, C_CDB, w["conv_dw_b_2"].rearrange("l (k p) -> (l k) p", p=P)),
                    (1, 0, w["conv_dw_w_2"][0].rearrange("t (a p) -> (t a) p", p=P)),
                    (1, 2 * TAPS, w["cmp_pe_2"][0].rearrange("a (k e) d -> (a k) (e d)", e=2)),
                    (2, 0, w["ffn_dw_w_2"][0, 0:2, :].rearrange("t (j p) -> (t j) p", p=P)),
                    (3, 0, w["ffn_dw_w_2"][0, 2:3, :].rearrange("t (j p) -> (t j) p", p=P)),
                    (3, NF2, w["ffn_dw_b_2"].rearrange("t (j p) -> (t j) p", p=P))]
            for i, r, src in rows:
                act.dma_start(prow[i][r:r + src.shape[0], :], src).then_inc(rows_loaded, 16)
            act.dma_start(memt[:, :, :], mem_dram).then_inc(mem_loaded, 16)
            act.dma_start(gain[:, :], w["norm_final"].rearrange("(a d) -> a d", a=1).to_broadcast([P, D])) \
               .then_inc(gain_loaded, 16)
            act.dma_start(posi[:, :], w["positions"].rearrange("a (t p) -> p (a t)", p=P),
                          allow_slow_non_contiguous=True).then_inc(pos_loaded, 16)
            act.wait_ge(rope_a, 1)
            act.activation(sn[:, :, 32:64], r0[:, :, :], ACT.Sin).then_inc(rope_s, 1)
            act.activation(cs[:, :, 0:32], r1[:, :, :], ACT.Sin).then_inc(rope_s, 1)
            act.wait_ge(x_loaded, 16 * NT)
            squares(0, xt, None, 0)
            act.wait_ge(cols_t, 1)
            act.activation(col[:, :], bank[7][:, 0:NCOLS], ACT.Copy).then_inc(cols_done, 1)
            act.wait_ge(cols_done, 1)
            hi(0)
            split_t(0, xh, C_MIX0, 0)
            act.wait_ge(mem_loaded, 16)
            squares(1, memt, None, 0)
            hi(1)
            hi(2)
            split_t(1, mh, C_MEMN, 4)
            hi(3)
            mem_block(0)
            norm(0, 2, 2, C_FFN, 1)
            ffn(0)
            mem_block(1)
            norm(1, 3, 3, C_MIX1, 5)
            n = at["down0"]
            hi_after = [n]

            def after(name):
                hi(at[name] + 3)

            act.wait_ge(block_used, at["down0"] + 1)
            after("down0")
            act.wait_ge(block_used, at["down1"] + 1)
            for t in range(NT):
                act.activation(ds[:, t, 0:QLR], bank[t][:, 0:QLR], ACT.Copy).then_inc(ds_out, 1)
            act.wait_ge(ds_out, 2)
            for t in range(NT):
                act.activation(junk_for(mla_sq, t + 1, QLR), ds[:, t, 0:QLR], ACT.Square,
                               accum_out=mst[:, 0, 0, t:t + 1]).then_inc(mla_sq, 1)
            after("down1")
            act.wait_ge(block_used, at["down2"] + 1)
            for t in range(NT):
                act.activation(ds[:, t, QLR:MLA_DOWN], bank[2 + t][:, 0:KVR + ROPE], ACT.Copy).then_inc(ds_out, 1)
            act.wait_ge(ds_out, 4)
            for t in range(NT):
                act.activation(junk_for(mla_sq, t + 3, KVR), ds[:, t, QLR:QLR + KVR], ACT.Square,
                               accum_out=mst[:, 0, 1, t:t + 1]).then_inc(mla_sq, 1)
            after("down2")
            mem_block(2)
            for f in range(4):
                act.wait_ge(cq_t, f // 2 + 1)
                act.activation(xh[:, f, :], bank[4 + f // 2][:, (f % 2) * SEQ:(f % 2 + 1) * SEQ], ACT.Copy,
                               scale=col[:, C_QN + f:C_QN + f + 1]).then_inc(cq_hi, 1)
            act.wait_ge(kr_t, 1)
            act.activation(krt[:, :], bank[6][:, 0:SEQ], ACT.Copy).then_inc(kr_out, 1)
            def heads_out(dst, i, first):
                act.wait_ge(qk_mm, first + i + 1)
                act.activation(dst[:, 2 * i:2 * i + 2, :].rearrange("p a s -> p (a s)"), bank[4 + i % 2][:, :],
                               ACT.Copy).then_inc(qk_out, 1)

            heads_out(qn, 0, 0)
            after("uq0")
            heads_out(qn, 1, 0)
            heads_out(qn, 2, 0)
            after("uq1")
            heads_out(qn, 3, 0)
            after("uq2")
            for i in range(4):
                heads_out(kn, i, 4)
            for i in range(4):
                act.wait_ge(v_mm, i + 1)
                t, hv = i // 2, i % 2
                act.activation(vv[:, t, hv * HALF:(hv + 1) * HALF], bank[(2, 3, 6, 2)[i]][:, :], ACT.Copy) \
                   .then_inc(v_out, 1)
            after("ukv")
            for i in range(2):
                act.wait_ge(qr_t, i + 1)
                act.activation(qrt[:, 2 * i:2 * i + 2, :].rearrange("p a s -> p (a s)"), bank[i][:, :], ACT.Copy) \
                   .then_inc(qr_out, 1)

            def mla_exp(h):
                act.wait_ge(s_max, h + 1)
                for t, (a, b) in enumerate(((0, P), (P, 3 * P))):
                    act.activation(sc[h % 2][:, a:b], sc[h % 2][:, a:b], ACT.Exp,
                                   bias=stat[:, h, 1, t:t + 1], accum_out=stat[:, h, 2, t:t + 1]) \
                       .then_inc(s_exp, 1)

            def mla_pt(h):
                act.wait_ge(p_t, h + 1)
                if h >= 2:
                    act.wait_ge(o_mm, h - 1)
                act.activation(pt[h % 2][:, :], bank[6][:, 0:3 * P], ACT.Copy).then_inc(p_out, 1)

            def mla_o(h):
                act.wait_ge(o_mm, h + 1)
                act.activation(xh[:, h, :], bank[7][:, (h % 2) * SEQ:(h % 2 + 1) * SEQ], ACT.Copy).then_inc(o_hi, 1)

            mla_exp(0)
            for h in range(1, HEADS + 1):
                mla_pt(h - 1)
                if h < HEADS:
                    mla_exp(h)
                mla_o(h - 1)
                if h in (4, 6):
                    after(f"wo{h // 2 - 2}")
            for i in (2, 3):
                after(f"wo{i}")
            mem_block(3)
            norm(2, 4, 4, C_FFN + 8, 9)
            ffn(1)
            mem_block(4)
            mem_block(5)
            squares(5, xt, res_done, 13)
            squares(6, xt, scaled, 1)
            split_t(5, xh, C_MIXN, 0)
            act.wait_ge(block_used, at["z_gt"] + 1)
            act.activation(e1[:, :], bank[1][:, :], ACT.Tanh, scale=0.5).then_inc(z_out, 1)
            hi(at["z_a"] + 3)
            after("z_gt")
            act.wait_ge(block_used, at["z_kcvc"] + 1)
            act.activation(kvc[:, :, :].rearrange("p a s -> p (a s)"), bank[2][:, :], ACT.Copy).then_inc(z_out, 1)
            act.wait_ge(z_out, 2)
            for g in range(GROUPS):
                act.dma_start(x4[0:DH, :, g, :], kvc[g * DH:(g + 1) * DH, :, :]).then_inc(shifted, 16)
                act.dma_start(x4[DH:P, :, g, 0:SEQ - 1], kvc[g * DH:(g + 1) * DH, :, 1:SEQ]).then_inc(shifted, 16)
            after("z_kcvc")
            for i in range(2):
                act.wait_ge(block_used, at[f"z_q{i}"] + 1)
                act.activation(qt[:, 2 * i:2 * i + 2, :].rearrange("p a s -> p (a s)"), bank[3 if i == 0 else 0][:, :],
                               ACT.Copy).then_inc(z_out, 1)
                after(f"z_q{i}")
            act.wait_ge(cmp_mm, 1)
            hs = bank[7][0:DH, 0:60]
            act.activation(hg[:, 0, :], hs, ACT.Square).then_inc(cmp_a, 1)
            act.wait_ge(cmp_d, 2)
            act.activation(hg[:, 1, :], hg[:, 2, :], ACT.Tanh, scale=GELU_S).then_inc(cmp_a, 1)
            act.wait_ge(block_used, at["z_ksw"] + 1)
            act.activation(ksw[:, :, :].rearrange("p a s -> p (a s)"), bank[1][:, :], ACT.Copy).then_inc(z_out, 1)
            after("z_ksw")
            act.wait_ge(cmp_mm, 2)
            act.activation(kcm[:, :], bank[7][:, 64:64 + NCMP], ACT.Copy, scale=0.5).then_inc(cmp_out, 1)
            act.activation(vcs[:, :, :], bank[7][0:NCMP, 128:256].rearrange("n (g d) -> n g d", g=GROUPS), ACT.Copy,
                           scale=0.5).then_inc(cmp_out, 1)
            act.wait_ge(cmp_out, 2)
            act.wait_ge(vbd_zero, 1)
            for h in range(NSA_HEADS):
                act.dma_start(vbd[h * NCMP:(h + 1) * NCMP, h * DH:(h + 1) * DH], vcs[:, h // REP, :]) \
                   .then_inc(vbd_set, 16)
            act.wait_ge(block_used, at["z_vsw"] + 1)
            act.activation(vsw[:, :, :].rearrange("p a s -> p (a s)"), bank[2][:, :], ACT.Copy).then_inc(z_out, 1)
            after("z_vsw")
            act.wait_ge(block_used, at["z_gl"] + 1)
            act.activation(gate[:, :, :].rearrange("p t c -> p (t c)"), bank[3][:, 0:NT * 24], ACT.Tanh, scale=0.5) \
               .then_inc(gl_a, 1)
            after("z_gl")
            for i, name in enumerate(("z_v", "z_u")):
                act.wait_ge(block_used, at[name] + 1)
                b = bank[(0, 1)[i]]
                if i == 1:
                    act.wait_ge(gz_d, 3)
                act.activation(e1[:, :], b[:, :], ACT.Square).then_inc(gz_a, 1)
                act.wait_ge(gz_d, 3 * i + 2)
                act.activation(e1[:, :], e2[:, :], ACT.Tanh, scale=GELU_S).then_inc(gz_a, 1)
                after(name)
            act.wait_ge(ws_t, 1)
            act.activation(wst[:, :, :].rearrange("p g t -> p (g t)"), bank[6][:, :], ACT.Copy).then_inc(ws_out, 1)
            act.wait_ge(cm_e, 1)
            act.activation(cm[1], cm[0], ACT.Exp, scale=NSA_SCALE).then_inc(cm_e, 1)
            act.wait_ge(pc_t, NT)
            act.activation(e1[0:120, 0:SEQ], bank[6][0:120, 0:SEQ], ACT.Copy).then_inc(pc_out, 1)

            def nsa_exp(u):
                act.wait_ge(n_max, u + 1)
                for t, (a, b) in enumerate(((0, P), (P, 3 * P))):
                    act.activation(s2[u % 2][:, a:b], s2[u % 2][:, a:b], ACT.Exp,
                                   bias=nst[:, 1, u, t:t + 1], accum_out=nst[:, 2, u, t:t + 1]) \
                       .then_inc(n_exp, 1)

            def nsa_pt(u):
                act.wait_ge(n_t, u + 1)
                if u >= 2:
                    act.wait_ge(o_all, u - 1)
                act.activation(p2[u % 2][:, :], bank[6][:, 0:3 * P], ACT.Copy).then_inc(n_out, 1)

            nsa_exp(0)
            for u in range(1, 2 * NSA_HEADS + 1):
                nsa_pt(u - 1)
                if u < 2 * NSA_HEADS:
                    nsa_exp(u)
            act.wait_ge(cvln_done, 1)
            act.activation(e1[:, :], e2[:, :], ACT.Tanh, scale=0.5).then_inc(cv_a, 1)
            act.wait_ge(o_all, 2 * NSA_HEADS)
            for t in range(NT):
                act.activation(yn[:, t, 0:HALF], bank[t][:, :], ACT.Copy).then_inc(yn_done, 1)
            act.wait_ge(yn_done, 2)
            act.wait_ge(cy_done, 1)
            act.wait_ge(gy_done, 2)
            for s, (a, b) in enumerate(((0, 512), (512, 768), (768, 1024))):
                for t in range(NT):
                    act.activation(junk_for(y_sq, 2 * s + t + 1, b - a), yn[:, t, a:b], ACT.Square,
                                   accum_out=lst[:, 32 + 2 * s + t:33 + 2 * s + t]).then_inc(y_sq, 1)
            split_t(6, xh, C_MOUT, 0)
            for i in range(4):
                after(f"wout{i}")
            mem_block(6)
            mem_block(7)
            norm(4, 7, 7, C_XN, 17)
            def x_q(h):
                act.wait_ge(block_used, at[f"xq{h}"] + 1)
                act.activation(qx[:, 2 * h:2 * h + 2, :].rearrange("p a s -> p (a s)"), bank[0][:, :], ACT.Copy) \
                   .then_inc(q_out, 1)
                after(f"xq{h}")

            def x_exp(h):
                act.wait_ge(a_max, h + 1)
                for t in range(NT):
                    act.activation(sx[h % 2][:, t, :], bank[4 + h % 2][:, t * SEQ:(t + 1) * SEQ], ACT.Exp, scale=XSCALE,
                                   bias=xst[:, h, 1, t:t + 1], accum_out=xst[:, h, 2, t:t + 1]) \
                       .then_inc(a_exp, 1)

            def x_pt(h):
                act.wait_ge(a_t, h + 1)
                if h >= 2:
                    act.wait_ge(ao_mm, h - 1)
                act.activation(px[h % 2][:, :, :].rearrange("p a s -> p (a s)"), bank[6][:, :], ACT.Copy) \
                   .then_inc(a_out, 1)

            def x_o(h):
                act.wait_ge(ao_mm, h + 1)
                act.activation(mh[:, 2 * h:2 * h + 2, :].rearrange("p a s -> p (a s)"), bank[7][:, :], ACT.Copy) \
                   .then_inc(ao_hi, 1)

            x_q(0)
            for h in range(1, XHEADS + 1):
                x_exp(h - 1)
                if h < XHEADS:
                    x_q(h)
                x_pt(h - 1)
                x_o(h - 1)
            for i in range(4):
                after(f"xo{i}")
            norm(5, 8, 8, C_FN2, 21)
            ffn(2)
            squares(9, xt, res_done, 25)

        @block.vector
        def _(dve):
            order = [0]

            def then(ins):
                order[0] += 1
                ins.then_inc(dve_order, 1)
                dve.wait_ge(dve_order, order[0])

            def lo(n):
                if n >= NB:
                    return
                dve.wait_ge(hi_done, n + 1)
                for r, h, l in split_views(n, raw[n % 3], wh[n % 3], wl[n % 3]):
                    ins = dve.tensor_tensor(l, r, h.bitcast(F32), ALU.subtract)
                ins.then_inc(lo_done, 1)

            def split_t(e, hi_, lo_, c0, banks):
                for k in range(KD):
                    if k % 2 == 0:
                        dve.wait_ge(t_hi, KD * e + k + 2)
                    src = bank[banks + k // 2][:, (k % 2) * SEQ:(k % 2 + 1) * SEQ]
                    dve.scalar_tensor_tensor(out=lo_[:, k, :], in0=src, scalar=col[:, c0 + k:c0 + k + 1],
                                             in1=hi_[:, k, :].bitcast(F32), op0=ALU.mult, op1=ALU.subtract) \
                       .then_inc(t_lo, 1)

            def diagonals(q):
                dve.wait_ge(rstd_done, q + 1)
                for t in range(NT):
                    dve.tensor_scalar(diag[:, t, :], ident, rstd[:, q, t:t + 1], None, ALU.mult) \
                       .then_inc(diag_done, 1)

            def residual():
                for t in range(NT):
                    for c in range(2):
                        part = xt[:, t, c * HALF:(c + 1) * HALF]
                        dve.tensor_tensor(part, bank[2 * t + c][:, :], part, ALU.add).then_inc(res_done, 1)

            def rescale(q):
                dve.wait_ge(rstd_done, q + 1)
                for t in range(NT):
                    for c in range(2):
                        part = xt[:, t, c * HALF:(c + 1) * HALF]
                        dve.scalar_tensor_tensor(out=part, in0=part, scalar=rstd[:, q, t:t + 1],
                                                 in1=gain[:, c * HALF:(c + 1) * HALF],
                                                 op0=ALU.mult, op1=ALU.mult).then_inc(scaled, 1)

            def norm(q, e, c0):
                diagonals(q)
                split_t(e, xh, xl, c0, 0)

            def ffn(layer):
                n0, m0 = at[f"ffn{layer}"], STEPS * layer

                def dlo(s, m):
                    dve.wait_ge(d_hi, m + 1)
                    dve.tensor_tensor(dl[s][:, :], draw[s][:, :], dh[s][:, :].bitcast(F32), ALU.subtract) \
                       .then_inc(d_lo, 1)

                def step(j, i, jj):
                    s = (m0 + jj) % 3
                    n, m = n0 + j, m0 + j
                    g, u = bank[4 + s][:, 0:SEQ], bank[4 + s][:, SEQ:2 * SEQ]
                    if layer == 2:
                        dve.wait_ge(conv_in, 2 * j + 2)
                        for half, (src, dst) in enumerate(((g, cg[s]), (u, cu[s]))):
                            for back in (1, 2):
                                if back == 2:
                                    dve.wait_ge(conv_tap, 4 * j + 2 * half + 1)
                                c = C_DW + (2 - back) * NF2 + half * STEPS
                                dve.scalar_tensor_tensor(
                                    out=dst[:, back:SEQ], in0=src[:, 0:SEQ - back],
                                    scalar=col[:, bass.ds(j + c, 1)], in1=dst[:, back:SEQ],
                                    op0=ALU.mult, op1=ALU.add).then_inc(conv_tap, 1)
                        dve.wait_ge(conv_tap, 4 * j + 4)
                        g, u = cg[s][:, :], cu[s][:, :]
                    dve.wait_ge(tanh_done, m + 1)
                    dve.scalar_tensor_tensor(out=ga[:, :], in0=th[s][:, :], scalar=1.0, in1=g,
                                             op0=ALU.add, op1=ALU.mult).then_inc(gated, 1)
                    dve.wait_ge(gated, m + 1)
                    dve.scalar_tensor_tensor(out=pr[s][:, :], in0=ga[:, :], scalar=0.5, in1=u,
                                             op0=ALU.mult, op1=ALU.mult).then_inc(prod_done, 1)
                    if i is not None or jj + 3 < STEPS:
                        ns = (n0 + jj) % 3
                        dve.wait_ge(hi_done, n + 4)
                        dve.tensor_tensor(wl[ns][:, :], raw[ns][:, :], wh[ns][:, :].bitcast(F32),
                                          ALU.subtract).then_inc(lo_done, 1)
                    else:
                        lo(n0 + jj + 3)
                    dve.wait_ge(h_hi, m + 1)
                    dve.tensor_tensor(hl[s][:, :], pr[s][:, :], hh[s][:, :].bitcast(F32), ALU.subtract) \
                       .then_inc(h_ready, 1)
                    if i is not None or jj + 2 < STEPS:
                        dlo((m0 + jj + 2) % 3, m + 2)

                for j in range(2):
                    dlo((m0 + j) % 3, m0 + j)
                step(0, None, 0)
                with dve.Fori(0, LOOPED // 3) as i:
                    for s in range(1, 4):
                        step(3 * i + s, i, s)
                for j in range(LOOPED + 1, STEPS):
                    step(j, None, j)

            def after(name):
                lo(at[name] + 3)

            dve.memset(zero[:, :].bitcast(F32), 0.0).then_inc(zero_set, 1)
            dve.sem_inc(prod_done, 3)
            dve.wait_ge(pos_loaded, 16)
            dve.wait_ge(con_loaded, 16)
            then(dve.tensor_copy(posf[:, :], posi[:, :]))
            inv = con[:, K_INV:K_INV + ROPE // 2]
            for t in range(NT):
                then(dve.tensor_scalar(ang[:, t, :], inv, posf[:, t:t + 1], None, ALU.mult))
            magic = 1.5 * 2.0 ** 23
            then(dve.tensor_scalar(kk[:, :, :], ang[:, :, :], float(1.0 / (2 * np.pi)), magic, ALU.mult, ALU.add))
            then(dve.tensor_scalar(kk[:, :, :], kk[:, :, :], -magic, None, ALU.add))
            rest = 2 * np.pi
            src = ang
            for bits in (2 ** 5, 2 ** 14, 2 ** 23, None):
                part = float(np.float32(rest)) if bits is None else float(np.floor(rest * bits) / bits)
                rest -= part
                then(dve.scalar_tensor_tensor(out=r0[:, :, :], in0=kk[:, :, :], scalar=-part, in1=src[:, :, :],
                                              op0=ALU.mult, op1=ALU.add))
                src = r0
            pi32 = 3.1415925
            then(dve.tensor_scalar(r0[:, :, :], r0[:, :, :], pi32, -pi32, ALU.min, ALU.max))
            then(dve.tensor_scalar(r1[:, :, :], r0[:, :, :], -1.0, None, ALU.mult))
            then(dve.tensor_tensor(r1[:, :, :], r1[:, :, :], r0[:, :, :], ALU.min))
            dve.tensor_scalar(r1[:, :, :], r1[:, :, :], float(np.pi / 2), None, ALU.add).then_inc(rope_a, 1)
            dve.wait_ge(rope_s, 2)
            dve.tensor_copy(cs[:, :, 32:64], cs[:, :, 0:32]).then_inc(rope_s, 1)
            dve.tensor_scalar(sn[:, :, 0:32], sn[:, :, 32:64], -1.0, None, ALU.mult).then_inc(rope_s, 1)
            dve.wait_ge(rstd_done, 1)
            dve.wait_ge(band_loaded, 16)
            edge = NG * P + NG * EDGE
            dve.tensor_scalar(bandr[:, 0:edge], band[:, 0:edge], rstd[:, 0, 0:1], None, ALU.mult) \
               .then_inc(pool_scaled, 1)
            dve.tensor_scalar(bandr[:, edge:NPOOL], band[:, edge:NPOOL], rstd[:, 0, 1:2], None, ALU.mult) \
               .then_inc(pool_scaled, 1)
            dve.wait_ge(raw_full[0], 32)
            dve.wait_ge(pscale_loaded, 16)
            rv = raw[0][:, :].rearrange("p (g c d) -> p g c d", g=NG, c=2)
            pv_ = pscale[:, :].rearrange("p (g a d) -> p g a d", g=NG, a=1).to_broadcast([P, NG, 2, 256])
            dve.tensor_tensor(rv, rv, pv_, ALU.mult).then_inc(pool_scaled, 1)
            dve.wait_ge(cols_done, 1)
            taps = col[:, C_CDW:C_CDW + 2 * TAPS]
            dve.tensor_scalar(taps, taps, 0.5, None, ALU.mult).then_inc(taps_halved, 1)
            lo(0)
            split_t(0, xh, xl, C_MIX0, 0)
            diagonals(1)
            lo(1)
            lo(2)
            split_t(1, mh, ml, C_MEMN, 4)
            dve.wait_ge(block_used, at["pool"] + 1)
            dve.sem_inc(region_free, 1)
            residual()
            lo(3)
            after("mem0")
            norm(2, 2, C_FFN)
            ffn(0)
            dve.wait_ge(down_done, 3 + STEPS)
            residual()
            after("mem1")
            norm(3, 3, C_MIX1)
            after("down0")
            after("down1")
            for part in range(2):
                dve.wait_ge(mla_rs, part + 1)
                for t in range(NT):
                    dve.tensor_scalar(dqk[:, part, t, :], ident, mst[:, 3, part, t:t + 1], None, ALU.mult) \
                       .then_inc(mla_dg, 1)
                if part == 0:
                    after("down2")
            after("mem2")

            def rope(src, dst, nh, t):
                n = nh * ROPE
                c = cs[:, t:t + 1, :].to_broadcast([P, nh, ROPE])
                s = src.rearrange("p (h d) -> p h d", h=nh)
                a3 = ra[:, 0:n].rearrange("p (h d) -> p h d", h=nh)
                b3 = rb[:, 0:n].rearrange("p (h d) -> p h d", h=nh)
                dve.tensor_tensor(a3, s, c, ALU.mult)
                dve.tensor_tensor(b3[:, :, 0:32], s[:, :, 32:64], sn[:, t:t + 1, 0:32].to_broadcast([P, nh, 32]),
                                  ALU.mult)
                then(dve.tensor_tensor(b3[:, :, 32:64], s[:, :, 0:32],
                                       sn[:, t:t + 1, 32:64].to_broadcast([P, nh, 32]), ALU.mult))
                return dve.tensor_tensor(dst, ra[:, 0:n], rb[:, 0:n], ALU.add)

            for t in range(NT):
                dve.wait_ge(ds_out, 4)
                then(rope(ds[:, t, QLR + KVR:MLA_DOWN], kr[:, t, 0:ROPE], 1, t))
                dve.tensor_copy(kr[:, t, ROPE:P], kr[:, t, 0:ROPE]).then_inc(kr_done, 1)
            for f in range(4):
                dve.wait_ge(cq_hi, f // 2 * 2 + 2)
                dve.scalar_tensor_tensor(out=xl[:, f, :], in0=bank[4 + f // 2][:, (f % 2) * SEQ:(f % 2 + 1) * SEQ],
                                         scalar=col[:, C_QN + f:C_QN + f + 1], in1=xh[:, f, :].bitcast(F32),
                                         op0=ALU.mult, op1=ALU.subtract).then_inc(cq_lo, 1)
            for b in range(3):
                after(f"uq{b}")
            dve.wait_ge(block_used, at["uq2"] + 1)
            for t in range(NT):
                if t:
                    dve.wait_ge(qr_done, t)
                rope(bank[t][:, :], qr[:, t, :], HEADS, t).then_inc(qr_done, 1)
            after("ukv")

            def mla_max(h):
                dve.wait_ge(s_mm, h + 1)
                if h >= 2:
                    dve.wait_ge(p_t, h - 1)
                for t, (a, b) in enumerate(((0, P), (P, 3 * P))):
                    ins = dve.tensor_tensor_reduce(sc[h % 2][:, a:b], bank[4 + h % 2][:, a:b], mask[:, a:b], MLA_SCALE,
                                                   3.0 * NEG, ALU.add, ALU.max, stat[:, h, 0, t:t + 1])
                then(ins)
                dve.tensor_scalar(stat[:, h, 1, :], stat[:, h, 0, :], -1.0, None, ALU.mult).then_inc(s_max, 1)

            def mla_norm(h):
                dve.wait_ge(s_exp, 2 * h + 2)
                then(dve.reciprocal(stat[:, h, 3, :], stat[:, h, 2, :]))
                for t, (a, b) in enumerate(((0, P), (P, 3 * P))):
                    ins = dve.tensor_scalar(sc[h % 2][:, a:b], sc[h % 2][:, a:b], stat[:, h, 3, t:t + 1], None,
                                            ALU.mult)
                    ins.then_inc(s_norm, 1)

            def mla_o(h):
                dve.wait_ge(o_hi, h + 1)
                dve.tensor_tensor(xl[:, h, :], bank[7][:, (h % 2) * SEQ:(h % 2 + 1) * SEQ], xh[:, h, :].bitcast(F32),
                                  ALU.subtract).then_inc(o_lo, 1)

            mla_max(0)
            for h in range(1, HEADS + 1):
                mla_norm(h - 1)
                if h < HEADS:
                    mla_max(h)
                mla_o(h - 1)
                if h in (4, 6):
                    after(f"wo{h // 2 - 2}")
            dve.wait_ge(block_used, at["wo3"] + 1)
            dve.sem_inc(region_free, 1)
            residual()
            after("wo2")
            after("wo3")
            after("mem3")
            norm(4, 4, C_FFN + 8)
            ffn(1)
            dve.wait_ge(down_done, 3 + 2 * STEPS)
            residual()
            after("mem4")
            dve.memset(vbd[:, :], 0.0).then_inc(vbd_zero, 1)
            dve.memset(hc[:, :, 0:PAD], 0.0)
            dve.wait_ge(gain_loaded, 16)
            rescale(5)
            after("mem5")
            norm(6, 5, C_MIXN)
            after("z_a")
            after("z_gt")
            dve.wait_ge(z_out, 1)
            then(dve.scalar_tensor_tensor(out=hc[:, :, PAD:PAD + SEQ], in0=e1[:, :].rearrange("p (a s) -> p a s", a=2),
                                          scalar=1.0, in1=bank[0][:, :].rearrange("p (a s) -> p a s", a=2),
                                          op0=ALU.add, op1=ALU.mult))
            dve.sem_inc(hc_done, 1)

            def conv(k0, k1):
                for k in range(k0, k1):
                    for c in range(2):
                        tap = col[:, C_CDW + 2 * k + c:C_CDW + 2 * k + c + 1]
                        if k == 0:
                            ins = dve.tensor_scalar(yc[:, c, :], hc[:, c, 0:SEQ], tap,
                                                    col[:, C_CDB + c:C_CDB + c + 1], ALU.mult, ALU.add)
                        else:
                            dve.wait_ge(cv_tap, 2 * (k - 1) + c + 1)
                            ins = dve.scalar_tensor_tensor(out=yc[:, c, :], in0=hc[:, c, k:k + SEQ], scalar=tap,
                                                           in1=yc[:, c, :], op0=ALU.mult, op1=ALU.add)
                        ins.then_inc(cv_tap, 1)

            conv(0, 3)
            after("z_kcvc")
            conv(3, 6)
            dve.wait_ge(shifted, 64)
            for a in range(2):
                src = bass.AP(x4[:, a, :, :].tensor, x4[:, a, :, :].offset,
                              [list(x4[:, a, :, :].ap[0]), [2, CMP_KT], [SEQ, GROUPS], [CMP_STRIDE, NCMP]])
                pe_ = col[:, C_PE + a * CMP_KT:C_PE + (a + 1) * CMP_KT]
                pe_ = bass.AP(pe_.tensor, pe_.offset, [list(pe_.ap[0]), [1, CMP_KT], [0, GROUPS], [0, NCMP]])
                dve.tensor_tensor(fl[:, a, :, :, :], src, pe_, ALU.add).then_inc(fl_done, 1)
            after("z_q0")
            conv(6, 8)
            after("z_q1")
            dve.wait_ge(cmp_a, 1)
            hs = bank[7][0:DH, 0:60]
            dve.tensor_scalar(hg[:, 3, :], hg[:, 0, :], GELU_C, 1.0, ALU.mult, ALU.add).then_inc(cmp_d, 1)
            dve.wait_ge(cmp_d, 1)
            dve.tensor_tensor(hg[:, 2, :], hg[:, 3, :], hs, ALU.mult).then_inc(cmp_d, 1)
            dve.wait_ge(cmp_a, 2)
            dve.scalar_tensor_tensor(out=hg[:, 3, :], in0=hg[:, 1, :], scalar=1.0, in1=hs, op0=ALU.add,
                                     op1=ALU.mult).then_inc(cmp_d, 1)
            after("z_ksw")
            conv(8, 11)
            after("z_vsw")
            conv(11, 14)
            dve.wait_ge(gl_a, 1)
            dve.tensor_scalar(gate[:, :, :], gate[:, :, :], 1.0, 0.5, ALU.add, ALU.mult).then_inc(gl_done, 1)
            after("z_gl")
            for i, name in enumerate(("z_v", "z_u")):
                b = bank[(0, 1)[i]]
                dve.wait_ge(gz_a, 2 * i + 1)
                dve.tensor_scalar(e3[:, :], e1[:, :], GELU_C, 1.0, ALU.mult, ALU.add).then_inc(gz_d, 1)
                dve.wait_ge(gz_d, 3 * i + 1)
                dve.tensor_tensor(e2[:, :], e3[:, :], b[:, :], ALU.mult).then_inc(gz_d, 1)
                after(name)
                dve.wait_ge(gz_a, 2 * i + 2)
                dve.scalar_tensor_tensor(out=(vg, uu)[i], in0=e1[:, :], scalar=1.0, in1=b[:, :], op0=ALU.add,
                                         op1=ALU.mult).then_inc(gz_d, 1)
                dve.wait_ge(gz_d, 3 * i + 3)
                if i == 0:
                    for t in range(NT):
                        dve.bn_stats(lst[:, 6 * t:6 * t + 6], vg[:, t * GW:(t + 1) * GW])
                    then(dve.memset(lst[:, 60:61], 0.0))
                    for t in range(NT):
                        dve.bn_aggr(lst[:, 12 + 2 * t:14 + 2 * t], lst[:, 6 * t:6 * t + 6]).then_inc(vn_done, 1)
            dve.wait_ge(ln_rs, 1)
            dve.wait_ge(z_params, 64)
            for t in range(NT):
                then(dve.tensor_scalar(vg[:, t * GW:(t + 1) * GW], vg[:, t * GW:(t + 1) * GW],
                                       lst[:, 12 + 2 * t:13 + 2 * t], lst[:, 20 + t:21 + t], ALU.subtract, ALU.mult))
            v3 = vg.rearrange("p (t c) -> p t c", t=NT)
            then(dve.tensor_tensor(v3, v3, lng[:, 0, 0:1, :].to_broadcast([P, NT, GW]), ALU.mult))
            dve.tensor_tensor(v3, v3, lng[:, 0, 1:2, :].to_broadcast([P, NT, GW]), ALU.add).then_inc(vn_done, 1)
            n240 = NT * NSA_HEADS * NCMP
            dve.wait_ge(sc_mm, GROUPS)

            def m3(ap):
                return ap.rearrange("p (t h n) -> p t h n", t=NT, h=NSA_HEADS)

            def m2(ap):
                return ap.rearrange("p (a n) -> p a n", n=NCMP)

            def over_heads(c0):
                return con[:, c0:c0 + NT * NCMP].rearrange("p (t a n) -> p t a n", t=NT, a=1) \
                    .to_broadcast([P, NT, NSA_HEADS, NCMP])

            def per_row(ap):
                return ap.rearrange("p (a b) -> p a b", b=1).to_broadcast([P, NT * NSA_HEADS, NCMP])

            mx = lst[:, 24:24 + 16]
            for g in range(GROUPS):
                bias = con[:, K_CB:K_CB + NT * NCMP].rearrange("p (t a n) -> p t a n", t=NT, a=1) \
                    .to_broadcast([P, NT, REP, NCMP])
                sc_g = bank[2 + g][:, 0:n240 // GROUPS].rearrange("p (t h n) -> p t h n", t=NT, h=REP)
                then(dve.tensor_tensor(m3(cm[2])[:, :, g * REP:(g + 1) * REP, :], sc_g, bias, ALU.add))
            then(dve.tensor_reduce(mx, m2(cm[2]), AX.X, ALU.max))
            dve.tensor_tensor(m2(cm[0]), m2(cm[2]), per_row(mx), ALU.subtract).then_inc(cm_e, 1)
            dve.wait_ge(cm_e, 2)
            then(dve.tensor_tensor(m3(cm[2]), m3(cm[1]), over_heads(K_C01), ALU.mult))
            then(dve.tensor_reduce(mx, m2(cm[2]), AX.X, ALU.add))
            then(dve.tensor_scalar(mx, mx, TINY, None, ALU.max))
            then(dve.reciprocal(mx, mx))
            dve.wait_ge(gl_done, 1)
            gv = gate[:, :, :].rearrange("p t (h b) -> p t h b", b=3)
            then(dve.tensor_tensor(mx.rearrange("p (t h) -> p t h", t=NT), mx.rearrange("p (t h) -> p t h", t=NT),
                                   gv[:, :, :, 0], ALU.mult))
            dve.tensor_tensor(m2(cm[3]), m2(cm[2]), per_row(mx), ALU.mult).then_inc(pc_done, 1)

            def nsa_max(u):
                dve.wait_ge(n_mm, u + 1)
                if u >= 2:
                    dve.wait_ge(n_t, u - 1)
                for t, (a, b) in enumerate(((0, P), (P, 3 * P))):
                    ins = dve.tensor_tensor_reduce(s2[u % 2][:, a:b], bank[4 + u % 2][:, a:b], mask[:, a:b], NSA_SCALE,
                                                   3.0 * NEG, ALU.add, ALU.max, nst[:, 0, u, t:t + 1])
                then(ins)
                dve.tensor_scalar(nst[:, 1, u, :], nst[:, 0, u, :], -1.0, None, ALU.mult).then_inc(n_max, 1)

            def nsa_norm(u):
                h, br = u // 2, u % 2
                dve.wait_ge(n_exp, 2 * u + 2)
                then(dve.reciprocal(nst[:, 3, u, :], nst[:, 2, u, :]))
                then(dve.tensor_tensor(nst[:, 3, u, :], nst[:, 3, u, :], gv[:, :, h, 1 + br], ALU.mult))
                for t, (a, b) in enumerate(((0, P), (P, 3 * P))):
                    dve.tensor_scalar(s2[u % 2][:, a:b], s2[u % 2][:, a:b], nst[:, 3, u, t:t + 1], None, ALU.mult) \
                       .then_inc(n_norm, 1)

            nsa_max(0)
            for u in range(1, 2 * NSA_HEADS + 1):
                nsa_norm(u - 1)
                if u < 2 * NSA_HEADS:
                    nsa_max(u)
                if u == 1:
                    dve.wait_ge(mix_mm, 1)
                    for t in range(NT):
                        dve.tensor_tensor(yn[:, t, 512:768], bank[7][:, t * GW:(t + 1) * GW], uu[:, t * GW:(t + 1) * GW],
                                          ALU.mult).then_inc(gy_done, 1)
                if u >= 1:
                    conv(min(TAPS, 14 + 2 * (u - 1)), min(TAPS, 14 + 2 * u))
            dve.wait_ge(ycs_t, 1)
            for t in range(NT):
                dve.bn_stats(lst[:, 6 * t:6 * t + 6], bank[3][:, t * CW_:(t + 1) * CW_])
            then(dve.memset(lst[:, 60:61], 0.0))
            for t in range(NT):
                dve.bn_aggr(lst[:, 40 + 2 * t:42 + 2 * t], lst[:, 6 * t:6 * t + 6]).then_inc(vn_done, 1)
            dve.wait_ge(ln_rs, 2)
            for t in range(NT):
                then(dve.tensor_scalar(e3[:, t * GW:(t + 1) * GW], bank[3][:, t * GW:(t + 1) * GW],
                                       lst[:, 40 + 2 * t:41 + 2 * t], lst[:, 44 + t:45 + t], ALU.subtract, ALU.mult))
            e3v = e3[:, :].rearrange("p (t c) -> p t c", t=NT)
            e2v = e2[:, :].rearrange("p (t c) -> p t c", t=NT)
            then(dve.tensor_tensor(e3v, e3v, lng[:, 1, 0:1, :].to_broadcast([P, NT, GW]), ALU.mult))
            dve.tensor_tensor(e2v, e3v, lng[:, 1, 1:2, :].to_broadcast([P, NT, GW]), ALU.add).then_inc(cvln_done, 1)
            dve.wait_ge(cv_a, 1)
            dve.scalar_tensor_tensor(out=yn[:, :, 768:1024], in0=e1[:, :].rearrange("p (t c) -> p t c", t=NT), scalar=1.0,
                                     in1=e2v, op0=ALU.add, op1=ALU.mult).then_inc(cy_done, 1)
            dve.wait_ge(y_rs, 1)
            for s in range(3):
                for t in range(NT):
                    dve.tensor_scalar(dseg[:, 2 * s + t, :], ident, lst[:, 48 + 2 * s + t:49 + 2 * s + t], None, ALU.mult) \
                       .then_inc(y_dg, 1)
            split_t(6, xh, xl, C_MOUT, 0)
            for i in range(3):
                after(f"wout{i}")
            dve.wait_ge(block_used, at["wout3"] + 1)
            residual()
            after("wout3")
            after("mem6")
            after("mem7")
            norm(7, 7, C_XN)
            def x_max(h):
                dve.wait_ge(a_mm, h + 1)
                then(dve.tensor_reduce(xst[:, h, 0, :], bank[4 + h % 2][:, :].rearrange("p (t s) -> p t s", t=NT), AX.X,
                                       ALU.max))
                dve.tensor_scalar(xst[:, h, 1, :], xst[:, h, 0, :], -XSCALE, None, ALU.mult).then_inc(a_max, 1)

            def x_norm(h):
                dve.wait_ge(a_exp, 2 * h + 2)
                then(dve.reciprocal(xst[:, h, 3, :], xst[:, h, 2, :]))
                for t in range(NT):
                    dve.tensor_scalar(sx[h % 2][:, t, :], sx[h % 2][:, t, :], xst[:, h, 3, t:t + 1], None, ALU.mult) \
                       .then_inc(a_norm, 1)

            def x_o(h):
                dve.wait_ge(ao_hi, h + 1)
                dve.tensor_tensor(ml[:, 2 * h:2 * h + 2, :].rearrange("p a s -> p (a s)"), bank[7][:, :],
                                  mh[:, 2 * h:2 * h + 2, :].rearrange("p a s -> p (a s)").bitcast(F32),
                                  ALU.subtract).then_inc(ao_lo, 1)

            after("xq0")
            for h in range(1, XHEADS + 1):
                x_max(h - 1)
                if h < XHEADS:
                    after(f"xq{h}")
                x_norm(h - 1)
                x_o(h - 1)
            for i in range(3):
                after(f"xo{i}")
            dve.wait_ge(block_used, at["xo3"] + 1)
            dve.sem_inc(region_free, 1)
            residual()
            after("xo3")
            norm(8, 8, C_FN2)
            ffn(2)
            dve.wait_ge(down_done, 3 + 3 * STEPS)
            residual()
            dve.wait_ge(last_gain_loaded, 16)
            rescale(9)

        @block.gpsimd
        def _(pool):
            order = [0]

            def then(ins):
                order[0] += 1
                ins.then_inc(pool_order, 1)
                pool.wait_ge(pool_order, order[0])

            def inverse_rms(q):
                pool.wait_ge(sq_done, 4 * (q + 1))
                then(pool.tensor_tensor(st1[:, q, :], ss[:, q, :, 0], ss[:, q, :, 1], ALU.add))
                then(pool.tensor_scalar(st2[:, q, :], st1[:, q, :], 1.0 / D, EPS, ALU.mult, ALU.add))
                pool.tensor_tensor(rstd[:, q, :], st2[:, q, :], mhalf[:, 0:NT], ALU.pow).then_inc(rstd_done, 1)

            then(pool.memset(mhalf[:, :], -0.5))
            for q in range(4):
                inverse_rms(q)
            for part, width in ((0, QLR), (1, KVR)):
                pool.wait_ge(mla_sq, 2 * part + 2)
                then(pool.tensor_scalar(mst[:, 1, part, :], mst[:, 0, part, :], 1.0 / width, EPS, ALU.mult, ALU.add))
                pool.tensor_tensor(mst[:, 3, part, :], mst[:, 1, part, :], mhalf[:, 0:NT], ALU.pow).then_inc(mla_rs, 1)
            inverse_rms(4)
            pool.wait_ge(down_done, 3 + 2 * STEPS)
            pool.dma_start(cw1[:, :, :, :], w["cmp_w1_2"][0].rearrange("a (k p) d -> p a k d", p=P)).then_inc(z_ws, 16)
            pool.dma_start(cw2[:, :, :], w["cmp_w2_2"][0].rearrange("a p d -> p a d")).then_inc(z_ws, 16)
            pool.dma_start(bsr[:, :], w["gmlp_bs_2"][0]).then_inc(z_ws, 16)
            for i, name in enumerate(("gmlp_ln_g_2", "gmlp_ln_b_2", "conv_ln_g_2", "conv_ln_b_2")):
                pool.dma_start(lng[:, i // 2, i % 2, :], w[name][0:1, :].to_broadcast([P, GW])).then_inc(z_params, 16)
            inverse_rms(5)
            pool.wait_ge(scaled, 4)
            pool.dma_start(gain[:, :], w["final_norm_g_2"].rearrange("(a d) -> a d", a=1).to_broadcast([P, D])) \
                .then_inc(last_gain_loaded, 16)
            inverse_rms(6)
            pool.wait_ge(cmp_mm, 1)
            pool.dma_start(ws.rearrange("p (g s) -> p g s", g=GG), w["gmlp_ws_2"][0].rearrange("g t s -> t g s")) \
                .then_inc(ws_loaded, 16)
            pool.wait_ge(ws_loaded, 16)
            w3 = ws.rearrange("p (g s) -> p g s", g=GG)
            pool.affine_select(out=w3, in_=w3, compare_op=ALU.is_ge, fill=0.0, base=0,
                               pattern=[[0, GG], [-1, P]], channel_multiplier=1).then_inc(ws_cut, 1)
            for i, (src, dst) in enumerate(((12, 20), (40, 44))):
                pool.wait_ge(vn_done, 2 if i == 0 else 5)
                var = lst[:, src:src + 4].rearrange("p (t b) -> p t b", b=2)[:, :, 1]
                then(pool.tensor_scalar(lst[:, 16 + 2 * i:18 + 2 * i], var, 1.0, 4.0 * EPS if i == 0 else EPS,
                                        ALU.mult, ALU.add))
                pool.tensor_tensor(lst[:, dst:dst + 2], lst[:, 16 + 2 * i:18 + 2 * i], mhalf[:, 0:NT], ALU.pow) \
                    .then_inc(ln_rs, 1)
            pool.wait_ge(y_sq, 6)
            then(pool.tensor_scalar(lst[:, 54:56], lst[:, 32:34], 1.0 / 512, EPS, ALU.mult, ALU.add))
            then(pool.tensor_scalar(lst[:, 56:60], lst[:, 34:38], 1.0 / 256, 4.0 * EPS, ALU.mult, ALU.add))
            pool.tensor_tensor(lst[:, 48:54], lst[:, 54:60], mhalf[:, 0:6], ALU.pow).then_inc(y_rs, 1)
            inverse_rms(7)
            inverse_rms(8)
            inverse_rms(9)

        @block.tensor
        def _(pe):
            def three(outp, a_hi, a_lo, b_hi, b_lo, start, stop, **kw):
                pe.matmul(outp, a_hi, b_hi, start=start, stop=False, **kw)
                pe.matmul(outp, a_hi, b_lo, start=False, stop=False, **kw)
                return pe.matmul(outp, a_lo, b_hi, start=False, stop=stop, **kw)

            def weights(name, k, c):
                n = at[name]
                pe.wait_ge(lo_done, n + 1)
                return k_view(wh[n % 3], k, c), k_view(wl[n % 3], k, c)

            def transpose_norm(e, src, dg, banks):
                for k in range(KD):
                    for t in range(NT):
                        o = bank[banks + k // 2][:, (k % 2) * SEQ + t * P:(k % 2) * SEQ + (t + 1) * P]
                        ins = pe.matmul(o, src[:, t, k * P:(k + 1) * P], dg(k, t), start=True, stop=True)
                    if k % 2:
                        ins.then_inc(t_done, 1)

            def columns(name, b, a_hi, a_lo, sub=None):
                h_, l_ = weights(name, KD, 2 * P)
                for f in range(2):
                    for k in range(KD):
                        s = (lambda v: v[:, k, f * P:(f + 1) * P]) if sub is None else (lambda v: sub(v, k, f))
                        ins = three(bank[b][:, f * SEQ:(f + 1) * SEQ], s(h_), s(l_), a_hi[:, k, :], a_lo[:, k, :],
                                    k == 0, k == KD - 1)
                ins.then_inc(block_used, 1)

            def tokens(name, b, width, a_hi, a_lo, at_col=None):
                h_, l_ = weights(name, KD, width)
                for t in range(NT):
                    for k in range(KD):
                        c = width * t if at_col is None else at_col
                        bb = b if at_col is None else b + t
                        ins = three(bank[bb][:, c:c + width], a_hi[:, k, t * P:(t + 1) * P],
                                    a_lo[:, k, t * P:(t + 1) * P], h_[:, k, :], l_[:, k, :], k == 0, k == KD - 1)
                ins.then_inc(block_used, 1)

            def row_block(name, i, a_hi, a_lo, first, last):
                h_, l_ = weights(name, 2, D)
                for kk_ in range(2):
                    for t in range(NT):
                        for c in range(2):
                            ins = three(bank[2 * t + c][:, :], a_hi[:, 2 * i + kk_, t * P:(t + 1) * P],
                                        a_lo[:, 2 * i + kk_, t * P:(t + 1) * P], h_[:, kk_, c * HALF:(c + 1) * HALF],
                                        l_[:, kk_, c * HALF:(c + 1) * HALF], first and kk_ == 0, last and kk_ == 1)
                ins.then_inc(block_used, 1)

            def mem_block(i):
                if i > 0:
                    pe.wait_ge(mem_out, i)
                if i < 4:
                    columns(f"mem{i}", 7, mh, ml)
                else:
                    tokens(f"mem{i}", 7, 2 * P, mh, ml)

            def norm(e, nd):
                pe.wait_ge(diag_done, nd)
                transpose_norm(e, xt, lambda k, t: diag[:, t, :], 0)
                pe.wait_ge(t_lo, KD * (e + 1))

            def ffn(layer):
                n0, m0 = at[f"ffn{layer}"], STEPS * layer
                for b in range(4):
                    pe.matmul(bank[b][:, :], zero[:, :], xh[:, 0:2, :], start=True, stop=False, skip_group_check=True)

                def up(j, jj):
                    n, m = n0 + j, m0 + j
                    ns, s = (n0 + jj) % 3, (m0 + jj) % 3
                    pe.wait_ge(lo_done, n + 1)
                    pe.wait_ge(prod_done, m + 1)
                    for half in range(2):
                        for k in range(KD):
                            a = (2 * k + half) * P
                            ins = three(bank[4 + s][:, half * SEQ:(half + 1) * SEQ], wh[ns][:, a:a + P],
                                        wl[ns][:, a:a + P], xh[:, k, :], xl[:, k, :], k == 0, k == KD - 1)
                    ins.then_inc(block_used, 1)

                def down(j, jj, last=False):
                    m = m0 + j
                    s = (m0 + jj) % 3
                    pe.wait_ge(d_lo, m + 1)
                    pe.wait_ge(h_ready, m + 1)
                    for t in range(NT):
                        for c in range(2):
                            ins = three(bank[2 * t + c][:, :], hh[s][:, t * P:(t + 1) * P], hl[s][:, t * P:(t + 1) * P],
                                        dh[s][:, c * HALF:(c + 1) * HALF], dl[s][:, c * HALF:(c + 1) * HALF],
                                        False, last, skip_group_check=True)
                    ins.then_inc(down_done, 1)

                up(0, 0)
                with pe.Fori(0, LOOPED // 3) as i:
                    for s in range(1, 4):
                        up(3 * i + s, s)
                        down(3 * i + s - 1, s - 1)
                for j in range(LOOPED + 1, STEPS):
                    up(j, j)
                    down(j - 1, j - 1)
                down(STEPS - 1, STEPS - 1, True)

            pe.sem_inc(down_done, 3)
            pe.wait_ge(con_loaded, 16)
            pe.wait_ge(rows_loaded, 16 * 15)
            c = 0
            for i, n in enumerate((C_CDW, 2 * TAPS + 2 * CMP_KT, 2 * NF2, 2 * NF2)):
                ins = pe.transpose(bank[7][:, c:c + n], prow[i][0:n, :], con[0:n, K_ID:K_ID + n])
                c += n
            ins.then_inc(cols_t, 1)
            pe.wait_ge(zero_set, 1)
            pe.wait_ge(x_loaded, 16 * NT)
            pe.wait_ge(pool_scaled, 2)
            for k in range(KD):
                g = k // 2
                o = (k % 2) * SEQ
                b = bank[k // 2]
                ks = slice(k * P, (k + 1) * P)
                e0, d1 = NG * P + g * EDGE, NG * P + NG * EDGE + g * P
                pe.matmul(b[:, o:o + P], xt[:, 0, ks], bandr[:, g * P:(g + 1) * P], start=True, stop=True)
                pe.matmul(b[:, o + P:o + SEQ], xt[:, 1, ks], bandr[:, d1:d1 + P], start=True, stop=True)
                ins = pe.matmul(b[:, o + P:o + P + EDGE], xt[:, 0, ks], bandr[:, e0:e0 + EDGE], start=False, stop=True,
                                skip_group_check=True)
                if k % 2:
                    ins.then_inc(t_done, 1)
            pe.wait_ge(t_lo, KD)
            h_, l_ = weights("pool", 2 * NG, 256)
            for t in range(NT):
                for g in range(NG):
                    for c in range(2):
                        k = 2 * g + c
                        ins = three(bank[2 * t + g // 2][:, (g % 2) * 256:(g % 2 + 1) * 256],
                                    xh[:, k, t * P:(t + 1) * P], xl[:, k, t * P:(t + 1) * P],
                                    h_[:, k, :], l_[:, k, :], c == 0, c == 1)
            ins.then_inc(block_used, 1)
            pe.wait_ge(mem_loaded, 16)
            pe.wait_ge(diag_done, 2)
            pe.wait_ge(cols_done, 1)
            transpose_norm(1, memt, lambda k, t: diag[:, t, :], 4)
            pe.wait_ge(t_lo, 2 * KD)
            mem_block(0)
            norm(2, 4)
            ffn(0)
            mem_block(1)
            norm(3, 6)
            for b in range(3):
                tokens(f"down{b}", (0, 0, 2)[b], MLA_DOWN // 3, xh, xl, at_col=(0, 192, 0)[b])
            mem_block(2)
            for f in range(4):
                part = f // 3
                pe.wait_ge(mla_dg, 2 * part + 2)
                for t in range(NT):
                    ins = pe.matmul(bank[4 + f // 2][:, (f % 2) * SEQ + t * P:(f % 2) * SEQ + (t + 1) * P],
                                    ds[:, t, f * P:(f + 1) * P], dqk[:, part, t, :], start=True, stop=True)
                if f % 2:
                    ins.then_inc(cq_t, 1)
            pe.wait_ge(kr_done, 2)
            for t in range(NT):
                ins = pe.transpose(bank[6][:, t * P:(t + 1) * P], kr[:, t, :], ident)
            ins.then_inc(kr_t, 1)
            pe.wait_ge(cq_lo, 4)
            hw = NOPE + ROPE
            for b, nh in enumerate((3, 3, 2)):
                h_, l_ = weights(f"uq{b}", 3, nh * hw)
                for i in range(nh):
                    h = 3 * b + i
                    if h >= 4 and h % 2 == 0:
                        pe.wait_ge(qk_out, h // 2 - 1)
                    for k in range(3):
                        ins = three(bank[4 + (h % 4) // 2][:, (h % 2) * SEQ:(h % 2 + 1) * SEQ],
                                    h_[:, k, i * hw:i * hw + NOPE], l_[:, k, i * hw:i * hw + NOPE],
                                    xh[:, k, :], xl[:, k, :], k == 0, k == 2)
                    if h % 2:
                        ins.then_inc(qk_mm, 1)
                for t in range(NT):
                    for k in range(3):
                        def rp(v):
                            return v[:, k, :].rearrange("p (h c) -> p h c", c=hw)[:, :, NOPE:hw]
                        ins = three(bank[t][:, 3 * b * ROPE:(3 * b + nh) * ROPE], xh[:, k, t * P:(t + 1) * P],
                                    xl[:, k, t * P:(t + 1) * P], rp(h_), rp(l_), k == 0, k == 2)
                ins.then_inc(block_used, 1)
            h_, l_ = weights("ukv", 1, 2048)
            pe.wait_ge(kr_out, 1)
            for h in range(HEADS):
                if h % 2 == 0:
                    pe.wait_ge(qk_out, 3 + h // 2)
                a = 2 * P * h
                ins = three(bank[4 + (h % 4) // 2][:, (h % 2) * SEQ:(h % 2 + 1) * SEQ], h_[:, 0, a:a + P], l_[:, 0, a:a + P],
                            xh[:, 3, :], xl[:, 3, :], True, True)
                if h % 2:
                    ins.then_inc(qk_mm, 1)
            for i in range(4):
                t, hv = i // 2, i % 2
                if i == 3:
                    pe.wait_ge(v_out, 1)

                def vp(v):
                    return v[:, 0, :].rearrange("p (h c) -> p h c", c=2 * P)[:, 4 * hv:4 * hv + 4, P:2 * P]
                ins = three(bank[(2, 3, 6, 2)[i]][:, :], xh[:, 3, t * P:(t + 1) * P], xl[:, 3, t * P:(t + 1) * P],
                            vp(h_), vp(l_), True, True)
                if i < 3:
                    ins.then_inc(v_mm, 1)
            ins.then_inc(v_mm, 1)
            pe.sem_inc(block_used, 1)
            pe.wait_ge(qr_done, 2)
            for i in range(4):
                for t in range(NT):
                    ins = pe.transpose(bank[i // 2][:, (i % 2) * SEQ + t * P:(i % 2) * SEQ + (t + 1) * P],
                                       qr[:, t, i * P:(i + 1) * P], ident)
                if i % 2:
                    ins.then_inc(qr_t, 1)
            pe.wait_ge(qr_out, 2)
            pe.wait_ge(v_out, 4)
            pe.wait_ge(qk_out, HEADS)

            def mla_scores(h):
                if h >= 2:
                    pe.wait_ge(s_max, h - 1)
                half = slice((h % 2) * ROPE, (h % 2 + 1) * ROPE)
                for t, (a, b, keys) in enumerate(((0, P, P), (P, 3 * P, SEQ))):
                    o = bank[4 + h % 2][:, a:b]
                    tok = slice(t * P, (t + 1) * P)
                    pe.matmul(o, qn[:, h, tok], kn[:, h, 0:keys], start=True, stop=False)
                    ins = pe.matmul(o, qrt[half, h // 2, tok], krt[half, 0:keys], start=False, stop=True)
                ins.then_inc(s_mm, 1)

            def mla_pt(h):
                pe.wait_ge(s_norm, 2 * h + 2)
                if h >= 1:
                    pe.wait_ge(p_out, h)
                for i, a in enumerate((0, P, 2 * P)):
                    ins = pe.transpose(bank[6][:, i * P:(i + 1) * P], sc[h % 2][:, a:a + P], ident)
                ins.then_inc(p_t, 1)

            def mla_pv(h):
                pe.wait_ge(p_out, h + 1)
                if h >= 1:
                    pe.wait_ge(o_lo, h)
                o = (h % 2) * SEQ
                pe.matmul(bank[7][:, o:o + SEQ], vv[:, 0, h * P:(h + 1) * P], pt[h % 2][:, 0:SEQ], start=True, stop=True)
                pe.matmul(bank[7][:, o + P:o + SEQ], vv[:, 1, h * P:(h + 1) * P], pt[h % 2][:, SEQ:SEQ + P], start=False,
                          stop=True, skip_group_check=True).then_inc(o_mm, 1)

            pe.wait_ge(mem_out, 3)
            mla_scores(0)
            for h in range(1, HEADS + 1):
                if h < HEADS:
                    mla_scores(h)
                mla_pt(h - 1)
                mla_pv(h - 1)
                if h in (3, 5, 7):
                    i = (h - 3) // 2
                    pe.wait_ge(o_lo, 2 * i + 2)
                    row_block(f"wo{i}", i, xh, xl, i == 0, False)
            pe.wait_ge(o_lo, HEADS)
            row_block("wo3", 3, xh, xl, False, True)
            mem_block(3)
            norm(4, 8)
            ffn(1)
            mem_block(4)
            mem_block(5)
            norm(5, 10)
            def z_bank(i):
                return i % 4

            columns("z_a", 0, xh, xl)
            columns("z_gt", 1, xh, xl)
            columns("z_kcvc", 2, xh, xl)

            columns("z_q0", 3, xh, xl)
            pe.wait_ge(hc_done, 1)
            columns("z_q1", 0, xh, xl)
            pe.wait_ge(fl_done, 2)
            pe.wait_ge(z_ws, 48)
            pe.wait_ge(mem_out, 6)
            for a in range(2):
                for k in range(CMP_KT):
                    ins = pe.matmul(bank[7][0:DH, 30 * a:30 * a + 30], cw1[:, a, k, :],
                                    fl[:, a, k, :, :].rearrange("p g n -> p (g n)"), start=k == 0, stop=k == CMP_KT - 1)
            ins.then_inc(cmp_mm, 1)
            columns("z_ksw", 1, xh, xl)
            pe.wait_ge(cmp_d, 3)
            for g in range(GROUPS):
                pe.matmul(bank[7][g * DH:(g + 1) * DH, 64:64 + NCMP], cw2[:, 0, :], hg[:, 3, g * NCMP:(g + 1) * NCMP],
                          start=True, stop=True)
            for g in range(GROUPS):
                ins = pe.matmul(bank[7][0:NCMP, 128 + g * DH:128 + (g + 1) * DH],
                                hg[:, 3, 30 + g * NCMP:30 + (g + 1) * NCMP], cw2[:, 1, :], start=True, stop=True)
            ins.then_inc(cmp_mm, 1)
            pe.wait_ge(z_out, 2)
            tokens("z_vsw", 2, 2 * P, xh, xl)
            pe.wait_ge(z_out, 3)
            tokens("z_gl", 3, 24, xh, xl)
            pe.wait_ge(z_out, 4)
            tokens("z_v", 0, GW, xh, xl)
            pe.wait_ge(z_out, 5)
            tokens("z_u", 1, GW, xh, xl)
            pe.wait_ge(ws_cut, 1)
            for g in range(GG):
                ins = pe.transpose(bank[6][:, g * P:(g + 1) * P], ws[:, g * P:(g + 1) * P], ident)
            ins.then_inc(ws_t, 1)
            pe.wait_ge(z_out, 6)
            pe.wait_ge(cmp_out, 2)
            pe.wait_ge(gl_a, 1)
            for g in range(GROUPS):
                rows_ = slice(g * DH, (g + 1) * DH)
                for t, j in ((t, j) for t in range(NT) for j in range(REP)):
                    c = (t * REP + j) * NCMP
                    ins = pe.matmul(bank[2 + g][:, c:c + NCMP], qt[rows_, j, t * P:(t + 1) * P], kcm[rows_, :], start=True,
                                    stop=True)
                ins.then_inc(sc_mm, 1)

            def nsa_scores(u):
                if u >= 2:
                    pe.wait_ge(n_max, u - 1)
                h, br = u // 2, u % 2
                g, j = h // REP, h % REP
                rows_ = slice(g * DH, (g + 1) * DH)
                for t, (a, b, keys) in enumerate(((0, P, P), (P, 3 * P, SEQ))):
                    ins = pe.matmul(bank[4 + u % 2][:, a:b], qt[rows_, j, t * P:(t + 1) * P], ksw[rows_, br, 0:keys],
                                    start=True, stop=True)
                ins.then_inc(n_mm, 1)

            nsa_scores(0)
            pe.wait_ge(ws_out, 1)
            pe.wait_ge(vn_done, 3)
            for t in range(NT):
                pe.matmul(bank[7][:, t * GW:(t + 1) * GW], bsr[:, :], con[0:GG, K_SEL:K_SEL + GW], start=True, stop=False,
                          skip_group_check=True)
                for g in range(GG):
                    o = t * GW + g * GW // GG
                    ins = pe.matmul(bank[7][:, o:o + GW // GG], wst[:, g, :], vg[:, o:o + GW // GG], start=False,
                                    stop=g == GG - 1, skip_group_check=True)
            ins.then_inc(mix_mm, 1)
            pe.wait_ge(pc_done, 1)
            for t in range(NT):
                pe.transpose(bank[6][0:120, t * P:(t + 1) * P], cm[3][:, t * 120:(t + 1) * 120], ident).then_inc(pc_t, 1)
            pe.wait_ge(pc_out, 1)
            pe.wait_ge(vbd_set, 16 * NSA_HEADS)
            pe.wait_ge(gz_d, 6)
            for t in range(NT):
                pe.matmul(bank[t][:, :], e1[0:120, t * P:(t + 1) * P], vbd[0:120, :], start=True, stop=False,
                          skip_group_check=True)

            def nsa_pt(u):
                pe.wait_ge(n_norm, 2 * u + 2)
                if u >= 1:
                    pe.wait_ge(n_out, u)
                for i, a in enumerate((0, P, 2 * P)):
                    ins = pe.transpose(bank[6][:, i * P:(i + 1) * P], s2[u % 2][:, a:a + P], ident)
                ins.then_inc(n_t, 1)

            def nsa_pv(u):
                h, br = u // 2, u % 2
                g = h // REP
                pe.wait_ge(n_out, u + 1)
                p_ = p2[u % 2]
                v0 = vsw[:, 0, br * P + g * DH:br * P + (g + 1) * DH]
                v1 = vsw[:, 1, br * P + g * DH:br * P + (g + 1) * DH]
                hs = slice(h * DH, (h + 1) * DH)
                last = u == 2 * NSA_HEADS - 1
                pe.matmul(bank[0][:, hs], p_[:, 0:P], v0, start=False, stop=last, skip_group_check=True)
                pe.matmul(bank[1][:, hs], p_[:, P:2 * P], v0, start=False, stop=False, skip_group_check=True)
                pe.matmul(bank[1][:, hs], p_[:, 2 * P:3 * P], v1, start=False, stop=last, skip_group_check=True) \
                  .then_inc(o_all, 1)

            for u in range(1, 2 * NSA_HEADS + 1):
                if u < 2 * NSA_HEADS:
                    nsa_scores(u)
                nsa_pt(u - 1)
                nsa_pv(u - 1)
            pe.wait_ge(cv_tap, 2 * TAPS)
            pe.wait_ge(gl_a, 1)
            for t in range(NT):
                for c in range(2):
                    ins = pe.transpose(bank[3][:, t * CW_ + c * P:t * CW_ + (c + 1) * P], yc[:, c, t * P:(t + 1) * P],
                                       ident)
            ins.then_inc(ycs_t, 1)
            pe.wait_ge(y_dg, 6)
            seg = (0, 0, 0, 0, 1, 1, 2, 2)
            transpose_norm(6, yn, lambda k, t: dseg[:, 2 * seg[k] + t, :], 0)
            pe.wait_ge(t_lo, KD * 7)
            for i in range(4):
                row_block(f"wout{i}", i, xh, xl, i == 0, i == 3)
            mem_block(6)
            mem_block(7)
            norm(7, 12)
            pe.wait_ge(mem_out, 8)

            def x_q(h):
                if h >= 1:
                    pe.wait_ge(q_out, h)
                columns(f"xq{h}", 0, xh, xl)

            def x_scores(h):
                pe.wait_ge(q_out, h + 1)
                if h >= 2:
                    pe.wait_ge(a_exp, 2 * h - 2)
                for t in range(NT):
                    for f in range(2):
                        ins = pe.matmul(bank[4 + h % 2][:, t * SEQ:(t + 1) * SEQ], qx[:, 2 * h + f, t * P:(t + 1) * P],
                                        km[:, 2 * h + f, :], start=f == 0, stop=f == 1)
                ins.then_inc(a_mm, 1)

            def x_pt(h):
                pe.wait_ge(a_norm, 2 * h + 2)
                if h >= 1:
                    pe.wait_ge(a_out, h)
                for kt in range(NT):
                    for t in range(NT):
                        ins = pe.transpose(bank[6][:, kt * SEQ + t * P:kt * SEQ + (t + 1) * P],
                                           sx[h % 2][:, t, kt * P:(kt + 1) * P], ident)
                ins.then_inc(a_t, 1)

            def x_pv(h):
                pe.wait_ge(a_out, h + 1)
                if h >= 1:
                    pe.wait_ge(ao_lo, h)
                for f in range(2):
                    for kt in range(NT):
                        c = h * XHD + f * P
                        ins = pe.matmul(bank[7][:, f * SEQ:(f + 1) * SEQ], vm[:, kt, c:c + P], px[h % 2][:, kt, :],
                                        start=kt == 0, stop=kt == NT - 1)
                ins.then_inc(ao_mm, 1)

            x_q(0)
            for h in range(1, XHEADS + 1):
                x_scores(h - 1)
                if h < XHEADS:
                    x_q(h)
                x_pt(h - 1)
                x_pv(h - 1)
            pe.wait_ge(ao_lo, XHEADS)
            for i in range(4):
                row_block(f"xo{i}", i, mh, ml, i == 0, i == 3)
            norm(8, 14)
            ffn(2)


INPUTS = (
    "x", "positions", "norm_mix", "norm_ffn", "norm_final", "pool_w", "pool_scale", "mla_w_down", "mla_q_norm",
    "mla_w_uq", "mla_kv_norm", "mla_w_ukv", "mla_w_o", "ffn_w_gate", "ffn_w_up", "ffn_w_down", "mem_2",
    "mix_norm_g_2", "w_in_2", "cmp_pe_2", "cmp_w1_2", "cmp_w2_2", "gmlp_ln_g_2", "gmlp_ln_b_2", "gmlp_ws_2",
    "gmlp_bs_2", "conv_dw_w_2", "conv_dw_b_2", "conv_ln_g_2", "conv_ln_b_2", "mix_out_g_2", "w_out_2",
    "xattn_norm_g_2", "mem_norm_g_2", "xattn_wq_2", "xattn_wk_2", "xattn_wv_2", "xattn_wo_2", "ffn_norm_g_2",
    "ffn_w_up_2", "ffn_dw_w_2", "ffn_dw_b_2", "ffn_w_down_2", "final_norm_g_2",
)


def kernel(**inputs):
    import numpy as _np
    import concourse.bacc as _bacc
    from concourse import mybir as _mybir
    from concourse.bass_utils import run_bass_kernel_spmd as _run

    nc = _bacc.Bacc("TRN2", target_bir_lowering=False, num_devices=1)
    arrays, w = {}, {}
    for name in INPUTS:
        a = _np.ascontiguousarray(inputs[name])
        arrays[f"in_{name}"] = a
        w[name] = nc.dram_tensor(f"in_{name}", a.shape, _mybir.dt.from_np(a.dtype), kind="ExternalInput").ap()
    extra = []
    for name, a in zip(("consts", "bands"), constants()):
        arrays[f"in_{name}"] = a
        extra.append(nc.dram_tensor(f"in_{name}", a.shape, _mybir.dt.from_np(a.dtype), kind="ExternalInput").ap())
    out = nc.dram_tensor("out_x", (1, SEQ, D), F32, kind="ExternalOutput").ap()
    build(nc, w, *extra, out)
    r = _run(nc, [arrays], core_ids=[0])
    return r.results[0]["out_x"]
```

```python
from contextlib import ExitStack

import numpy as np

import concourse.bass as bass
from concourse import mybir

F32 = mybir.dt.float32
F32R = mybir.dt.float32r
I32 = mybir.dt.int32
ACT = mybir.ActivationFunctionType
ALU = mybir.AluOpType
AX = mybir.AxisListType

P = 128
SEQ = 256
NT = SEQ // P
D = 1024
KD = D // P
HALF = 512
EPS = 1e-6
ROOT_D = 2.0 ** -5
assert D * ROOT_D ** 2 == 1.0
NEG = -1e30
TINY = 1e-30

POOL_WINDOWS = (2, 4, 8, 16)
NG = len(POOL_WINDOWS)
EDGE = max(POOL_WINDOWS)

HEADS = 8
NOPE = 128
ROPE = 64
QLR = 384
KVR = 128
MLA_DOWN = QLR + KVR + ROPE
MLA_SCALE = float(NOPE + ROPE) ** -0.5

FF = 2816
STEPS = FF // P
LOOPED = 18

NSA_HEADS = 8
DH = 64
GROUPS = 2
REP = NSA_HEADS // GROUPS
NSA_SCALE = float(DH) ** -0.5
CMP_BLOCK = 32
CMP_STRIDE = 16
NCMP = (SEQ - CMP_BLOCK) // CMP_STRIDE + 1
CMP_KT = CMP_BLOCK * DH // P
GW = 256
GG = 4
CW_ = 256
TAPS = 31
PAD = TAPS - 1
FTAPS = 3
XHEADS = 4
XHD = D // XHEADS
XSCALE = float(XHD) ** -0.5
GELU_C = 0.044715
GELU_S = float(np.sqrt(2.0 / np.pi))

WOUT_ORDER = (2, 3, 0, 1)
TAPS_BEFORE = 14
U_TURN, U_STATS, U_LN, U_SILU, U_SQUARES, U_TURN_Y, U_SPLIT = 7, 8, 9, 10, 12, 14, 15

C_MIX0, C_MIX1, C_FFN = 0, 8, 16
C_QN, C_KVN = 32, 35
C_MIXN, C_MOUT, C_XN, C_MEMN, C_FN2 = 36, 44, 52, 60, 68
C_CDB = 76
C_CDW = 78
C_PE = C_CDW + 2 * TAPS
C_DW = C_PE + 2 * CMP_KT
NF2 = 2 * FF // P
NCOLS = C_DW + 4 * NF2

K_ID = 0
K_MASK = K_ID + P
K_CB = K_MASK + 3 * P
K_C01 = K_CB + NT * NCMP
K_INV = K_C01 + NT * NCMP
K_SEL = K_INV + ROPE // 2
NCONST = K_SEL + GW
NPOOL = NG * P + NG * EDGE + NG * P


def constants():
    c = np.zeros((P, NCONST), np.float32)
    c[:, K_ID:K_ID + P] = np.eye(P, dtype=np.float32)
    causal = np.where(np.arange(P)[None, :] <= np.arange(P)[:, None], 0.0, NEG).astype(np.float32)
    c[:, K_MASK:K_MASK + P] = causal
    c[:, K_MASK + 2 * P:K_MASK + 3 * P] = causal
    t = np.arange(SEQ).reshape(NT, P)
    end = np.arange(NCMP) * CMP_STRIDE + CMP_BLOCK - 1
    ok = (end[None, None, :] <= t[:, :, None]).transpose(1, 0, 2).reshape(P, NT * NCMP)
    c[:, K_CB:K_CB + NT * NCMP] = np.where(ok, 0.0, NEG)
    c[:, K_C01:K_C01 + NT * NCMP] = ok
    theta = np.float32(10000.0)
    power = np.arange(0, ROPE, 2, dtype=np.float32) / np.float32(ROPE)
    c[:, K_INV:K_INV + ROPE // 2] = (np.float32(1.0) / (theta ** power).astype(np.float32))[None, :]
    for g in range(GG):
        c[g, K_SEL + g * GW // GG:K_SEL + (g + 1) * GW // GG] = 1.0
    bands = np.zeros((P, NPOOL), np.float32)
    full = np.zeros((NG, SEQ, SEQ), np.float64)
    for g, win in enumerate(POOL_WINDOWS):
        for tok in range(SEQ):
            lo = max(0, tok - win + 1)
            full[g, lo:tok + 1, tok] = 1.0 / min(tok + 1, win)
            full[g, tok, tok] -= 1.0
    a, b = NG * P, NG * P + NG * EDGE
    bands[:, :a] = full[:, :P, :P].transpose(1, 0, 2).reshape(P, -1)
    bands[:, a:b] = full[:, :P, P:P + EDGE].transpose(1, 0, 2).reshape(P, -1)
    bands[:, b:] = full[:, P:, P:].transpose(1, 0, 2).reshape(P, -1)
    return c, bands


def weight_blocks(w):
    out = []

    def view(k, c):
        return lambda slot: slot[:, 0:k * c].rearrange("p (k c) -> p k c", k=k)

    def rows(src):
        return src.rearrange("(k p) n -> p k n", p=P)

    def halves(name, src, k, c):
        v = view(k, c)
        h = (k + 1) // 2
        out.append((name, k * c, [(v, (slice(0, h), slice(0, c)), src[:, 0:h, :]),
                                  (v, (slice(h, k), slice(0, c)), src[:, h:k, :])]))

    def cols(name, src, a, c):
        halves(name, rows(src)[:, :, a:a + c], KD, c)

    def pair(name, src, a, b):
        v = view(KD, 2 * P)
        out.append((name, KD * 2 * P, [(v, (slice(0, KD), slice(0, P)), rows(src)[:, :, a:a + P]),
                                       (v, (slice(0, KD), slice(P, 2 * P)), rows(src)[:, :, b:b + P])]))

    def rowpair(name, src, i):
        halves(name, rows(src)[:, 2 * i:2 * i + 2, :], 2, D)

    def mem(i):
        cols(f"mem{i}", w["xattn_wk_2"][0] if i < 4 else w["xattn_wv_2"][0], (i % 4) * 2 * P, 2 * P)

    def ffn(layer):
        for j in range(STEPS):
            out.append((f"ffn{layer}", KD * 2 * P, None))

    halves("pool", w["pool_w"][0].rearrange("g (c p) d -> p (g c) d", p=P), 2 * NG, 256)
    mem(0)
    ffn(0)
    mem(1)
    for b in range(3):
        cols(f"down{b}", w["mla_w_down"][0], b * MLA_DOWN // 3, MLA_DOWN // 3)
    mem(2)
    hw = NOPE + ROPE
    for b, n in enumerate((3, 3, 2)):
        halves(f"uq{b}", rows(w["mla_w_uq"][0])[:, :, 3 * b * hw:(3 * b + n) * hw], 3, n * hw)
    halves("ukv", w["mla_w_ukv"][0].rearrange("p (k c) -> p k c", k=2), 2, D)
    for i in range(4):
        rowpair(f"wo{i}", w["mla_w_o"][0], i)
    mem(3)
    ffn(1)
    mem(4)
    mem(5)
    win = w["w_in_2"][0]
    z = NSA_HEADS * DH
    zg = z + 6 * P + 24
    zc = zg + 2 * GW
    cols("z_a", win, zc, CW_)
    cols("z_gt", win, zc + CW_, CW_)
    cols("z_kcvc", win, z, 2 * P)
    pair("z_q0", win, 0, REP * DH)
    pair("z_q1", win, P, REP * DH + P)
    pair("z_ksw", win, z + 2 * P, z + 4 * P)
    pair("z_vsw", win, z + 3 * P, z + 5 * P)
    cols("z_gl", win, z + 6 * P, 24)
    cols("z_v", win, zg + GW, GW)
    cols("z_u", win, zg, GW)
    for i in WOUT_ORDER:
        rowpair(f"wout{i}", w["w_out_2"][0], i)
    mem(6)
    mem(7)
    for i in range(4):
        cols(f"xq{i}", w["xattn_wq_2"][0], i * XHD, XHD)
    for i in range(4):
        rowpair(f"xo{i}", w["xattn_wo_2"][0], i)
    ffn(2)
    return out


def build(nc, w, consts, bands, out):
    blocks = weight_blocks(w)
    names = [b[0] for b in blocks]
    at = {name: names.index(name) for name in names}
    used_cols = [b[1] for b in blocks]
    NB = len(blocks)
    x_dram = w["x"].rearrange("b (t p) d -> p (b t) d", p=P)
    mem_dram = w["mem_2"].rearrange("b (t p) d -> p (b t) d", p=P)
    out_dram = out.rearrange("b (t p) d -> p (b t) d", p=P)

    def gate_up(layer):
        if layer < 2:
            return (w["ffn_w_gate"][layer], w["ffn_w_up"][layer])
        return (w["ffn_w_up_2"][0][:, 0:FF], w["ffn_w_up_2"][0][:, FF:2 * FF])

    def down_rows(layer):
        return w["ffn_w_down"][layer] if layer < 2 else w["ffn_w_down_2"][0]

    with ExitStack() as ctx:
        def sb(name, shape, dt=F32):
            return ctx.enter_context(nc.sbuf_tensor(name, shape, dt))

        def sem(name):
            return ctx.enter_context(nc.semaphore(name))

        raw = [sb(f"raw{s}", [P, 2048]) for s in range(3)]
        wh = [sb(f"wh{s}", [P, 2048], F32R) for s in range(3)]
        wl = [sb(f"wl{s}", [P, 2048], F32R) for s in range(3)]
        xt = sb("x_tok", [P, NT, D])
        xh = sb("xh", [P, KD, SEQ], F32R)
        xl = sb("xl", [P, KD, SEQ], F32R)
        mh = sb("mh", [P, KD, SEQ], F32R)
        ml = sb("ml", [P, KD, SEQ], F32R)
        km = sb("k_mem", [P, KD, SEQ])
        vm = sb("v_mem", [P, NT, D])
        hh = [sb(f"hh{s}", [P, SEQ], F32R) for s in range(3)]
        hl = [sb(f"hl{s}", [P, SEQ], F32R) for s in range(3)]
        zero = sb("zero", [P, P], F32R)
        con = sb("con", [P, NCONST])
        col = sb("col", [P, NCOLS])
        gain = sb("gain", [P, D])
        diag = sb("diag", [P, NT, P])
        junk = sb("junk", [P, HALF])
        ss = sb("ss", [P, 16, NT, 2])
        st1 = sb("st1", [P, 16, NT])
        st2 = sb("st2", [P, 16, NT])
        rstd = sb("rstd", [P, 16, NT])
        mhalf = sb("mhalf", [P, 16])
        cs = sb("cs", [P, NT, ROPE])
        sn = sb("sn", [P, NT, ROPE])
        base = nc.sbuf_base
        REGION = 61312
        ctx.enter_context(nc.sbuf_tensor("region", [P, REGION // 4], F32))
        base = (base + 31) // 32 * 32
        cursor = [0]

        def at_(name, shape, dt=F32, off=None):
            if off is not None:
                cursor[0] = off
            n = 4
            for d in shape[1:]:
                n *= d
            t = nc.alloc_sbuf_tensor_at(name, shape, dt, offset=base + cursor[0])
            cursor[0] += (n + 31) // 32 * 32
            assert cursor[0] <= REGION - 32, (name, cursor[0])
            return t

        memt = at_("mem_tok", [P, NT, D], off=0)
        band = at_("band", [P, NPOOL])
        bandr = at_("bandr", [P, NPOOL])
        pscale = at_("pscale", [P, D])
        prow = [at_(f"prow{i}", [P, P]) for i in range(4)]
        posi = at_("posi", [P, NT], I32)
        posf = at_("posf", [P, NT])
        ang = at_("ang", [P, NT, ROPE // 2])
        kk = at_("kk", [P, NT, ROPE // 2])
        r0 = at_("r0", [P, NT, ROPE // 2])
        r1 = at_("r1", [P, NT, ROPE // 2])
        draw = [at_(f"draw{s}", [P, D], off=(0 if s == 0 else None)) for s in range(3)]
        dh = [at_(f"dh{s}", [P, D], F32R) for s in range(3)]
        dl = [at_(f"dl{s}", [P, D], F32R) for s in range(3)]
        th = [at_(f"th{s}", [P, SEQ]) for s in range(3)]
        pr = [at_(f"pr{s}", [P, SEQ]) for s in range(3)]
        ga = at_("ga", [P, SEQ])
        cg = [at_(f"cg{s}", [P, SEQ]) for s in range(3)]
        cu = [at_(f"cu{s}", [P, SEQ]) for s in range(3)]
        ds = at_("ds", [P, NT, MLA_DOWN], off=0)
        dqk = at_("dqk", [P, 2, NT, P])
        qn = at_("qn", [P, HEADS, SEQ])
        qr = at_("qr", [P, NT, HEADS * ROPE])
        qrt = at_("qrt", [P, HEADS // 2, SEQ])
        kn = at_("kn", [P, HEADS, SEQ])
        vv = at_("vv", [P, NT, HEADS * P])
        kr = at_("kr", [P, NT, P])
        krt = at_("krt", [P, SEQ])
        ra = at_("ra", [P, HEADS * ROPE])
        rb = at_("rb", [P, HEADS * ROPE])
        sc = [at_(f"sc{s}", [P, 3 * P]) for s in range(2)]
        pt = [at_(f"pt{s}", [P, 3 * P]) for s in range(2)]
        stat = at_("stat", [P, HEADS, 4, NT])
        mst = at_("mst", [P, 4, 2, NT])
        qt = at_("qt", [P, REP, SEQ], off=0)
        ksw = at_("ksw", [P, 2, SEQ])
        kvc = at_("kvc", [P, 2, SEQ])
        vsw = at_("vsw", [P, NT, 2 * P])
        x4 = at_("x4", [P, 2, GROUPS, SEQ])
        fl = at_("fl", [P, 2, CMP_KT, GROUPS, NCMP])
        yn = at_("yn", [P, NT, D])
        cw1 = at_("cw1", [P, 2, CMP_KT, DH])
        cw2 = at_("cw2", [DH, 2, DH])
        hg = at_("hg", [DH, 4, 2 * GROUPS * NCMP])
        kcm = at_("kcm", [P, NCMP])
        vcs = at_("vcs", [NCMP, GROUPS, DH])
        vbd = at_("vbd", [P, NSA_HEADS * DH])
        hc = at_("hc", [P, 2, PAD + SEQ])
        yc = at_("yc", [P, 2, SEQ])
        gate = at_("gate", [P, NT, 24])
        e1 = at_("e1", [P, HALF])
        e2 = at_("e2", [P, HALF])
        e3 = at_("e3", [P, HALF])
        wst = at_("wst", [P, GG, P])
        bsr = at_("bsr", [GG, P])
        lng = at_("lng", [P, 2, 2, GW])
        s2 = [kvc[:, :, :].rearrange("p a s -> p (a s)")[:, 0:3 * P],
              fl[:, :, :, :, :].rearrange("p a k g n -> p (a k g n)")[:, GG * P:GG * P + 3 * P]]
        p2 = [at_(f"p2_{s}", [P, 3 * P]) for s in range(2)]
        nst = at_("nst", [P, 4, 2 * NSA_HEADS, NT])
        lst = at_("lst", [P, 64])
        uu = x4[:, :, :, :].rearrange("p a g s -> p (a g s)")[:, 0:HALF]
        vg = x4[:, :, :, :].rearrange("p a g s -> p (a g s)")[:, HALF:2 * HALF]
        ws = fl[:, :, :, :, :].rearrange("p a k g n -> p (a k g n)")[:, 0:GG * P]
        cm = [cw1[:, 0, :, :].rearrange("p k d -> p (k d)")[:, 240 * i:240 * i + 240] for i in range(4)]
        dseg = cw1[:, 1, :, :].rearrange("p k d -> p (k d)")[:, 0:768].rearrange("p (a b) -> p a b", a=6)
        qx = at_("qx", [P, KD, SEQ], off=0)
        sx = [at_(f"sx{s}", [P, NT, SEQ]) for s in range(2)]
        px = [at_(f"px{s}", [P, NT, SEQ]) for s in range(2)]
        xst = at_("xst", [P, XHEADS, 4, NT])

        bank = [ctx.enter_context(nc.psum_tensor(f"bank{i}", [P, HALF], F32)) for i in range(8)]

        raw_full = [sem(f"raw_full{s}") for s in range(3)]
        hi_done, lo_done, block_used = sem("hi_done"), sem("lo_done"), sem("block_used")
        d_full = [sem(f"d_full{s}") for s in range(3)]
        d_hi, d_lo, down_done = sem("d_hi"), sem("d_lo"), sem("down_done")
        tanh_done, gated, prod_done = sem("tanh_done"), sem("gated"), sem("prod_done")
        h_hi, h_ready = sem("h_hi"), sem("h_ready")
        conv_in, conv_tap, conv_silu = sem("conv_in"), sem("conv_tap"), sem("conv_silu")
        x_loaded, con_loaded, band_loaded = sem("x_loaded"), sem("con_loaded"), sem("band_loaded")
        mem_loaded, rows_loaded, pscale_loaded = sem("mem_loaded"), sem("rows_loaded"), sem("pscale_loaded")
        gain_loaded, pos_loaded = sem("gain_loaded"), sem("pos_loaded")
        last_gain_loaded = sem("last_gain_loaded")
        zero_set, mhalf_set = sem("zero_set"), sem("mhalf_set")
        cols_t, cols_done, taps_halved = sem("cols_t"), sem("cols_done"), sem("taps_halved")
        pool_scaled = sem("pool_scaled")
        sq_done, rstd_done = sem("sq_done"), sem("rstd_done")
        res_done, diag_done = sem("res_done"), sem("diag_done")
        t_done, t_hi, t_lo = sem("t_done"), sem("t_hi"), sem("t_lo")
        bank_sum = sem("bank_sum")
        gained = sem("gained")
        mem_out = sem("mem_out")
        region_free = sem("region_free")
        scaled = sem("scaled")
        rope_a, rope_s = sem("rope_a"), sem("rope_s")
        ds_out, mla_sq, mla_rs, mla_dg = sem("ds_out"), sem("mla_sq"), sem("mla_rs"), sem("mla_dg")
        cq_t, cq_hi, cq_lo = sem("cq_t"), sem("cq_hi"), sem("cq_lo")
        kr_done, kr_t, kr_out = sem("kr_done"), sem("kr_t"), sem("kr_out")
        qk_mm, qk_out = sem("qk_mm"), sem("qk_out")
        v_mm, v_out = sem("v_mm"), sem("v_out")
        qr_done, qr_t, qr_out = sem("qr_done"), sem("qr_t"), sem("qr_out")
        s_mm, s_max, s_exp, s_norm = sem("s_mm"), sem("s_max"), sem("s_exp"), sem("s_norm")
        p_t, p_out, o_mm, o_hi, o_lo = sem("p_t"), sem("p_out"), sem("o_mm"), sem("o_hi"), sem("o_lo")
        z_out = sem("z_out")
        z_params = sem("z_params")
        z_ws, ws_loaded, ws_cut = sem("z_ws"), sem("ws_loaded"), sem("ws_cut")
        hc_done, cv_tap = sem("hc_done"), sem("cv_tap")
        shifted, fl_done, cmp_mm, cmp_a, cmp_d, cmp_out = (sem("shifted"), sem("fl_done"), sem("cmp_mm"),
                                                         sem("cmp_a"), sem("cmp_d"), sem("cmp_out"))
        vbd_zero, vbd_set = sem("vbd_zero"), sem("vbd_set")
        gl_a, gl_done = sem("gl_a"), sem("gl_done")
        gz_a, gz_d = sem("gz_a"), sem("gz_d")
        ws_t, ws_out, ln_rs, vn_done, mix_mm, gy_done = (sem("ws_t"), sem("ws_out"), sem("ln_rs"),
                                                        sem("vn_done"), sem("mix_mm"), sem("gy_done"))
        ycs_t, cvln_done, cv_a, cy_done = sem("ycs_t"), sem("cvln_done"), sem("cv_a"), sem("cy_done")
        sc_mm, cm_e, pc_done, pc_t, pc_out = (sem("sc_mm"), sem("cm_e"), sem("pc_done"), sem("pc_t"),
                                             sem("pc_out"))
        n_mm, n_max, n_exp, n_norm, n_t, n_out = (sem("n_mm"), sem("n_max"), sem("n_exp"), sem("n_norm"),
                                                  sem("n_t"), sem("n_out"))
        o_all, yn_done, y_sq, y_rs, y_dg = sem("o_all"), sem("yn_done"), sem("y_sq"), sem("y_rs"), sem("y_dg")
        q_out = sem("q_out")
        a_mm, a_max, a_exp, a_norm, a_t, a_out, ao_mm, ao_hi, ao_lo = (
            sem("a_mm"), sem("a_max"), sem("a_exp"), sem("a_norm"), sem("a_t"), sem("a_out"),
            sem("ao_mm"), sem("ao_hi"), sem("ao_lo"))
        dve_order, act_order, pool_order = sem("dve_order"), sem("act_order"), sem("pool_order")
        stored = sem("stored")

        ident = con[:, K_ID:K_ID + P]
        mask = con[:, K_MASK:K_MASK + 3 * P]

        def split_views(n, *slots):
            if names[n] not in ("z_q0", "z_q1"):
                return [[t[:, 0:used_cols[n]] for t in slots]]
            by_head = [t[:, :].rearrange("p (k j g d) -> p k j g d", k=KD, j=2, g=GROUPS) for t in slots[1:]]
            by_group = slots[0][:, :].rearrange("p (k g j d) -> p k g j d", k=KD, j=2, g=GROUPS)
            return [[by_group[:, :, g, :, :]] + [v[:, :, :, g, :] for v in by_head] for g in range(GROUPS)]

        def k_view(t, k, c):
            return t[:, 0:k * c].rearrange("p (k c) -> p k c", k=k)

        block = ctx.enter_context(nc.Block())

        @block.sync
        def _(sp):
            def load(n):
                _, _, parts = blocks[n]
                if n >= 3:
                    sp.wait_ge(hi_done, n - 2)
                    sp.wait_ge(lo_done, n - 2)
                for v, (ks, cs_), src in parts:
                    sp.dma_start(v(raw[n % 3])[:, ks, cs_], src).then_inc(raw_full[n % 3], 32 // len(parts))

            def ffn(layer):
                n0, m0 = at[f"ffn{layer}"], STEPS * layer
                gu = gate_up(layer)
                dn = down_rows(layer)

                def load_gu(s, j, n):
                    slot = raw[s][:, :].rearrange("p (k h c) -> p k h c", k=KD, h=2)
                    sp.wait_ge(hi_done, n - 2)
                    sp.wait_ge(lo_done, n - 2)
                    for half in range(2):
                        src = gu[half].rearrange("(k p) n -> p k n", p=P)[:, :, bass.ds(j * P, P)]
                        sp.dma_start(slot[:, :, half, :], src).then_inc(raw_full[s], 16)

                def load_d(s, j, m):
                    if not isinstance(m, int) or m >= 3:
                        sp.wait_ge(d_lo, m - 2)
                    sp.dma_start(draw[s][:, :], dn[bass.ds(j * P, P), :]).then_inc(d_full[s], 16)

                for j in range(3):
                    load_gu((n0 + j) % 3, j, n0 + j)
                sp.wait_ge(region_free, layer + 1)
                for j in range(3):
                    load_d((m0 + j) % 3, j, m0 + j)
                with sp.Fori(0, LOOPED // 3) as i:
                    for s in range(3, 6):
                        load_gu((n0 + s) % 3, 3 * i + s, 3 * i + n0 + s)
                        load_d((m0 + s) % 3, 3 * i + s, 3 * i + m0 + s)
                for j in range(LOOPED + 3, STEPS):
                    load_gu((n0 + j) % 3, j, n0 + j)
                    load_d((m0 + j) % 3, j, m0 + j)

            n = 0
            while n < NB:
                if names[n].startswith("ffn"):
                    ffn(int(names[n][3:]))
                    n += STEPS
                else:
                    load(n)
                    n += 1
            for t in range(NT):
                sp.wait_ge(scaled, NT + 2 * t + 2)
                sp.dma_start(out_dram[:, t, :], xt[:, t, :]).then_inc(stored, 16)
            sp.wait_ge(stored, 16 * NT)

        @block.scalar
        def _(act):
            junk_writer = [None]

            def junk_for(signal, count, width):
                if junk_writer[0] is not None:
                    act.wait_ge(*junk_writer[0])
                junk_writer[0] = (signal, count)
                return junk[:, 0:width]

            def hi(n):
                if n >= NB:
                    return
                act.wait_ge(raw_full[n % 3], 32 * (n // 3 + 1))
                if n >= 3:
                    act.wait_ge(block_used, n - 2)
                if n == 0:
                    act.wait_ge(pool_scaled, 3)
                for r, h in split_views(n, raw[n % 3], wh[n % 3]):
                    ins = act.activation(h, r, ACT.Copy)
                ins.then_inc(hi_done, 1)

            def squares(q, src, ready, first):
                for t in range(NT):
                    for c in range(2):
                        if ready is not None:
                            act.wait_ge(ready, first + 2 * t + c)
                        act.activation(junk_for(sq_done, 4 * q + 2 * t + c + 1, HALF),
                                       src[:, t, c * HALF:(c + 1) * HALF], ACT.Square, scale=ROOT_D,
                                       accum_out=ss[:, q, t, c:c + 1]).then_inc(sq_done, 1)

            def split_t(e, dst, c0, banks, ks=range(KD), done=0):
                for i, k in enumerate(ks):
                    if k % 2 == 0:
                        act.wait_ge(t_done, (KD * e + done + i) // 2 + 1)
                    src = bank[banks + k // 2][:, (k % 2) * SEQ:(k % 2 + 1) * SEQ]
                    act.activation(dst[:, k, :], src, ACT.Copy, scale=col[:, c0 + k:c0 + k + 1]) \
                       .then_inc(t_hi, 1)

            def mem_block(i):
                n = at[f"mem{i}"]
                act.wait_ge(block_used, n + 1)
                src = bank[7][:, :].rearrange("p (a s) -> p a s", a=2)
                if i < 4:
                    dst = km[:, 2 * i:2 * i + 2, :]
                else:
                    dst = vm[:, :, (i - 4) * 256:(i - 3) * 256]
                act.activation(dst, src, ACT.Copy).then_inc(mem_out, 1)

            def after(name):
                hi(at[name] + 3)

            def ffn(layer):
                n0, m0 = at[f"ffn{layer}"], STEPS * layer

                def dhi(s, m, q):
                    act.wait_ge(d_full[s], q)
                    act.wait_ge(down_done, m + 1)
                    act.activation(dh[s][:, :], draw[s][:, :], ACT.Copy).then_inc(d_hi, 1)

                def step(j, i, jj):
                    s = (m0 + jj) % 3
                    n, m = n0 + j, m0 + j
                    act.wait_ge(block_used, n + 1)
                    b = bank[4 + s]
                    if layer < 2:
                        act.activation(th[s][:, :], b[:, 0:SEQ], ACT.Tanh, scale=0.5).then_inc(tanh_done, 1)
                    else:
                        for half, dst in ((0, cg[s]), (1, cu[s])):
                            c2 = C_DW + 2 * NF2 + half * STEPS
                            cb = C_DW + 3 * NF2 + half * STEPS
                            act.activation(dst[:, :], b[:, half * SEQ:(half + 1) * SEQ], ACT.Identity,
                                           scale=col[:, bass.ds(j + c2, 1)],
                                           bias=col[:, bass.ds(j + cb, 1)]).then_inc(conv_in, 1)
                    if i is not None or jj + 3 < STEPS:
                        ns = (n0 + jj) % 3
                        act.wait_ge(raw_full[ns], 32 * ((n0 + jj) // 3 + 2) + (0 if i is None else 32 * i))
                        act.activation(wh[ns][:, :], raw[ns][:, :], ACT.Copy).then_inc(hi_done, 1)
                    else:
                        hi(n0 + jj + 3)
                    if layer == 2:
                        act.wait_ge(conv_tap, 4 * (j + 1) - 2)
                        act.activation(th[s][:, :], cg[s][:, :], ACT.Tanh, scale=0.5).then_inc(tanh_done, 1)
                    act.wait_ge(prod_done, m + 4)
                    act.wait_ge(down_done, m + 1)
                    act.activation(hh[s][:, :], pr[s][:, :], ACT.Copy).then_inc(h_hi, 1)
                    if i is not None or jj + 2 < STEPS:
                        s2_ = (m0 + jj + 2) % 3
                        q = 16 * ((m0 + jj + 2) // 3 + 1) + (0 if i is None else 16 * i)
                        dhi(s2_, m + 2, q)

                for j in range(2):
                    dhi((m0 + j) % 3, m0 + j, 16 * ((m0 + j) // 3 + 1))
                step(0, None, 0)
                with act.Fori(0, LOOPED // 3) as i:
                    for s in range(1, 4):
                        step(3 * i + s, i, s)
                for j in range(LOOPED + 1, STEPS):
                    step(j, None, j)

            def norm(q, e, c0, first, filler):
                squares(q, xt, res_done, first)
                if filler is not None:
                    mem_block(filler)
                split_t(e, xh, c0, 0)
                if filler is not None:
                    after(f"mem{filler}")

            for t in range(NT):
                act.dma_start(xt[:, t, :], x_dram[:, t, :]).then_inc(x_loaded, 16)
            act.dma_start(con[:, :], consts).then_inc(con_loaded, 16)
            act.dma_start(band[:, :], bands).then_inc(band_loaded, 16)
            act.dma_start(pscale[:, :], w["pool_scale"][0:1, :].to_broadcast([P, D])).then_inc(pscale_loaded, 16)
            rows = [(0, 0, w["norm_mix"].rearrange("l (k p) -> (l k) p", p=P)),
                    (0, C_FFN, w["norm_ffn"].rearrange("l (k p) -> (l k) p", p=P)),
                    (0, C_QN, w["mla_q_norm"].rearrange("l (k p) -> (l k) p", p=P)),
                    (0, C_KVN, w["mla_kv_norm"].rearrange("l (k p) -> (l k) p", p=P)),
                    (0, C_MIXN, w["mix_norm_g_2"].rearrange("l (k p) -> (l k) p", p=P)),
                    (0, C_MOUT, w["mix_out_g_2"].rearrange("l (k p) -> (l k) p", p=P)),
                    (0, C_XN, w["xattn_norm_g_2"].rearrange("l (k p) -> (l k) p", p=P)),
                    (0, C_MEMN, w["mem_norm_g_2"].rearrange("l (k p) -> (l k) p", p=P)),
                    (0, C_FN2, w["ffn_norm_g_2"].rearrange("l (k p) -> (l k) p", p=P)),
                    (0, C_CDB, w["conv_dw_b_2"].rearrange("l (k p) -> (l k) p", p=P)),
                    (1, 0, w["conv_dw_w_2"][0].rearrange("t (a p) -> (t a) p", p=P)),
                    (1, 2 * TAPS, w["cmp_pe_2"][0].rearrange("a (k e) d -> (a k) (e d)", e=2)),
                    (2, 0, w["ffn_dw_w_2"][0, 0:2, :].rearrange("t (j p) -> (t j) p", p=P)),
                    (3, 0, w["ffn_dw_w_2"][0, 2:3, :].rearrange("t (j p) -> (t j) p", p=P)),
                    (3, NF2, w["ffn_dw_b_2"].rearrange("t (j p) -> (t j) p", p=P))]
            for i, r, src in rows:
                act.dma_start(prow[i][r:r + src.shape[0], :], src).then_inc(rows_loaded, 16)
            act.dma_start(memt[:, :, :], mem_dram).then_inc(mem_loaded, 16)
            act.dma_start(gain[:, :], w["norm_final"].rearrange("(a d) -> a d", a=1).to_broadcast([P, D])) \
               .then_inc(gain_loaded, 16)
            act.dma_start(posi[:, :], w["positions"].rearrange("a (t p) -> p (a t)", p=P),
                          allow_slow_non_contiguous=True).then_inc(pos_loaded, 16)
            act.wait_ge(rope_a, 1)
            act.activation(sn[:, :, 32:64], r0[:, :, :], ACT.Sin).then_inc(rope_s, 1)
            act.activation(cs[:, :, 0:32], r1[:, :, :], ACT.Sin).then_inc(rope_s, 1)
            act.wait_ge(x_loaded, 16 * NT)
            squares(0, xt, None, 0)
            act.wait_ge(cols_t, 1)
            act.activation(col[:, :], bank[7][:, 0:NCOLS], ACT.Copy).then_inc(cols_done, 1)
            act.wait_ge(cols_done, 1)
            hi(0)
            split_t(0, xh, C_MIX0, 0)
            act.wait_ge(mem_loaded, 16)
            squares(1, memt, None, 0)
            hi(1)
            hi(2)
            split_t(1, mh, C_MEMN, 4)
            squares(2, xt, res_done, 1)
            hi(3)
            mem_block(0)
            split_t(2, xh, C_FFN, 0)
            after("mem0")
            ffn(0)
            norm(3, 3, C_MIX1, 5, 1)
            after("down0")
            act.wait_ge(block_used, at["down1"] + 1)
            for t in range(NT):
                act.activation(ds[:, t, 0:QLR], bank[t][:, 0:QLR], ACT.Copy).then_inc(ds_out, 1)
            act.wait_ge(ds_out, 2)
            for t in range(NT):
                act.activation(junk_for(mla_sq, t + 1, QLR), ds[:, t, 0:QLR], ACT.Square,
                               accum_out=mst[:, 0, 0, t:t + 1]).then_inc(mla_sq, 1)
            after("down1")
            act.wait_ge(block_used, at["down2"] + 1)
            for t in range(NT):
                act.activation(ds[:, t, QLR:MLA_DOWN], bank[2 + t][:, 0:KVR + ROPE], ACT.Copy).then_inc(ds_out, 1)
            act.wait_ge(ds_out, 4)
            for t in range(NT):
                act.activation(junk_for(mla_sq, t + 3, KVR), ds[:, t, QLR:QLR + KVR], ACT.Square,
                               accum_out=mst[:, 0, 1, t:t + 1]).then_inc(mla_sq, 1)
            after("down2")
            mem_block(2)
            after("mem2")
            for f in range(4):
                act.wait_ge(cq_t, f // 2 + 1)
                act.activation(xh[:, f, :], bank[4 + f // 2][:, (f % 2) * SEQ:(f % 2 + 1) * SEQ], ACT.Copy,
                               scale=col[:, C_QN + f:C_QN + f + 1]).then_inc(cq_hi, 1)
            act.wait_ge(kr_t, 1)
            act.activation(krt[:, :], bank[6][:, 0:SEQ], ACT.Copy).then_inc(kr_out, 1)
            def heads_out(dst, i, first):
                act.wait_ge(qk_mm, first + i + 1)
                act.activation(dst[:, 2 * i:2 * i + 2, :].rearrange("p a s -> p (a s)"), bank[4 + i % 2][:, :],
                               ACT.Copy).then_inc(qk_out, 1)

            heads_out(qn, 0, 0)
            after("uq0")
            heads_out(qn, 1, 0)
            heads_out(qn, 2, 0)
            after("uq1")
            heads_out(qn, 3, 0)
            after("uq2")
            for i in range(4):
                heads_out(kn, i, 4)
            for i in range(4):
                if i < 3:
                    act.wait_ge(v_mm, i + 1)
                else:
                    act.wait_ge(block_used, at["ukv"] + 1)
                t, hv = i // 2, i % 2
                act.activation(vv[:, t, hv * HALF:(hv + 1) * HALF], bank[(2, 3, 6, 2)[i]][:, :], ACT.Copy) \
                   .then_inc(v_out, 1)
            after("ukv")
            for i in range(2):
                act.wait_ge(qr_t, i + 1)
                act.activation(qrt[:, 2 * i:2 * i + 2, :].rearrange("p a s -> p (a s)"), bank[i][:, :], ACT.Copy) \
                   .then_inc(qr_out, 1)

            def mla_exp(h):
                act.wait_ge(s_max, h + 1)
                for t, (a, b) in enumerate(((0, P), (P, 3 * P))):
                    act.activation(sc[h % 2][:, a:b], sc[h % 2][:, a:b], ACT.Exp,
                                   bias=stat[:, h, 1, t:t + 1], accum_out=stat[:, h, 2, t:t + 1]) \
                       .then_inc(s_exp, 1)

            def mla_pt(h):
                act.wait_ge(p_t, h + 1)
                if h >= 2:
                    act.wait_ge(o_mm, h - 1)
                act.activation(pt[h % 2][:, :], bank[6][:, 0:3 * P], ACT.Copy).then_inc(p_out, 1)

            def mla_o(h):
                act.wait_ge(o_mm, h + 1)
                act.activation(xh[:, h, :], bank[7][:, (h % 2) * SEQ:(h % 2 + 1) * SEQ], ACT.Copy).then_inc(o_hi, 1)

            mla_exp(0)
            for h in range(1, HEADS + 1):
                if h < HEADS:
                    mla_exp(h)
                mla_pt(h - 1)
                mla_o(h - 1)
                if h in (4, 6):
                    after(f"wo{h // 2 - 2}")
            after("wo2")
            after("wo3")
            norm(4, 4, C_FFN + 8, 9, 3)
            ffn(1)
            squares(5, xt, res_done, 13)
            squares(6, xt, gained, 1)
            mem_block(4)
            after("mem4")
            split_t(5, xh, C_MIXN, 0)
            mem_block(5)
            after("mem5")
            act.wait_ge(block_used, at["z_gt"] + 1)
            act.activation(e1[:, :], bank[1][:, :], ACT.Tanh, scale=0.5).then_inc(z_out, 1)
            hi(at["z_a"] + 3)
            after("z_gt")
            act.wait_ge(block_used, at["z_kcvc"] + 1)
            act.activation(kvc[:, :, :].rearrange("p a s -> p (a s)"), bank[2][:, :], ACT.Copy).then_inc(z_out, 1)
            act.wait_ge(z_out, 2)
            for g in range(GROUPS):
                act.dma_start(x4[0:DH, :, g, :], kvc[g * DH:(g + 1) * DH, :, :]).then_inc(shifted, 16)
                act.dma_start(x4[DH:P, :, g, 0:SEQ - 1], kvc[g * DH:(g + 1) * DH, :, 1:SEQ]).then_inc(shifted, 16)
            after("z_kcvc")
            for i in range(2):
                act.wait_ge(block_used, at[f"z_q{i}"] + 1)
                act.activation(qt[:, 2 * i:2 * i + 2, :].rearrange("p a s -> p (a s)"), bank[3 if i == 0 else 0][:, :],
                               ACT.Copy).then_inc(z_out, 1)
                after(f"z_q{i}")
            act.wait_ge(cmp_mm, 1)
            hs = bank[7][0:DH, 0:60]
            act.activation(hg[:, 0, :], hs, ACT.Square).then_inc(cmp_a, 1)
            act.wait_ge(cmp_d, 2)
            act.activation(hg[:, 1, :], hg[:, 2, :], ACT.Tanh, scale=GELU_S).then_inc(cmp_a, 1)
            act.wait_ge(block_used, at["z_ksw"] + 1)
            act.activation(ksw[:, :, :].rearrange("p a s -> p (a s)"), bank[1][:, :], ACT.Copy).then_inc(z_out, 1)
            after("z_ksw")
            act.wait_ge(cmp_mm, 2)
            act.activation(kcm[:, :], bank[7][:, 64:64 + NCMP], ACT.Copy, scale=0.5).then_inc(cmp_out, 1)
            act.activation(vcs[:, :, :], bank[7][0:NCMP, 128:256].rearrange("n (g d) -> n g d", g=GROUPS), ACT.Copy,
                           scale=0.5).then_inc(cmp_out, 1)
            act.wait_ge(cmp_out, 2)
            act.wait_ge(vbd_zero, 1)
            for h in range(NSA_HEADS):
                act.dma_start(vbd[h * NCMP:(h + 1) * NCMP, h * DH:(h + 1) * DH], vcs[:, h // REP, :]) \
                   .then_inc(vbd_set, 16)
            act.wait_ge(block_used, at["z_vsw"] + 1)
            act.activation(vsw[:, :, :].rearrange("p a s -> p (a s)"), bank[2][:, :], ACT.Copy).then_inc(z_out, 1)
            after("z_vsw")
            act.wait_ge(block_used, at["z_gl"] + 1)
            act.activation(gate[:, :, :].rearrange("p t c -> p (t c)"), bank[3][:, 0:NT * 24], ACT.Tanh, scale=0.5) \
               .then_inc(gl_a, 1)
            after("z_gl")
            for i, name in enumerate(("z_v", "z_u")):
                act.wait_ge(block_used, at[name] + 1)
                b = bank[(0, 1)[i]]
                if i == 1:
                    act.wait_ge(gz_d, 3)
                act.activation(e1[:, :], b[:, :], ACT.Square).then_inc(gz_a, 1)
                act.wait_ge(gz_d, 3 * i + 2)
                act.activation(e1[:, :], e2[:, :], ACT.Tanh, scale=GELU_S).then_inc(gz_a, 1)
                after(name)
            act.wait_ge(ws_t, 1)
            act.activation(wst[:, :, :].rearrange("p g t -> p (g t)"), bank[6][:, :], ACT.Copy).then_inc(ws_out, 1)
            act.wait_ge(cm_e, 1)
            act.activation(cm[1], cm[0], ACT.Exp, scale=NSA_SCALE).then_inc(cm_e, 1)
            act.wait_ge(pc_t, NT)
            act.activation(e1[0:120, 0:SEQ], bank[6][0:120, 0:SEQ], ACT.Copy).then_inc(pc_out, 1)

            def nsa_exp(u):
                act.wait_ge(n_max, u + 1)
                for t, (a, b) in enumerate(((0, P), (P, 3 * P))):
                    act.activation(s2[u % 2][:, a:b], s2[u % 2][:, a:b], ACT.Exp,
                                   bias=nst[:, 1, u, t:t + 1], accum_out=nst[:, 2, u, t:t + 1]) \
                       .then_inc(n_exp, 1)

            def nsa_pt(u):
                act.wait_ge(n_t, u + 1)
                if u >= 2:
                    act.wait_ge(o_all, u - 1)
                act.activation(p2[u % 2][:, :], bank[6][:, 0:3 * P], ACT.Copy).then_inc(n_out, 1)

            nsa_exp(0)
            for u in range(1, 2 * NSA_HEADS + 1):
                if u < 2 * NSA_HEADS:
                    nsa_exp(u)
                nsa_pt(u - 1)
                if u == U_SILU:
                    act.wait_ge(cvln_done, 1)
                    act.activation(e1[:, :], e2[:, :], ACT.Tanh, scale=0.5).then_inc(cv_a, 1)
                if u == U_SQUARES:
                    act.wait_ge(gy_done, 2)
                    act.wait_ge(cy_done, 1)
                    for s, (a, b) in ((1, (512, 768)), (2, (768, 1024))):
                        for t in range(NT):
                            act.activation(junk_for(y_sq, 2 * s + t - 1, b - a), yn[:, t, a:b], ACT.Square,
                                           accum_out=lst[:, 32 + 2 * s + t:33 + 2 * s + t]).then_inc(y_sq, 1)
                if u == U_SPLIT:
                    split_t(6, xh, C_MOUT, 0, range(4, KD))
            act.wait_ge(o_all, 2 * NSA_HEADS)
            for t in range(NT):
                if t == 1:
                    act.wait_ge(yn_done, 1)
                act.activation(junk_for(y_sq, 5 + t, HALF), bank[t][:, :], ACT.Square,
                               accum_out=lst[:, 32 + t:33 + t]).then_inc(y_sq, 1)
            split_t(6, xh, C_MOUT, 4, range(4), 4)
            for i in WOUT_ORDER[:3]:
                after(f"wout{i}")
            squares(7, xt, res_done, 17)
            after(f"wout{WOUT_ORDER[3]}")
            mem_block(6)
            split_t(7, xh, C_XN, 0)
            after("mem6")
            mem_block(7)
            after("mem7")
            def x_q(h):
                act.wait_ge(block_used, at[f"xq{h}"] + 1)
                act.activation(qx[:, 2 * h:2 * h + 2, :].rearrange("p a s -> p (a s)"), bank[h % 2][:, :], ACT.Copy) \
                   .then_inc(q_out, 1)
                if h < 2:
                    after(f"xq{h}")

            def x_exp(h):
                act.wait_ge(a_max, h + 1)
                for t in range(NT):
                    act.activation(sx[h % 2][:, t, :], bank[4 + h % 2][:, t * SEQ:(t + 1) * SEQ], ACT.Exp, scale=XSCALE,
                                   bias=xst[:, h, 1, t:t + 1], accum_out=xst[:, h, 2, t:t + 1]) \
                       .then_inc(a_exp, 1)

            def x_pt(h):
                act.wait_ge(a_t, h + 1)
                if h >= 2:
                    act.wait_ge(ao_mm, h - 1)
                act.activation(px[h % 2][:, :, :].rearrange("p a s -> p (a s)"), bank[6][:, :], ACT.Copy) \
                   .then_inc(a_out, 1)

            def x_o(h):
                act.wait_ge(ao_mm, h + 1)
                act.activation(mh[:, 2 * h:2 * h + 2, :].rearrange("p a s -> p (a s)"), bank[7][:, :], ACT.Copy) \
                   .then_inc(ao_hi, 1)

            x_q(0)
            x_q(1)
            x_exp(0)
            for h in range(1, XHEADS + 1):
                if h + 1 < XHEADS:
                    x_q(h + 1)
                x_pt(h - 1)
                if h + 1 < XHEADS:
                    after(f"xq{h + 1}")
                if h < XHEADS:
                    x_exp(h)
                else:
                    after("xo0")
                x_o(h - 1)
            for i in range(1, 4):
                after(f"xo{i}")
            norm(8, 8, C_FN2, 21, None)
            ffn(2)
            squares(9, xt, res_done, 25)

        @block.vector
        def _(dve):
            order = [0]

            def then(ins):
                order[0] += 1
                ins.then_inc(dve_order, 1)
                dve.wait_ge(dve_order, order[0])

            def lo(n):
                if n >= NB:
                    return
                dve.wait_ge(hi_done, n + 1)
                for r, h, l in split_views(n, raw[n % 3], wh[n % 3], wl[n % 3]):
                    ins = dve.tensor_tensor(l, r, h.bitcast(F32), ALU.subtract)
                ins.then_inc(lo_done, 1)

            def split_t(e, hi_, lo_, c0, banks, ks=range(KD), done=0):
                for i, k in enumerate(ks):
                    if k % 2 == 0:
                        dve.wait_ge(t_hi, KD * e + done + i + 2)
                    src = bank[banks + k // 2][:, (k % 2) * SEQ:(k % 2 + 1) * SEQ]
                    dve.scalar_tensor_tensor(out=lo_[:, k, :], in0=src, scalar=col[:, c0 + k:c0 + k + 1],
                                             in1=hi_[:, k, :].bitcast(F32), op0=ALU.mult, op1=ALU.subtract) \
                       .then_inc(t_lo, 1)

            def diagonals(q):
                for t in range(NT):
                    dve.wait_ge(rstd_done, NT * q + t + 1)
                    dve.tensor_scalar(diag[:, t, :], ident, rstd[:, q, t:t + 1], None, ALU.mult) \
                       .then_inc(diag_done, 1)

            def residual(r, last, count):
                for t in range(NT):
                    for c in range(2):
                        part = xt[:, t, c * HALF:(c + 1) * HALF]
                        if (t, c) == (NT - 1, 1):
                            dve.wait_ge(last, count)
                        else:
                            dve.wait_ge(bank_sum, 3 * r + 2 * t + c + 1)
                        dve.tensor_tensor(part, bank[2 * t + c][:, :], part, ALU.add).then_inc(res_done, 1)

            def times_gain():
                for t in range(NT):
                    for c in range(2):
                        part = xt[:, t, c * HALF:(c + 1) * HALF]
                        dve.wait_ge(sq_done, 4 * 5 + 2 * t + c + 1)
                        dve.tensor_tensor(part, part, gain[:, c * HALF:(c + 1) * HALF], ALU.mult).then_inc(gained, 1)

            def times_rstd():
                dve.wait_ge(t_done, (KD // 2) * 6)
                for t in range(NT):
                    dve.tensor_scalar(xt[:, t, :], xt[:, t, :], rstd[:, 5, t:t + 1], None, ALU.mult) \
                       .then_inc(scaled, 1)

            def last_norm(q):
                for t in range(NT):
                    dve.wait_ge(rstd_done, NT * q + t + 1)
                    for c in range(2):
                        part = xt[:, t, c * HALF:(c + 1) * HALF]
                        dve.scalar_tensor_tensor(out=part, in0=part, scalar=rstd[:, q, t:t + 1],
                                                 in1=gain[:, c * HALF:(c + 1) * HALF],
                                                 op0=ALU.mult, op1=ALU.mult).then_inc(scaled, 1)

            def norm(q, e, c0):
                diagonals(q)
                split_t(e, xh, xl, c0, 0)

            def ffn(layer):
                n0, m0 = at[f"ffn{layer}"], STEPS * layer

                def dlo(s, m):
                    dve.wait_ge(d_hi, m + 1)
                    dve.tensor_tensor(dl[s][:, :], draw[s][:, :], dh[s][:, :].bitcast(F32), ALU.subtract) \
                       .then_inc(d_lo, 1)

                def step(j, i, jj):
                    s = (m0 + jj) % 3
                    n, m = n0 + j, m0 + j
                    g, u = bank[4 + s][:, 0:SEQ], bank[4 + s][:, SEQ:2 * SEQ]
                    if layer == 2:
                        dve.wait_ge(conv_in, 2 * j + 2)
                        for half, (src, dst) in enumerate(((g, cg[s]), (u, cu[s]))):
                            for back in (1, 2):
                                if back == 2:
                                    dve.wait_ge(conv_tap, 4 * j + 2 * half + 1)
                                c = C_DW + (2 - back) * NF2 + half * STEPS
                                dve.scalar_tensor_tensor(
                                    out=dst[:, back:SEQ], in0=src[:, 0:SEQ - back],
                                    scalar=col[:, bass.ds(j + c, 1)], in1=dst[:, back:SEQ],
                                    op0=ALU.mult, op1=ALU.add).then_inc(conv_tap, 1)
                        dve.wait_ge(conv_tap, 4 * j + 4)
                        g, u = cg[s][:, :], cu[s][:, :]
                    dve.wait_ge(tanh_done, m + 1)
                    dve.scalar_tensor_tensor(out=ga[:, :], in0=th[s][:, :], scalar=1.0, in1=g,
                                             op0=ALU.add, op1=ALU.mult).then_inc(gated, 1)
                    dve.wait_ge(gated, m + 1)
                    dve.scalar_tensor_tensor(out=pr[s][:, :], in0=ga[:, :], scalar=0.5, in1=u,
                                             op0=ALU.mult, op1=ALU.mult).then_inc(prod_done, 1)
                    if i is not None or jj + 3 < STEPS:
                        ns = (n0 + jj) % 3
                        dve.wait_ge(hi_done, n + 4)
                        dve.tensor_tensor(wl[ns][:, :], raw[ns][:, :], wh[ns][:, :].bitcast(F32),
                                          ALU.subtract).then_inc(lo_done, 1)
                    else:
                        lo(n0 + jj + 3)
                    dve.wait_ge(h_hi, m + 1)
                    dve.tensor_tensor(hl[s][:, :], pr[s][:, :], hh[s][:, :].bitcast(F32), ALU.subtract) \
                       .then_inc(h_ready, 1)
                    if i is not None or jj + 2 < STEPS:
                        dlo((m0 + jj + 2) % 3, m + 2)

                for j in range(2):
                    dlo((m0 + j) % 3, m0 + j)
                step(0, None, 0)
                with dve.Fori(0, LOOPED // 3) as i:
                    for s in range(1, 4):
                        step(3 * i + s, i, s)
                for j in range(LOOPED + 1, STEPS):
                    step(j, None, j)

            def after(name):
                lo(at[name] + 3)

            dve.memset(zero[:, :].bitcast(F32), 0.0).then_inc(zero_set, 1)
            dve.sem_inc(prod_done, 3)
            dve.wait_ge(pos_loaded, 16)
            dve.wait_ge(con_loaded, 16)
            then(dve.tensor_copy(posf[:, :], posi[:, :]))
            inv = con[:, K_INV:K_INV + ROPE // 2]
            for t in range(NT):
                then(dve.tensor_scalar(ang[:, t, :], inv, posf[:, t:t + 1], None, ALU.mult))
            magic = 1.5 * 2.0 ** 23
            then(dve.tensor_scalar(kk[:, :, :], ang[:, :, :], float(1.0 / (2 * np.pi)), magic, ALU.mult, ALU.add))
            then(dve.tensor_scalar(kk[:, :, :], kk[:, :, :], -magic, None, ALU.add))
            rest = 2 * np.pi
            src = ang
            for bits in (2 ** 5, 2 ** 14, 2 ** 23, None):
                part = float(np.float32(rest)) if bits is None else float(np.floor(rest * bits) / bits)
                rest -= part
                then(dve.scalar_tensor_tensor(out=r0[:, :, :], in0=kk[:, :, :], scalar=-part, in1=src[:, :, :],
                                              op0=ALU.mult, op1=ALU.add))
                src = r0
            pi32 = 3.1415925
            then(dve.tensor_scalar(r0[:, :, :], r0[:, :, :], pi32, -pi32, ALU.min, ALU.max))
            then(dve.tensor_scalar(r1[:, :, :], r0[:, :, :], -1.0, None, ALU.mult))
            then(dve.tensor_tensor(r1[:, :, :], r1[:, :, :], r0[:, :, :], ALU.min))
            dve.tensor_scalar(r1[:, :, :], r1[:, :, :], float(np.pi / 2), None, ALU.add).then_inc(rope_a, 1)
            dve.wait_ge(rope_s, 2)
            dve.tensor_copy(cs[:, :, 32:64], cs[:, :, 0:32]).then_inc(rope_s, 1)
            dve.tensor_scalar(sn[:, :, 0:32], sn[:, :, 32:64], -1.0, None, ALU.mult).then_inc(rope_s, 1)
            dve.wait_ge(rstd_done, NT)
            dve.wait_ge(band_loaded, 16)
            edge = NG * P + NG * EDGE
            dve.tensor_scalar(bandr[:, 0:edge], band[:, 0:edge], rstd[:, 0, 0:1], None, ALU.mult) \
               .then_inc(pool_scaled, 1)
            dve.tensor_scalar(bandr[:, edge:NPOOL], band[:, edge:NPOOL], rstd[:, 0, 1:2], None, ALU.mult) \
               .then_inc(pool_scaled, 1)
            dve.wait_ge(raw_full[0], 32)
            dve.wait_ge(pscale_loaded, 16)
            rv = raw[0][:, :].rearrange("p (g c d) -> p g c d", g=NG, c=2)
            pv_ = pscale[:, :].rearrange("p (g a d) -> p g a d", g=NG, a=1).to_broadcast([P, NG, 2, 256])
            dve.tensor_tensor(rv, rv, pv_, ALU.mult).then_inc(pool_scaled, 1)
            dve.wait_ge(cols_done, 1)
            taps = col[:, C_CDW:C_CDW + 2 * TAPS]
            dve.tensor_scalar(taps, taps, 0.5, None, ALU.mult).then_inc(taps_halved, 1)
            lo(0)
            split_t(0, xh, xl, C_MIX0, 0)
            diagonals(1)
            lo(1)
            lo(2)
            split_t(1, mh, ml, C_MEMN, 4)
            residual(0, block_used, at["pool"] + 1)
            dve.sem_inc(region_free, 1)
            norm(2, 2, C_FFN)
            lo(3)
            after("mem0")
            ffn(0)
            residual(1, down_done, 3 + STEPS)
            norm(3, 3, C_MIX1)
            after("mem1")
            after("down0")
            after("down1")
            for part in range(2):
                dve.wait_ge(mla_rs, part + 1)
                for t in range(NT):
                    dve.tensor_scalar(dqk[:, part, t, :], ident, mst[:, 3, part, t:t + 1], None, ALU.mult) \
                       .then_inc(mla_dg, 1)
                if part == 0:
                    after("down2")
            after("mem2")

            def rope(src, dst, nh, t):
                n = nh * ROPE
                c = cs[:, t:t + 1, :].to_broadcast([P, nh, ROPE])
                s = src.rearrange("p (h d) -> p h d", h=nh)
                a3 = ra[:, 0:n].rearrange("p (h d) -> p h d", h=nh)
                b3 = rb[:, 0:n].rearrange("p (h d) -> p h d", h=nh)
                dve.tensor_tensor(a3, s, c, ALU.mult)
                dve.tensor_tensor(b3[:, :, 0:32], s[:, :, 32:64], sn[:, t:t + 1, 0:32].to_broadcast([P, nh, 32]),
                                  ALU.mult)
                then(dve.tensor_tensor(b3[:, :, 32:64], s[:, :, 0:32],
                                       sn[:, t:t + 1, 32:64].to_broadcast([P, nh, 32]), ALU.mult))
                return dve.tensor_tensor(dst, ra[:, 0:n], rb[:, 0:n], ALU.add)

            for t in range(NT):
                dve.wait_ge(ds_out, 4)
                then(rope(ds[:, t, QLR + KVR:MLA_DOWN], kr[:, t, 0:ROPE], 1, t))
                dve.tensor_copy(kr[:, t, ROPE:P], kr[:, t, 0:ROPE]).then_inc(kr_done, 1)
            for f in range(4):
                dve.wait_ge(cq_hi, f // 2 * 2 + 2)
                dve.scalar_tensor_tensor(out=xl[:, f, :], in0=bank[4 + f // 2][:, (f % 2) * SEQ:(f % 2 + 1) * SEQ],
                                         scalar=col[:, C_QN + f:C_QN + f + 1], in1=xh[:, f, :].bitcast(F32),
                                         op0=ALU.mult, op1=ALU.subtract).then_inc(cq_lo, 1)
            for b in range(3):
                after(f"uq{b}")
            dve.wait_ge(block_used, at["uq2"] + 1)
            for t in range(NT):
                if t:
                    dve.wait_ge(qr_done, t)
                rope(bank[t][:, :], qr[:, t, :], HEADS, t).then_inc(qr_done, 1)
            after("ukv")

            def mla_max(h):
                dve.wait_ge(s_mm, h + 1)
                if h >= 2:
                    dve.wait_ge(p_t, h - 1)
                for t, (a, b) in enumerate(((0, P), (P, 3 * P))):
                    ins = dve.tensor_tensor_reduce(sc[h % 2][:, a:b], bank[4 + h % 2][:, a:b], mask[:, a:b], MLA_SCALE,
                                                   3.0 * NEG, ALU.add, ALU.max, stat[:, h, 0, t:t + 1])
                then(ins)
                dve.tensor_scalar(stat[:, h, 1, :], stat[:, h, 0, :], -1.0, None, ALU.mult).then_inc(s_max, 1)

            def mla_norm(h):
                dve.wait_ge(s_exp, 2 * h + 2)
                then(dve.reciprocal(stat[:, h, 3, :], stat[:, h, 2, :]))
                for t, (a, b) in enumerate(((0, P), (P, 3 * P))):
                    ins = dve.tensor_scalar(sc[h % 2][:, a:b], sc[h % 2][:, a:b], stat[:, h, 3, t:t + 1], None,
                                            ALU.mult)
                    ins.then_inc(s_norm, 1)

            def mla_o(h):
                dve.wait_ge(o_hi, h + 1)
                dve.tensor_tensor(xl[:, h, :], bank[7][:, (h % 2) * SEQ:(h % 2 + 1) * SEQ], xh[:, h, :].bitcast(F32),
                                  ALU.subtract).then_inc(o_lo, 1)

            mla_max(0)
            for h in range(1, HEADS + 1):
                if h < HEADS:
                    mla_max(h)
                mla_norm(h - 1)
                mla_o(h - 1)
                if h in (4, 6):
                    after(f"wo{h // 2 - 2}")
            after("wo2")
            residual(2, block_used, at["wo3"] + 1)
            dve.sem_inc(region_free, 1)
            after("wo3")
            norm(4, 4, C_FFN + 8)
            after("mem3")
            ffn(1)
            residual(3, down_done, 3 + 2 * STEPS)
            dve.wait_ge(gain_loaded, 16)
            times_gain()
            dve.memset(vbd[:, :], 0.0).then_inc(vbd_zero, 1)
            dve.memset(hc[:, :, 0:PAD], 0.0)
            diagonals(6)
            after("mem4")
            split_t(5, xh, xl, C_MIXN, 0)
            after("mem5")
            times_rstd()
            after("z_a")
            after("z_gt")
            dve.wait_ge(z_out, 1)
            then(dve.scalar_tensor_tensor(out=hc[:, :, PAD:PAD + SEQ], in0=e1[:, :].rearrange("p (a s) -> p a s", a=2),
                                          scalar=1.0, in1=bank[0][:, :].rearrange("p (a s) -> p a s", a=2),
                                          op0=ALU.add, op1=ALU.mult))
            dve.sem_inc(hc_done, 1)

            def conv(k0, k1):
                for k in range(k0, k1):
                    for c in range(2):
                        tap = col[:, C_CDW + 2 * k + c:C_CDW + 2 * k + c + 1]
                        if k == 0:
                            ins = dve.tensor_scalar(yc[:, c, :], hc[:, c, 0:SEQ], tap,
                                                    col[:, C_CDB + c:C_CDB + c + 1], ALU.mult, ALU.add)
                        else:
                            dve.wait_ge(cv_tap, 2 * (k - 1) + c + 1)
                            ins = dve.scalar_tensor_tensor(out=yc[:, c, :], in0=hc[:, c, k:k + SEQ], scalar=tap,
                                                           in1=yc[:, c, :], op0=ALU.mult, op1=ALU.add)
                        ins.then_inc(cv_tap, 1)

            conv(0, 3)
            after("z_kcvc")
            conv(3, 6)
            dve.wait_ge(shifted, 64)
            for a in range(2):
                src = bass.AP(x4[:, a, :, :].tensor, x4[:, a, :, :].offset,
                              [list(x4[:, a, :, :].ap[0]), [2, CMP_KT], [SEQ, GROUPS], [CMP_STRIDE, NCMP]])
                pe_ = col[:, C_PE + a * CMP_KT:C_PE + (a + 1) * CMP_KT]
                pe_ = bass.AP(pe_.tensor, pe_.offset, [list(pe_.ap[0]), [1, CMP_KT], [0, GROUPS], [0, NCMP]])
                dve.tensor_tensor(fl[:, a, :, :, :], src, pe_, ALU.add).then_inc(fl_done, 1)
            after("z_q0")
            conv(6, 8)
            after("z_q1")
            dve.wait_ge(cmp_a, 1)
            hs = bank[7][0:DH, 0:60]
            dve.tensor_scalar(hg[:, 3, :], hg[:, 0, :], GELU_C, 1.0, ALU.mult, ALU.add).then_inc(cmp_d, 1)
            dve.wait_ge(cmp_d, 1)
            dve.tensor_tensor(hg[:, 2, :], hg[:, 3, :], hs, ALU.mult).then_inc(cmp_d, 1)
            dve.wait_ge(cmp_a, 2)
            dve.scalar_tensor_tensor(out=hg[:, 3, :], in0=hg[:, 1, :], scalar=1.0, in1=hs, op0=ALU.add,
                                     op1=ALU.mult).then_inc(cmp_d, 1)
            after("z_ksw")
            conv(8, 11)
            after("z_vsw")
            conv(11, TAPS_BEFORE)
            dve.wait_ge(gl_a, 1)
            dve.tensor_scalar(gate[:, :, :], gate[:, :, :], 1.0, 0.5, ALU.add, ALU.mult).then_inc(gl_done, 1)
            after("z_gl")
            for i, name in enumerate(("z_v", "z_u")):
                b = bank[(0, 1)[i]]
                dve.wait_ge(gz_a, 2 * i + 1)
                dve.tensor_scalar(e3[:, :], e1[:, :], GELU_C, 1.0, ALU.mult, ALU.add).then_inc(gz_d, 1)
                dve.wait_ge(gz_d, 3 * i + 1)
                dve.tensor_tensor(e2[:, :], e3[:, :], b[:, :], ALU.mult).then_inc(gz_d, 1)
                after(name)
                dve.wait_ge(gz_a, 2 * i + 2)
                dve.scalar_tensor_tensor(out=(vg, uu)[i], in0=e1[:, :], scalar=1.0, in1=b[:, :], op0=ALU.add,
                                         op1=ALU.mult).then_inc(gz_d, 1)
                dve.wait_ge(gz_d, 3 * i + 3)
                if i == 0:
                    for t in range(NT):
                        dve.bn_stats(lst[:, 6 * t:6 * t + 6], vg[:, t * GW:(t + 1) * GW])
                    then(dve.memset(lst[:, 60:61], 0.0))
                    for t in range(NT):
                        dve.bn_aggr(lst[:, 12 + 2 * t:14 + 2 * t], lst[:, 6 * t:6 * t + 6]).then_inc(vn_done, 1)
            dve.wait_ge(ln_rs, 1)
            dve.wait_ge(z_params, 64)
            for t in range(NT):
                then(dve.tensor_scalar(vg[:, t * GW:(t + 1) * GW], vg[:, t * GW:(t + 1) * GW],
                                       lst[:, 12 + 2 * t:13 + 2 * t], lst[:, 20 + t:21 + t], ALU.subtract, ALU.mult))
            v3 = vg.rearrange("p (t c) -> p t c", t=NT)
            then(dve.tensor_tensor(v3, v3, lng[:, 0, 0:1, :].to_broadcast([P, NT, GW]), ALU.mult))
            dve.tensor_tensor(v3, v3, lng[:, 0, 1:2, :].to_broadcast([P, NT, GW]), ALU.add).then_inc(vn_done, 1)
            n240 = NT * NSA_HEADS * NCMP
            dve.wait_ge(sc_mm, GROUPS)

            def m3(ap):
                return ap.rearrange("p (t h n) -> p t h n", t=NT, h=NSA_HEADS)

            def m2(ap):
                return ap.rearrange("p (a n) -> p a n", n=NCMP)

            def over_heads(c0):
                return con[:, c0:c0 + NT * NCMP].rearrange("p (t a n) -> p t a n", t=NT, a=1) \
                    .to_broadcast([P, NT, NSA_HEADS, NCMP])

            def per_row(ap):
                return ap.rearrange("p (a b) -> p a b", b=1).to_broadcast([P, NT * NSA_HEADS, NCMP])

            mx = lst[:, 24:24 + 16]
            for g in range(GROUPS):
                bias = con[:, K_CB:K_CB + NT * NCMP].rearrange("p (t a n) -> p t a n", t=NT, a=1) \
                    .to_broadcast([P, NT, REP, NCMP])
                sc_g = bank[2 + g][:, 0:n240 // GROUPS].rearrange("p (t h n) -> p t h n", t=NT, h=REP)
                then(dve.tensor_tensor(m3(cm[2])[:, :, g * REP:(g + 1) * REP, :], sc_g, bias, ALU.add))
            then(dve.tensor_reduce(mx, m2(cm[2]), AX.X, ALU.max))
            dve.tensor_tensor(m2(cm[0]), m2(cm[2]), per_row(mx), ALU.subtract).then_inc(cm_e, 1)
            dve.wait_ge(cm_e, 2)
            then(dve.tensor_tensor(m3(cm[2]), m3(cm[1]), over_heads(K_C01), ALU.mult))
            then(dve.tensor_reduce(mx, m2(cm[2]), AX.X, ALU.add))
            then(dve.tensor_scalar(mx, mx, TINY, None, ALU.max))
            then(dve.reciprocal(mx, mx))
            dve.wait_ge(gl_done, 1)
            gv = gate[:, :, :].rearrange("p t (h b) -> p t h b", b=3)
            then(dve.tensor_tensor(mx.rearrange("p (t h) -> p t h", t=NT), mx.rearrange("p (t h) -> p t h", t=NT),
                                   gv[:, :, :, 0], ALU.mult))
            dve.tensor_tensor(m2(cm[3]), m2(cm[2]), per_row(mx), ALU.mult).then_inc(pc_done, 1)

            def nsa_max(u):
                dve.wait_ge(n_mm, u + 1)
                if u >= 2:
                    dve.wait_ge(n_t, u - 1)
                for t, (a, b) in enumerate(((0, P), (P, 3 * P))):
                    ins = dve.tensor_tensor_reduce(s2[u % 2][:, a:b], bank[4 + u % 2][:, a:b], mask[:, a:b], NSA_SCALE,
                                                   3.0 * NEG, ALU.add, ALU.max, nst[:, 0, u, t:t + 1])
                then(ins)
                dve.tensor_scalar(nst[:, 1, u, :], nst[:, 0, u, :], -1.0, None, ALU.mult).then_inc(n_max, 1)

            def nsa_norm(u):
                h, br = u // 2, u % 2
                dve.wait_ge(n_exp, 2 * u + 2)
                then(dve.reciprocal(nst[:, 3, u, :], nst[:, 2, u, :]))
                then(dve.tensor_tensor(nst[:, 3, u, :], nst[:, 3, u, :], gv[:, :, h, 1 + br], ALU.mult))
                for t, (a, b) in enumerate(((0, P), (P, 3 * P))):
                    dve.tensor_scalar(s2[u % 2][:, a:b], s2[u % 2][:, a:b], nst[:, 3, u, t:t + 1], None, ALU.mult) \
                       .then_inc(n_norm, 1)

            e3v = e3[:, :].rearrange("p (t c) -> p t c", t=NT)
            e2v = e2[:, :].rearrange("p (t c) -> p t c", t=NT)

            def y_diagonals(segments):
                for s in segments:
                    for t in range(NT):
                        dve.tensor_scalar(dseg[:, 2 * s + t, :], ident, lst[:, 48 + 2 * s + t:49 + 2 * s + t], None,
                                          ALU.mult).then_inc(y_dg, 1)

            nsa_max(0)
            for u in range(1, 2 * NSA_HEADS + 1):
                if u < 2 * NSA_HEADS:
                    nsa_max(u)
                nsa_norm(u - 1)
                if u == 1:
                    dve.wait_ge(mix_mm, 1)
                    for t in range(NT):
                        dve.tensor_tensor(yn[:, t, 512:768], bank[7][:, t * GW:(t + 1) * GW], uu[:, t * GW:(t + 1) * GW],
                                          ALU.mult).then_inc(gy_done, 1)
                conv(min(TAPS, TAPS_BEFORE + 3 * (u - 1)), min(TAPS, TAPS_BEFORE + 3 * u))
                if u == U_STATS:
                    dve.wait_ge(ycs_t, 1)
                    for t in range(NT):
                        dve.bn_stats(lst[:, 6 * t:6 * t + 6], bank[3][:, t * CW_:(t + 1) * CW_])
                    then(dve.memset(lst[:, 60:61], 0.0))
                    for t in range(NT):
                        dve.bn_aggr(lst[:, 40 + 2 * t:42 + 2 * t], lst[:, 6 * t:6 * t + 6]).then_inc(vn_done, 1)
                if u == U_LN:
                    dve.wait_ge(ln_rs, 2)
                    for t in range(NT):
                        then(dve.tensor_scalar(e3[:, t * GW:(t + 1) * GW], bank[3][:, t * GW:(t + 1) * GW],
                                               lst[:, 40 + 2 * t:41 + 2 * t], lst[:, 44 + t:45 + t], ALU.subtract,
                                               ALU.mult))
                    then(dve.tensor_tensor(e3v, e3v, lng[:, 1, 0:1, :].to_broadcast([P, NT, GW]), ALU.mult))
                    dve.tensor_tensor(e2v, e3v, lng[:, 1, 1:2, :].to_broadcast([P, NT, GW]), ALU.add) \
                       .then_inc(cvln_done, 1)
                if u == U_SILU + 1:
                    dve.wait_ge(cv_a, 1)
                    dve.scalar_tensor_tensor(out=yn[:, :, 768:1024], in0=e1[:, :].rearrange("p (t c) -> p t c", t=NT),
                                             scalar=1.0, in1=e2v, op0=ALU.add, op1=ALU.mult).then_inc(cy_done, 1)
                if u == U_SQUARES + 1:
                    dve.wait_ge(y_rs, 1)
                    y_diagonals((1, 2))
                if u == U_SPLIT:
                    split_t(6, xh, xl, C_MOUT, 0, range(4, KD))
            dve.wait_ge(o_all, 2 * NSA_HEADS)
            for t in (1, 0):
                if t == 0:
                    dve.wait_ge(y_sq, 5)
                dve.tensor_copy(yn[:, t, 0:HALF], bank[t][:, :]).then_inc(yn_done, 1)
            dve.wait_ge(y_rs, 2)
            y_diagonals((0,))
            split_t(6, xh, xl, C_MOUT, 4, range(4), 4)
            for i in WOUT_ORDER[:3]:
                after(f"wout{i}")
            residual(4, block_used, at[f"wout{WOUT_ORDER[3]}"] + 1)
            after(f"wout{WOUT_ORDER[3]}")
            diagonals(7)
            split_t(7, xh, xl, C_XN, 0)
            after("mem6")
            after("mem7")
            def x_max(h):
                dve.wait_ge(a_mm, h + 1)
                then(dve.tensor_reduce(xst[:, h, 0, :], bank[4 + h % 2][:, :].rearrange("p (t s) -> p t s", t=NT), AX.X,
                                       ALU.max))
                dve.tensor_scalar(xst[:, h, 1, :], xst[:, h, 0, :], -XSCALE, None, ALU.mult).then_inc(a_max, 1)

            def x_norm(h):
                dve.wait_ge(a_exp, 2 * h + 2)
                then(dve.reciprocal(xst[:, h, 3, :], xst[:, h, 2, :]))
                for t in range(NT):
                    dve.tensor_scalar(sx[h % 2][:, t, :], sx[h % 2][:, t, :], xst[:, h, 3, t:t + 1], None, ALU.mult) \
                       .then_inc(a_norm, 1)

            def x_o(h):
                dve.wait_ge(ao_hi, h + 1)
                dve.tensor_tensor(ml[:, 2 * h:2 * h + 2, :].rearrange("p a s -> p (a s)"), bank[7][:, :],
                                  mh[:, 2 * h:2 * h + 2, :].rearrange("p a s -> p (a s)").bitcast(F32),
                                  ALU.subtract).then_inc(ao_lo, 1)

            after("xq0")
            after("xq1")
            x_max(0)
            x_norm(0)
            for h in range(1, XHEADS + 1):
                if h + 1 < XHEADS:
                    after(f"xq{h + 1}")
                if h < XHEADS:
                    x_max(h)
                    x_norm(h)
                else:
                    after("xo0")
                x_o(h - 1)
            for i in (1, 2):
                after(f"xo{i}")
            residual(5, block_used, at["xo3"] + 1)
            dve.sem_inc(region_free, 1)
            after("xo3")
            norm(8, 8, C_FN2)
            ffn(2)
            residual(6, down_done, 3 + 3 * STEPS)
            dve.wait_ge(last_gain_loaded, 16)
            last_norm(9)

        @block.gpsimd
        def _(pool):
            order = [0]

            def then(ins):
                order[0] += 1
                ins.then_inc(pool_order, 1)
                pool.wait_ge(pool_order, order[0])

            def inverse_rms(q):
                for t in range(NT):
                    one = slice(t, t + 1)
                    pool.wait_ge(sq_done, 4 * q + 2 * t + 2)
                    then(pool.tensor_scalar(st1[:, q, one], ss[:, q, t, 0:1], ss[:, q, t, 1:2], EPS, ALU.add, ALU.add))
                    pool.tensor_tensor(rstd[:, q, one], st1[:, q, one], mhalf[:, 0:1], ALU.pow).then_inc(rstd_done, 1)

            def inverse_rms_after_norm():
                for t in range(NT):
                    one = slice(t, t + 1)
                    r = rstd[:, 5, one]
                    pool.wait_ge(sq_done, 4 * 6 + 2 * t + 2)
                    then(pool.tensor_scalar(st1[:, 6, one], ss[:, 6, t, 0:1], ss[:, 6, t, 1:2], r, ALU.add, ALU.mult))
                    then(pool.tensor_scalar(st1[:, 6, one], st1[:, 6, one], r, EPS, ALU.mult, ALU.add))
                    then(pool.tensor_tensor(st2[:, 6, one], st1[:, 6, one], mhalf[:, 0:1], ALU.pow))
                    pool.tensor_tensor(rstd[:, 6, one], st2[:, 6, one], r, ALU.mult).then_inc(rstd_done, 1)

            then(pool.memset(mhalf[:, :], -0.5))
            for q in range(4):
                inverse_rms(q)
            for part, width in ((0, QLR), (1, KVR)):
                pool.wait_ge(mla_sq, 2 * part + 2)
                then(pool.tensor_scalar(mst[:, 1, part, :], mst[:, 0, part, :], 1.0 / width, EPS, ALU.mult, ALU.add))
                pool.tensor_tensor(mst[:, 3, part, :], mst[:, 1, part, :], mhalf[:, 0:NT], ALU.pow).then_inc(mla_rs, 1)
            inverse_rms(4)
            pool.wait_ge(down_done, 3 + 2 * STEPS)
            pool.dma_start(cw1[:, :, :, :], w["cmp_w1_2"][0].rearrange("a (k p) d -> p a k d", p=P)).then_inc(z_ws, 16)
            pool.dma_start(cw2[:, :, :], w["cmp_w2_2"][0].rearrange("a p d -> p a d")).then_inc(z_ws, 16)
            pool.dma_start(bsr[:, :], w["gmlp_bs_2"][0]).then_inc(z_ws, 16)
            for i, name in enumerate(("gmlp_ln_g_2", "gmlp_ln_b_2", "conv_ln_g_2", "conv_ln_b_2")):
                pool.dma_start(lng[:, i // 2, i % 2, :], w[name][0:1, :].to_broadcast([P, GW])).then_inc(z_params, 16)
            inverse_rms(5)
            inverse_rms_after_norm()
            pool.wait_ge(gained, 4)
            pool.dma_start(gain[:, :], w["final_norm_g_2"].rearrange("(a d) -> a d", a=1).to_broadcast([P, D])) \
                .then_inc(last_gain_loaded, 16)
            pool.wait_ge(cmp_mm, 1)
            pool.dma_start(ws.rearrange("p (g s) -> p g s", g=GG), w["gmlp_ws_2"][0].rearrange("g t s -> t g s")) \
                .then_inc(ws_loaded, 16)
            pool.wait_ge(ws_loaded, 16)
            w3 = ws.rearrange("p (g s) -> p g s", g=GG)
            pool.affine_select(out=w3, in_=w3, compare_op=ALU.is_ge, fill=0.0, base=0,
                               pattern=[[0, GG], [-1, P]], channel_multiplier=1).then_inc(ws_cut, 1)
            for i, (src, dst) in enumerate(((12, 20), (40, 44))):
                pool.wait_ge(vn_done, 2 if i == 0 else 5)
                var = lst[:, src:src + 4].rearrange("p (t b) -> p t b", b=2)[:, :, 1]
                then(pool.tensor_scalar(lst[:, 16 + 2 * i:18 + 2 * i], var, 1.0, 4.0 * EPS if i == 0 else EPS,
                                        ALU.mult, ALU.add))
                pool.tensor_tensor(lst[:, dst:dst + 2], lst[:, 16 + 2 * i:18 + 2 * i], mhalf[:, 0:NT], ALU.pow) \
                    .then_inc(ln_rs, 1)
            pool.wait_ge(y_sq, 4)
            then(pool.tensor_scalar(lst[:, 56:60], lst[:, 34:38], 1.0 / 256, 4.0 * EPS, ALU.mult, ALU.add))
            pool.tensor_tensor(lst[:, 50:54], lst[:, 56:60], mhalf[:, 0:4], ALU.pow).then_inc(y_rs, 1)
            pool.wait_ge(y_sq, 6)
            then(pool.tensor_scalar(lst[:, 54:56], lst[:, 32:34], 1.0 / 512, EPS, ALU.mult, ALU.add))
            pool.tensor_tensor(lst[:, 48:50], lst[:, 54:56], mhalf[:, 0:2], ALU.pow).then_inc(y_rs, 1)
            inverse_rms(7)
            inverse_rms(8)
            inverse_rms(9)

        @block.tensor
        def _(pe):
            def three(outp, a_hi, a_lo, b_hi, b_lo, start, stop, **kw):
                pe.matmul(outp, a_hi, b_hi, start=start, stop=False, **kw)
                pe.matmul(outp, a_hi, b_lo, start=False, stop=False, **kw)
                return pe.matmul(outp, a_lo, b_hi, start=False, stop=stop, **kw)

            def weights(name, k, c):
                n = at[name]
                pe.wait_ge(lo_done, n + 1)
                return k_view(wh[n % 3], k, c), k_view(wl[n % 3], k, c)

            def transpose_norm(src, dg, banks, ks=range(KD), ready=None):
                for t in range(NT):
                    if ready is not None:
                        ready(t)
                    for k in ks:
                        o = bank[banks + k // 2][:, (k % 2) * SEQ + t * P:(k % 2) * SEQ + (t + 1) * P]
                        ins = pe.matmul(o, src[:, t, k * P:(k + 1) * P], dg(k, t), start=True, stop=True)
                        if k % 2 and t == NT - 1:
                            ins.then_inc(t_done, 1)

            def split_wait(e):
                return lambda k: pe.wait_ge(t_lo, KD * e + max(k + 1, 2))

            def columns(name, b, a_hi, a_lo, ready=None):
                h_, l_ = weights(name, KD, 2 * P)
                for f in range(2):
                    for k in range(KD):
                        if ready is not None and f == 0:
                            ready(k)
                        fs = slice(f * P, (f + 1) * P)
                        ins = three(bank[b][:, f * SEQ:(f + 1) * SEQ], h_[:, k, fs], l_[:, k, fs], a_hi[:, k, :],
                                    a_lo[:, k, :], k == 0, k == KD - 1)
                ins.then_inc(block_used, 1)

            def tokens(name, b, width, a_hi, a_lo, at_col=None, ready=None):
                h_, l_ = weights(name, KD, width)
                for t in range(NT):
                    for k in range(KD):
                        if ready is not None and t == 0:
                            ready(k)
                        c = width * t if at_col is None else at_col
                        bb = b if at_col is None else b + t
                        ins = three(bank[bb][:, c:c + width], a_hi[:, k, t * P:(t + 1) * P],
                                    a_lo[:, k, t * P:(t + 1) * P], h_[:, k, :], l_[:, k, :], k == 0, k == KD - 1)
                ins.then_inc(block_used, 1)

            def row_block(name, i, a_hi, a_lo, first, last, tiles=range(NT), ready=None):
                h_, l_ = weights(name, 2, D)
                for t in tiles:
                    if ready is not None:
                        ready(t)
                    for c in range(2):
                        for kk_ in range(2):
                            ins = three(bank[2 * t + c][:, :], a_hi[:, 2 * i + kk_, t * P:(t + 1) * P],
                                        a_lo[:, 2 * i + kk_, t * P:(t + 1) * P], h_[:, kk_, c * HALF:(c + 1) * HALF],
                                        l_[:, kk_, c * HALF:(c + 1) * HALF], first and kk_ == 0, last and kk_ == 1)
                        if last and (t, c) != (NT - 1, 1):
                            ins.then_inc(bank_sum, 1)
                ins.then_inc(block_used, 1)

            def mem_block(i):
                if i > 0:
                    pe.wait_ge(mem_out, i)
                if i < 4:
                    columns(f"mem{i}", 7, mh, ml)
                else:
                    tokens(f"mem{i}", 7, 2 * P, mh, ml)

            def diagonal_ready(nd):
                return lambda t: pe.wait_ge(diag_done, nd - 1 + t)

            def norm(e, nd, rs):
                pe.wait_ge(res_done, rs)
                transpose_norm(xt, lambda k, t: diag[:, t, :], 0, ready=diagonal_ready(nd))

            def ffn(layer, e):
                n0, m0 = at[f"ffn{layer}"], STEPS * layer
                split = split_wait(e)

                def up(j, jj):
                    n, m = n0 + j, m0 + j
                    ns, s = (n0 + jj) % 3, (m0 + jj) % 3
                    pe.wait_ge(lo_done, n + 1)
                    pe.wait_ge(prod_done, m + 1)
                    for half in range(2):
                        for k in range(KD):
                            if jj == 0 and half == 0:
                                split(k)
                            a = (2 * k + half) * P
                            ins = three(bank[4 + s][:, half * SEQ:(half + 1) * SEQ], wh[ns][:, a:a + P],
                                        wl[ns][:, a:a + P], xh[:, k, :], xl[:, k, :], k == 0, k == KD - 1)
                    ins.then_inc(block_used, 1)

                def down(j, jj, last=False):
                    m = m0 + j
                    s = (m0 + jj) % 3
                    pe.wait_ge(d_lo, m + 1)
                    pe.wait_ge(h_ready, m + 1)
                    for t in range(NT):
                        for c in range(2):
                            ins = three(bank[2 * t + c][:, :], hh[s][:, t * P:(t + 1) * P], hl[s][:, t * P:(t + 1) * P],
                                        dh[s][:, c * HALF:(c + 1) * HALF], dl[s][:, c * HALF:(c + 1) * HALF],
                                        False, last, skip_group_check=True)
                            if last and (t, c) != (NT - 1, 1):
                                ins.then_inc(bank_sum, 1)
                    ins.then_inc(down_done, 1)

                up(0, 0)
                for b in range(4):
                    pe.matmul(bank[b][:, :], zero[:, :], xh[:, 0:2, :], start=True, stop=False, skip_group_check=True)
                with pe.Fori(0, LOOPED // 3) as i:
                    for s in range(1, 4):
                        up(3 * i + s, s)
                        down(3 * i + s - 1, s - 1)
                for j in range(LOOPED + 1, STEPS):
                    up(j, j)
                    down(j - 1, j - 1)
                down(STEPS - 1, STEPS - 1, True)

            pe.sem_inc(down_done, 3)
            pe.wait_ge(con_loaded, 16)
            pe.wait_ge(rows_loaded, 16 * 15)
            c = 0
            for i, n in enumerate((C_CDW, 2 * TAPS + 2 * CMP_KT, 2 * NF2, 2 * NF2)):
                ins = pe.transpose(bank[7][:, c:c + n], prow[i][0:n, :], con[0:n, K_ID:K_ID + n])
                c += n
            ins.then_inc(cols_t, 1)
            pe.wait_ge(zero_set, 1)
            pe.wait_ge(x_loaded, 16 * NT)
            pe.wait_ge(pool_scaled, 2)
            for k in range(KD):
                g = k // 2
                o = (k % 2) * SEQ
                b = bank[k // 2]
                ks = slice(k * P, (k + 1) * P)
                e0, d1 = NG * P + g * EDGE, NG * P + NG * EDGE + g * P
                pe.matmul(b[:, o:o + P], xt[:, 0, ks], bandr[:, g * P:(g + 1) * P], start=True, stop=True)
                pe.matmul(b[:, o + P:o + SEQ], xt[:, 1, ks], bandr[:, d1:d1 + P], start=True, stop=True)
                ins = pe.matmul(b[:, o + P:o + P + EDGE], xt[:, 0, ks], bandr[:, e0:e0 + EDGE], start=False, stop=True,
                                skip_group_check=True)
                if k % 2:
                    ins.then_inc(t_done, 1)
            h_, l_ = weights("pool", 2 * NG, 256)
            split = split_wait(0)
            for t in range(NT):
                for g in range(NG):
                    for c in range(2):
                        k = 2 * g + c
                        if t == 0:
                            split(k)
                        ins = three(bank[2 * t + g // 2][:, (g % 2) * 256:(g % 2 + 1) * 256],
                                    xh[:, k, t * P:(t + 1) * P], xl[:, k, t * P:(t + 1) * P],
                                    h_[:, k, :], l_[:, k, :], c == 0, c == 1)
                    if g % 2 and (t, g) != (NT - 1, NG - 1):
                        ins.then_inc(bank_sum, 1)
            ins.then_inc(block_used, 1)
            pe.wait_ge(mem_loaded, 16)
            pe.wait_ge(diag_done, 2)
            pe.wait_ge(cols_done, 1)
            transpose_norm(memt, lambda k, t: diag[:, t, :], 4)
            pe.wait_ge(t_lo, KD * 2)
            mem_block(0)
            norm(2, 4, 4)
            ffn(0, 2)
            mem_block(1)
            norm(3, 6, 8)
            for b in range(3):
                tokens(f"down{b}", (0, 0, 2)[b], MLA_DOWN // 3, xh, xl, at_col=(0, 192, 0)[b],
                       ready=split_wait(3) if b == 0 else None)
            mem_block(2)
            for f in range(4):
                part = f // 3
                pe.wait_ge(mla_dg, 2 * part + 2)
                for t in range(NT):
                    ins = pe.matmul(bank[4 + f // 2][:, (f % 2) * SEQ + t * P:(f % 2) * SEQ + (t + 1) * P],
                                    ds[:, t, f * P:(f + 1) * P], dqk[:, part, t, :], start=True, stop=True)
                if f % 2:
                    ins.then_inc(cq_t, 1)
            pe.wait_ge(kr_done, 2)
            for t in range(NT):
                ins = pe.transpose(bank[6][:, t * P:(t + 1) * P], kr[:, t, :], ident)
            ins.then_inc(kr_t, 1)
            pe.wait_ge(cq_lo, 4)
            hw = NOPE + ROPE
            for b, nh in enumerate((3, 3, 2)):
                h_, l_ = weights(f"uq{b}", 3, nh * hw)
                for i in range(nh):
                    h = 3 * b + i
                    if h >= 4 and h % 2 == 0:
                        pe.wait_ge(qk_out, h // 2 - 1)
                    for k in range(3):
                        ins = three(bank[4 + (h % 4) // 2][:, (h % 2) * SEQ:(h % 2 + 1) * SEQ],
                                    h_[:, k, i * hw:i * hw + NOPE], l_[:, k, i * hw:i * hw + NOPE],
                                    xh[:, k, :], xl[:, k, :], k == 0, k == 2)
                    if h % 2:
                        ins.then_inc(qk_mm, 1)
                for t in range(NT):
                    for k in range(3):
                        def rp(v):
                            return v[:, k, :].rearrange("p (h c) -> p h c", c=hw)[:, :, NOPE:hw]
                        ins = three(bank[t][:, 3 * b * ROPE:(3 * b + nh) * ROPE], xh[:, k, t * P:(t + 1) * P],
                                    xl[:, k, t * P:(t + 1) * P], rp(h_), rp(l_), k == 0, k == 2)
                ins.then_inc(block_used, 1)
            h_, l_ = weights("ukv", 1, 2048)
            pe.wait_ge(kr_out, 1)
            for h in range(HEADS):
                if h % 2 == 0:
                    pe.wait_ge(qk_out, 3 + h // 2)
                a = 2 * P * h
                ins = three(bank[4 + (h % 4) // 2][:, (h % 2) * SEQ:(h % 2 + 1) * SEQ], h_[:, 0, a:a + P], l_[:, 0, a:a + P],
                            xh[:, 3, :], xl[:, 3, :], True, True)
                if h % 2:
                    ins.then_inc(qk_mm, 1)
            for i in range(4):
                t, hv = i // 2, i % 2
                if i == 3:
                    pe.wait_ge(v_out, 1)

                def vp(v):
                    return v[:, 0, :].rearrange("p (h c) -> p h c", c=2 * P)[:, 4 * hv:4 * hv + 4, P:2 * P]
                ins = three(bank[(2, 3, 6, 2)[i]][:, :], xh[:, 3, t * P:(t + 1) * P], xl[:, 3, t * P:(t + 1) * P],
                            vp(h_), vp(l_), True, True)
                if i < 3:
                    ins.then_inc(v_mm, 1)
            ins.then_inc(block_used, 1)
            pe.wait_ge(qr_done, 2)
            for i in range(4):
                for t in range(NT):
                    ins = pe.transpose(bank[i // 2][:, (i % 2) * SEQ + t * P:(i % 2) * SEQ + (t + 1) * P],
                                       qr[:, t, i * P:(i + 1) * P], ident)
                if i % 2:
                    ins.then_inc(qr_t, 1)
            pe.wait_ge(qr_out, 2)
            pe.wait_ge(v_out, 4)
            pe.wait_ge(qk_out, HEADS)

            def mla_scores(h):
                if h >= 2:
                    pe.wait_ge(s_max, h - 1)
                half = slice((h % 2) * ROPE, (h % 2 + 1) * ROPE)
                for t, (a, b, keys) in enumerate(((0, P, P), (P, 3 * P, SEQ))):
                    o = bank[4 + h % 2][:, a:b]
                    tok = slice(t * P, (t + 1) * P)
                    pe.matmul(o, qn[:, h, tok], kn[:, h, 0:keys], start=True, stop=False)
                    ins = pe.matmul(o, qrt[half, h // 2, tok], krt[half, 0:keys], start=False, stop=True)
                ins.then_inc(s_mm, 1)

            def mla_pt(h):
                pe.wait_ge(s_norm, 2 * h + 2)
                if h >= 1:
                    pe.wait_ge(p_out, h)
                for i, a in enumerate((0, P, 2 * P)):
                    ins = pe.transpose(bank[6][:, i * P:(i + 1) * P], sc[h % 2][:, a:a + P], ident)
                ins.then_inc(p_t, 1)

            def mla_pv(h):
                pe.wait_ge(p_out, h + 1)
                if h >= 1:
                    pe.wait_ge(o_lo, h)
                o = (h % 2) * SEQ
                pe.matmul(bank[7][:, o:o + SEQ], vv[:, 0, h * P:(h + 1) * P], pt[h % 2][:, 0:SEQ], start=True, stop=True)
                pe.matmul(bank[7][:, o + P:o + SEQ], vv[:, 1, h * P:(h + 1) * P], pt[h % 2][:, SEQ:SEQ + P], start=False,
                          stop=True, skip_group_check=True).then_inc(o_mm, 1)

            pe.wait_ge(mem_out, 3)
            mla_scores(0)
            mla_scores(1)
            for h in range(HEADS):
                mla_pt(h)
                if h + 2 < HEADS:
                    mla_scores(h + 2)
                mla_pv(h)
                if h in (2, 4):
                    i = h // 2 - 1
                    pe.wait_ge(o_lo, 2 * i + 2)
                    row_block(f"wo{i}", i, xh, xl, i == 0, False)
            row_block("wo2", 2, xh, xl, False, False)
            pe.wait_ge(o_lo, HEADS)
            row_block("wo3", 3, xh, xl, False, True)
            mem_block(3)
            norm(4, 8, 12)
            ffn(1, 4)
            mem_block(4)
            norm(5, 10, 16)
            mem_block(5)
            pe.wait_ge(t_lo, KD * 6)
            columns("z_a", 0, xh, xl)
            columns("z_gt", 1, xh, xl)
            columns("z_kcvc", 2, xh, xl)

            columns("z_q0", 3, xh, xl)
            pe.wait_ge(hc_done, 1)
            columns("z_q1", 0, xh, xl)
            pe.wait_ge(fl_done, 2)
            pe.wait_ge(z_ws, 48)
            pe.wait_ge(mem_out, 6)
            for a in range(2):
                for k in range(CMP_KT):
                    ins = pe.matmul(bank[7][0:DH, 30 * a:30 * a + 30], cw1[:, a, k, :],
                                    fl[:, a, k, :, :].rearrange("p g n -> p (g n)"), start=k == 0, stop=k == CMP_KT - 1)
            ins.then_inc(cmp_mm, 1)
            columns("z_ksw", 1, xh, xl)
            pe.wait_ge(cmp_d, 3)
            for g in range(GROUPS):
                pe.matmul(bank[7][g * DH:(g + 1) * DH, 64:64 + NCMP], cw2[:, 0, :], hg[:, 3, g * NCMP:(g + 1) * NCMP],
                          start=True, stop=True)
            for g in range(GROUPS):
                ins = pe.matmul(bank[7][0:NCMP, 128 + g * DH:128 + (g + 1) * DH],
                                hg[:, 3, 30 + g * NCMP:30 + (g + 1) * NCMP], cw2[:, 1, :], start=True, stop=True)
            ins.then_inc(cmp_mm, 1)
            pe.wait_ge(z_out, 2)
            tokens("z_vsw", 2, 2 * P, xh, xl)
            pe.wait_ge(z_out, 3)
            tokens("z_gl", 3, 24, xh, xl)
            pe.wait_ge(z_out, 4)
            tokens("z_v", 0, GW, xh, xl)
            pe.wait_ge(z_out, 5)
            tokens("z_u", 1, GW, xh, xl)
            pe.wait_ge(ws_cut, 1)
            for g in range(GG):
                ins = pe.transpose(bank[6][:, g * P:(g + 1) * P], ws[:, g * P:(g + 1) * P], ident)
            ins.then_inc(ws_t, 1)
            pe.wait_ge(z_out, 6)
            pe.wait_ge(cmp_out, 2)
            pe.wait_ge(gl_a, 1)
            for g in range(GROUPS):
                rows_ = slice(g * DH, (g + 1) * DH)
                for t, j in ((t, j) for t in range(NT) for j in range(REP)):
                    c = (t * REP + j) * NCMP
                    ins = pe.matmul(bank[2 + g][:, c:c + NCMP], qt[rows_, j, t * P:(t + 1) * P], kcm[rows_, :], start=True,
                                    stop=True)
                ins.then_inc(sc_mm, 1)

            def nsa_scores(u):
                if u >= 2:
                    pe.wait_ge(n_max, u - 1)
                h, br = u // 2, u % 2
                g, j = h // REP, h % REP
                rows_ = slice(g * DH, (g + 1) * DH)
                for t, (a, b, keys) in enumerate(((0, P, P), (P, 3 * P, SEQ))):
                    ins = pe.matmul(bank[4 + u % 2][:, a:b], qt[rows_, j, t * P:(t + 1) * P], ksw[rows_, br, 0:keys],
                                    start=True, stop=True)
                ins.then_inc(n_mm, 1)

            nsa_scores(0)
            nsa_scores(1)
            pe.wait_ge(ws_out, 1)
            pe.wait_ge(vn_done, 3)
            for t in range(NT):
                pe.matmul(bank[7][:, t * GW:(t + 1) * GW], bsr[:, :], con[0:GG, K_SEL:K_SEL + GW], start=True, stop=False,
                          skip_group_check=True)
                for g in range(GG):
                    o = t * GW + g * GW // GG
                    ins = pe.matmul(bank[7][:, o:o + GW // GG], wst[:, g, :], vg[:, o:o + GW // GG], start=False,
                                    stop=g == GG - 1, skip_group_check=True)
            ins.then_inc(mix_mm, 1)
            pe.wait_ge(pc_done, 1)
            for t in range(NT):
                pe.transpose(bank[6][0:120, t * P:(t + 1) * P], cm[3][:, t * 120:(t + 1) * 120], ident).then_inc(pc_t, 1)
            pe.wait_ge(pc_out, 1)
            pe.wait_ge(vbd_set, 16 * NSA_HEADS)
            pe.wait_ge(gz_d, 6)
            for t in range(NT):
                pe.matmul(bank[t][:, :], e1[0:120, t * P:(t + 1) * P], vbd[0:120, :], start=True, stop=False,
                          skip_group_check=True)

            def nsa_pt(u):
                pe.wait_ge(n_norm, 2 * u + 2)
                if u >= 1:
                    pe.wait_ge(n_out, u)
                for i, a in enumerate((0, P, 2 * P)):
                    ins = pe.transpose(bank[6][:, i * P:(i + 1) * P], s2[u % 2][:, a:a + P], ident)
                ins.then_inc(n_t, 1)

            def nsa_pv(u):
                h, br = u // 2, u % 2
                g = h // REP
                pe.wait_ge(n_out, u + 1)
                p_ = p2[u % 2]
                v0 = vsw[:, 0, br * P + g * DH:br * P + (g + 1) * DH]
                v1 = vsw[:, 1, br * P + g * DH:br * P + (g + 1) * DH]
                hs = slice(h * DH, (h + 1) * DH)
                last = u == 2 * NSA_HEADS - 1
                pe.matmul(bank[0][:, hs], p_[:, 0:P], v0, start=False, stop=last, skip_group_check=True)
                pe.matmul(bank[1][:, hs], p_[:, P:2 * P], v0, start=False, stop=False, skip_group_check=True)
                pe.matmul(bank[1][:, hs], p_[:, 2 * P:3 * P], v1, start=False, stop=last, skip_group_check=True) \
                  .then_inc(o_all, 1)

            seg = (0, 0, 0, 0, 1, 1, 2, 2)
            for u in range(2 * NSA_HEADS):
                nsa_pt(u)
                if u + 2 < 2 * NSA_HEADS:
                    nsa_scores(u + 2)
                nsa_pv(u)
                if u == U_TURN - 1:
                    pe.wait_ge(cv_tap, 2 * TAPS)
                    for t in range(NT):
                        for c in range(2):
                            ins = pe.transpose(bank[3][:, t * CW_ + c * P:t * CW_ + (c + 1) * P],
                                               yc[:, c, t * P:(t + 1) * P], ident)
                    ins.then_inc(ycs_t, 1)
                if u == U_TURN_Y - 1:
                    pe.wait_ge(y_dg, 4)
                    transpose_norm(yn, lambda k, t: dseg[:, 2 * seg[k] + t, :], 0, range(4, KD))
            pe.wait_ge(t_lo, KD * 6 + 4)

            def attention_left(t):
                if t == 0:
                    pe.wait_ge(yn_done, 2)
                    pe.wait_ge(y_sq, 6)

            row_block("wout2", 2, xh, xl, True, False, (1, 0), attention_left)
            pe.wait_ge(y_dg, 6)
            transpose_norm(yn, lambda k, t: dseg[:, t, :], 4, range(4))
            row_block("wout3", 3, xh, xl, False, False)
            pe.wait_ge(t_lo, KD * 7)
            row_block("wout0", 0, xh, xl, False, False)
            row_block("wout1", 1, xh, xl, False, True)
            mem_block(6)
            norm(7, 12, 20)
            mem_block(7)
            pe.wait_ge(t_lo, KD * 8)
            pe.wait_ge(mem_out, 8)

            def x_q(h):
                if h >= 2:
                    pe.wait_ge(q_out, h - 1)
                columns(f"xq{h}", h % 2, xh, xl)

            def x_scores(h):
                pe.wait_ge(q_out, h + 1)
                if h >= 2:
                    pe.wait_ge(a_exp, 2 * h - 2)
                for t in range(NT):
                    for f in range(2):
                        ins = pe.matmul(bank[4 + h % 2][:, t * SEQ:(t + 1) * SEQ], qx[:, 2 * h + f, t * P:(t + 1) * P],
                                        km[:, 2 * h + f, :], start=f == 0, stop=f == 1)
                ins.then_inc(a_mm, 1)

            def x_pt(h):
                pe.wait_ge(a_norm, 2 * h + 2)
                if h >= 1:
                    pe.wait_ge(a_out, h)
                for kt in range(NT):
                    for t in range(NT):
                        ins = pe.transpose(bank[6][:, kt * SEQ + t * P:kt * SEQ + (t + 1) * P],
                                           sx[h % 2][:, t, kt * P:(kt + 1) * P], ident)
                ins.then_inc(a_t, 1)

            def x_pv(h):
                pe.wait_ge(a_out, h + 1)
                if h >= 1:
                    pe.wait_ge(ao_lo, h)
                for f in range(2):
                    for kt in range(NT):
                        c = h * XHD + f * P
                        ins = pe.matmul(bank[7][:, f * SEQ:(f + 1) * SEQ], vm[:, kt, c:c + P], px[h % 2][:, kt, :],
                                        start=kt == 0, stop=kt == NT - 1)
                ins.then_inc(ao_mm, 1)

            x_q(0)
            x_q(1)
            x_scores(0)
            for h in range(XHEADS):
                if h + 2 < XHEADS:
                    x_q(h + 2)
                x_pt(h)
                if h + 1 < XHEADS:
                    x_scores(h + 1)
                else:
                    row_block("xo0", 0, mh, ml, True, False)
                x_pv(h)
            for i in (1, 2):
                row_block(f"xo{i}", i, mh, ml, False, False)
            pe.wait_ge(ao_lo, XHEADS)
            row_block("xo3", 3, mh, ml, False, True)
            norm(8, 14, 24)
            ffn(2, 8)


INPUTS = (
    "x", "positions", "norm_mix", "norm_ffn", "norm_final", "pool_w", "pool_scale", "mla_w_down", "mla_q_norm",
    "mla_w_uq", "mla_kv_norm", "mla_w_ukv", "mla_w_o", "ffn_w_gate", "ffn_w_up", "ffn_w_down", "mem_2",
    "mix_norm_g_2", "w_in_2", "cmp_pe_2", "cmp_w1_2", "cmp_w2_2", "gmlp_ln_g_2", "gmlp_ln_b_2", "gmlp_ws_2",
    "gmlp_bs_2", "conv_dw_w_2", "conv_dw_b_2", "conv_ln_g_2", "conv_ln_b_2", "mix_out_g_2", "w_out_2",
    "xattn_norm_g_2", "mem_norm_g_2", "xattn_wq_2", "xattn_wk_2", "xattn_wv_2", "xattn_wo_2", "ffn_norm_g_2",
    "ffn_w_up_2", "ffn_dw_w_2", "ffn_dw_b_2", "ffn_w_down_2", "final_norm_g_2",
)


def kernel(**inputs):
    import numpy as _np
    import concourse.bacc as _bacc
    from concourse import mybir as _mybir
    from concourse.bass_utils import run_bass_kernel_spmd as _run

    nc = _bacc.Bacc("TRN2", target_bir_lowering=False, num_devices=1)
    arrays, w = {}, {}
    for name in INPUTS:
        a = _np.ascontiguousarray(inputs[name])
        arrays[f"in_{name}"] = a
        w[name] = nc.dram_tensor(f"in_{name}", a.shape, _mybir.dt.from_np(a.dtype), kind="ExternalInput").ap()
    extra = []
    for name, a in zip(("consts", "bands"), constants()):
        arrays[f"in_{name}"] = a
        extra.append(nc.dram_tensor(f"in_{name}", a.shape, _mybir.dt.from_np(a.dtype), kind="ExternalInput").ap())
    out = nc.dram_tensor("out_x", (1, SEQ, D), F32, kind="ExternalOutput").ap()
    build(nc, w, *extra, out)
    r = _run(nc, [arrays], core_ids=[0])
    return r.results[0]["out_x"]
```

```python
from contextlib import ExitStack

import numpy as np

import concourse.bass as bass
from concourse import mybir

F32 = mybir.dt.float32
F32R = mybir.dt.float32r
I32 = mybir.dt.int32
ACT = mybir.ActivationFunctionType
ALU = mybir.AluOpType
AX = mybir.AxisListType

P = 128
SEQ = 256
NT = SEQ // P
D = 1024
KD = D // P
HALF = 512
EPS = 1e-6
ROOT_D = 2.0 ** -5
assert D * ROOT_D ** 2 == 1.0
NEG = -1e30
TINY = 1e-30

POOL_WINDOWS = (2, 4, 8, 16)
NG = len(POOL_WINDOWS)
EDGE = max(POOL_WINDOWS)

HEADS = 8
NOPE = 128
ROPE = 64
QLR = 384
KVR = 128
MLA_DOWN = QLR + KVR + ROPE
VALUE_BANK = (2, 3, 6, 7)
MLA_SCALE = float(NOPE + ROPE) ** -0.5

FF = 2816
STEPS = FF // P
LOOPED = 18

NSA_HEADS = 8
DH = 64
GROUPS = 2
REP = NSA_HEADS // GROUPS
NSA_SCALE = float(DH) ** -0.5
CMP_BLOCK = 32
CMP_STRIDE = 16
NCMP = (SEQ - CMP_BLOCK) // CMP_STRIDE + 1
CMP_KT = CMP_BLOCK * DH // P
GW = 256
GG = 4
CW_ = 256
TAPS = 31
PAD = TAPS - 1
XHEADS = 4
QUERY_BANK = (5, 1, 0, 1)
XHD = D // XHEADS
XSCALE = float(XHD) ** -0.5
GELU_C = 0.044715
GELU_S = float(np.sqrt(2.0 / np.pi))

WOUT_ORDER = (2, 3, 0, 1)
POOL_TAPS = 25
TAPS_BEFORE = 14
TAPS_PER_STEP = 4
VECTOR_TAPS = ([(k, 0) for k in range(POOL_TAPS)]
               + [(k, c) for k in range(POOL_TAPS, TAPS) for c in range(2)])
U_MEM = {6: 3, 7: 9}
MEM_PER_STEP = 3
MEM_STEPS = -(-NT * KD // MEM_PER_STEP)
U_TURN, U_STATS, U_LN, U_SILU, U_SQUARES, U_TURN_Y, U_SPLIT = 7, 8, 9, 10, 11, 13, 14

C_MIX0, C_MIX1, C_FFN = 0, 8, 16
C_QN, C_KVN = 32, 35
C_MIXN, C_MOUT, C_XN, C_MEMN, C_FN2 = 36, 44, 52, 60, 68
C_CDB = 76
C_CDW = 78
C_PE = C_CDW + 2 * TAPS
C_DW = C_PE + 2 * CMP_KT
NF2 = 2 * FF // P
NCOLS = C_DW + 4 * NF2
EARLY = C_CDW
EARLY_ROWS, LATE_ROWS = 10, 5

K_ID = 0
K_MASK = K_ID + P
K_CB = K_MASK + 3 * P
K_C01 = K_CB + NT * NCMP
K_INV = K_C01 + NT * NCMP
K_SEL = K_INV + ROPE // 2
NCONST = K_SEL + GW
NPOOL = NG * P + NG * EDGE + NG * P


def constants():
    c = np.zeros((P, NCONST), np.float32)
    c[:, K_ID:K_ID + P] = np.eye(P, dtype=np.float32)
    causal = np.where(np.arange(P)[None, :] <= np.arange(P)[:, None], 0.0, NEG).astype(np.float32)
    c[:, K_MASK:K_MASK + P] = causal
    c[:, K_MASK + 2 * P:K_MASK + 3 * P] = causal
    t = np.arange(SEQ).reshape(NT, P)
    end = np.arange(NCMP) * CMP_STRIDE + CMP_BLOCK - 1
    ok = (end[None, None, :] <= t[:, :, None]).transpose(1, 0, 2).reshape(P, NT * NCMP)
    c[:, K_CB:K_CB + NT * NCMP] = np.where(ok, 0.0, NEG)
    c[:, K_C01:K_C01 + NT * NCMP] = ok
    theta = np.float32(10000.0)
    power = np.arange(0, ROPE, 2, dtype=np.float32) / np.float32(ROPE)
    c[:, K_INV:K_INV + ROPE // 2] = (np.float32(1.0) / (theta ** power).astype(np.float32))[None, :]
    for g in range(GG):
        c[g, K_SEL + g * GW // GG:K_SEL + (g + 1) * GW // GG] = 1.0
    bands = np.zeros((P, NPOOL), np.float32)
    full = np.zeros((NG, SEQ, SEQ), np.float64)
    for g, win in enumerate(POOL_WINDOWS):
        for tok in range(SEQ):
            lo = max(0, tok - win + 1)
            full[g, lo:tok + 1, tok] = 1.0 / min(tok + 1, win)
            full[g, tok, tok] -= 1.0
    a, b = NG * P, NG * P + NG * EDGE
    bands[:, :a] = full[:, :P, :P].transpose(1, 0, 2).reshape(P, -1)
    bands[:, a:b] = full[:, :P, P:P + EDGE].transpose(1, 0, 2).reshape(P, -1)
    bands[:, b:] = full[:, P:, P:].transpose(1, 0, 2).reshape(P, -1)
    return c, bands


def weight_blocks(w):
    out = []

    def view(k, c):
        return lambda slot: slot[:, 0:k * c].rearrange("p (k c) -> p k c", k=k)

    def rows(src):
        return src.rearrange("(k p) n -> p k n", p=P)

    def halves(name, src, k, c):
        v = view(k, c)
        h = (k + 1) // 2
        out.append((name, k * c, [(v, (slice(0, h), slice(0, c)), src[:, 0:h, :]),
                                  (v, (slice(h, k), slice(0, c)), src[:, h:k, :])]))

    def cols(name, src, a, c):
        halves(name, rows(src)[:, :, a:a + c], KD, c)

    def pair(name, src, a, b):
        v = view(KD, 2 * P)
        out.append((name, KD * 2 * P, [(v, (slice(0, KD), slice(0, P)), rows(src)[:, :, a:a + P]),
                                       (v, (slice(0, KD), slice(P, 2 * P)), rows(src)[:, :, b:b + P])]))

    def rowpair(name, src, i):
        halves(name, rows(src)[:, 2 * i:2 * i + 2, :], 2, D)

    def mem(i):
        cols(f"mem{i}", w["xattn_wk_2"][0] if i < 4 else w["xattn_wv_2"][0], (i % 4) * 2 * P, 2 * P)

    def ffn(layer):
        for j in range(STEPS):
            out.append((f"ffn{layer}", KD * 2 * P, None))

    halves("pool", w["pool_w"][0].rearrange("g (c p) d -> p (g c) d", p=P), 2 * NG, 256)
    mem(0)
    ffn(0)
    mem(1)
    for b in range(3):
        cols(f"down{b}", w["mla_w_down"][0], b * MLA_DOWN // 3, MLA_DOWN // 3)
    mem(2)
    hw = NOPE + ROPE
    for b, n in enumerate((3, 3, 2)):
        halves(f"uq{b}", rows(w["mla_w_uq"][0])[:, :, 3 * b * hw:(3 * b + n) * hw], 3, n * hw)
    halves("ukv", w["mla_w_ukv"][0].rearrange("p (k c) -> p k c", k=2), 2, D)
    for i in range(4):
        rowpair(f"wo{i}", w["mla_w_o"][0], i)
    mem(3)
    ffn(1)
    mem(4)
    mem(5)
    win = w["w_in_2"][0]
    z = NSA_HEADS * DH
    zg = z + 6 * P + 24
    zc = zg + 2 * GW
    cols("z_a", win, zc, CW_)
    cols("z_gt", win, zc + CW_, CW_)
    cols("z_v", win, zg + GW, GW)
    cols("z_u", win, zg, GW)
    cols("z_kcvc", win, z, 2 * P)
    pair("z_q0", win, 0, REP * DH)
    pair("z_q1", win, P, REP * DH + P)
    pair("z_ksw", win, z + 2 * P, z + 4 * P)
    pair("z_vsw", win, z + 3 * P, z + 5 * P)
    cols("z_gl", win, z + 6 * P, 24)
    mem(6)
    mem(7)
    for i in WOUT_ORDER:
        rowpair(f"wout{i}", w["w_out_2"][0], i)
    for i in range(4):
        cols(f"xq{i}", w["xattn_wq_2"][0], i * XHD, XHD)
    for i in range(4):
        rowpair(f"xo{i}", w["xattn_wo_2"][0], i)
    ffn(2)
    return out


def build(nc, w, consts, bands, out):
    blocks = weight_blocks(w)
    names = [b[0] for b in blocks]
    at = {name: names.index(name) for name in names}
    used_cols = [b[1] for b in blocks]
    NB = len(blocks)
    x_dram = w["x"].rearrange("b (t p) d -> p (b t) d", p=P)
    mem_dram = w["mem_2"].rearrange("b (t p) d -> p (b t) d", p=P)
    out_dram = out.rearrange("b (t p) d -> p (b t) d", p=P)

    def gate_up(layer):
        if layer < 2:
            return (w["ffn_w_gate"][layer], w["ffn_w_up"][layer])
        return (w["ffn_w_up_2"][0][:, 0:FF], w["ffn_w_up_2"][0][:, FF:2 * FF])

    def down_rows(layer):
        return w["ffn_w_down"][layer] if layer < 2 else w["ffn_w_down_2"][0]

    with ExitStack() as ctx:
        def sb(name, shape, dt=F32):
            return ctx.enter_context(nc.sbuf_tensor(name, shape, dt))

        def sem(name):
            return ctx.enter_context(nc.semaphore(name))

        raw = [sb(f"raw{s}", [P, 2048]) for s in range(3)]
        wh = [sb(f"wh{s}", [P, 2048], F32R) for s in range(3)]
        wl = [sb(f"wl{s}", [P, 2048], F32R) for s in range(3)]
        xt = sb("x_tok", [P, NT, D])
        xh = sb("xh", [P, KD, SEQ], F32R)
        xl = sb("xl", [P, KD, SEQ], F32R)
        mh = sb("mh", [P, KD, SEQ], F32R)
        ml = sb("ml", [P, KD, SEQ], F32R)
        km = sb("k_mem", [P, KD, SEQ])
        vm = sb("v_mem", [P, NT, D])
        hh = [sb(f"hh{s}", [P, SEQ], F32R) for s in range(3)]
        hl = [sb(f"hl{s}", [P, SEQ], F32R) for s in range(3)]
        zero = sb("zero", [P, P], F32R)
        con = sb("con", [P, NCONST])
        col = sb("col", [P, NCOLS])
        gain = sb("gain", [P, D])
        junk = sb("junk", [P, HALF])
        tapped = sb("tapped", [P, SEQ])
        ss = sb("ss", [P, 16, NT, 2])
        st1 = sb("st1", [P, 16, NT])
        st2 = sb("st2", [P, 16, NT])
        rstd = sb("rstd", [P, 16, NT])
        mhalf = sb("mhalf", [P, 16])
        cs = sb("cs", [P, NT, ROPE])
        sn = sb("sn", [P, NT, ROPE])
        base = nc.sbuf_base
        REGION = 61312
        ctx.enter_context(nc.sbuf_tensor("region", [P, REGION // 4], F32))
        base = (base + 31) // 32 * 32
        cursor = [0]

        def at_(name, shape, dt=F32, off=None):
            if off is not None:
                cursor[0] = off
            n = 4
            for d in shape[1:]:
                n *= d
            t = nc.alloc_sbuf_tensor_at(name, shape, dt, offset=base + cursor[0])
            cursor[0] += (n + 31) // 32 * 32
            assert cursor[0] <= REGION - 32, (name, cursor[0])
            return t

        memt = at_("mem_tok", [P, NT, D], off=0)
        band = at_("band", [P, NPOOL])
        bandr = at_("bandr", [P, NPOOL])
        pscale = at_("pscale", [P, D])
        prow = [at_(f"prow{i}", [P, P]) for i in range(4)]
        posi = at_("posi", [P, NT], I32)
        posf = at_("posf", [P, NT])
        ang = at_("ang", [P, NT, ROPE // 2])
        kk = at_("kk", [P, NT, ROPE // 2])
        r0 = at_("r0", [P, NT, ROPE // 2])
        r1 = at_("r1", [P, NT, ROPE // 2])
        draw = [at_(f"draw{s}", [P, D], off=(0 if s == 0 else None)) for s in range(3)]
        dh = [at_(f"dh{s}", [P, D], F32R) for s in range(3)]
        dl = [at_(f"dl{s}", [P, D], F32R) for s in range(3)]
        th = [at_(f"th{s}", [P, SEQ]) for s in range(3)]
        pr = [at_(f"pr{s}", [P, SEQ]) for s in range(3)]
        ga = at_("ga", [P, SEQ])
        cg = [at_(f"cg{s}", [P, SEQ]) for s in range(3)]
        cu = [at_(f"cu{s}", [P, SEQ]) for s in range(3)]
        XN = 9 * D * 4
        xn = at_("xn", [P, NT, D], off=XN)
        ds = at_("ds", [P, NT, MLA_DOWN], off=0)
        qn = at_("qn", [P, HEADS, SEQ])
        qr = at_("qr", [P, NT, HEADS * ROPE])
        qrt = at_("qrt", [P, HEADS // 2, SEQ])
        kn = at_("kn", [P, HEADS, SEQ])
        vv = at_("vv", [P, NT, HEADS * P])
        kr = at_("kr", [P, NT, P])
        krt = at_("krt", [P, SEQ])
        ra = at_("ra", [P, HEADS * ROPE])
        rb = at_("rb", [P, HEADS * ROPE])
        sc = [at_(f"sc{s}", [P, 3 * P]) for s in range(2)]
        pt = [at_(f"pt{s}", [P, 3 * P]) for s in range(2)]
        stat = at_("stat", [P, HEADS, 4, NT])
        mst = at_("mst", [P, 4, 2, NT])
        qt = at_("qt", [P, REP, SEQ], off=0)
        ksw = at_("ksw", [P, 2, SEQ])
        kvc = at_("kvc", [P, 2, SEQ])
        vsw = at_("vsw", [P, NT, 2 * P])
        x4 = at_("x4", [P, 2, GROUPS, SEQ])
        fl = at_("fl", [P, 2, CMP_KT, GROUPS, NCMP])
        cw1 = at_("cw1", [P, 2, CMP_KT, DH])
        cw2 = at_("cw2", [DH, 2, DH])
        hg = at_("hg", [DH, 4, 2 * GROUPS * NCMP])
        kcm = at_("kcm", [P, NCMP])
        vcs = at_("vcs", [NCMP, GROUPS, DH])
        vbd = at_("vbd", [P, NSA_HEADS * DH])
        hc = at_("hc", [P, 2, PAD + SEQ])
        yc = at_("yc", [P, 2, SEQ])
        gate = at_("gate", [P, NT, 24])
        glf = at_("glf", [24, SEQ])
        p2_0 = at_("p2_0", [P, 3 * P])
        yn = at_("yn", [P, NT, D], off=XN)
        e1 = at_("e1", [P, HALF])
        e2 = at_("e2", [P, HALF])
        e3 = at_("e3", [P, HALF])
        wst = at_("wst", [P, GG, P])
        bsr = at_("bsr", [GG, P])
        lng = at_("lng", [P, 2, 2, GW])
        s2 = [kvc[:, :, :].rearrange("p a s -> p (a s)")[:, 0:3 * P],
              fl[:, :, :, :, :].rearrange("p a k g n -> p (a k g n)")[:, GG * P:GG * P + 3 * P]]
        p2 = [p2_0, at_("p2_1", [P, 3 * P])]
        nst = at_("nst", [P, 4, 2 * NSA_HEADS, NT])
        lst = at_("lst", [P, 64])
        uu, vg = yn[:, :, 3 * GW:4 * GW], yn[:, :, 0:GW]
        ws = fl[:, :, :, :, :].rearrange("p a k g n -> p (a k g n)")[:, 0:GG * P]
        cm = [cw1[:, 0, :, :].rearrange("p k d -> p (k d)")[:, 240 * i:240 * i + 240] for i in range(4)]
        qx = at_("qx", [P, KD, SEQ], off=0)
        sx = [at_(f"sx{s}", [P, NT, SEQ]) for s in range(2)]
        px = [at_(f"px{s}", [P, NT, SEQ]) for s in range(2)]
        xst = at_("xst", [P, XHEADS, 4, NT])

        bank = [ctx.enter_context(nc.psum_tensor(f"bank{i}", [P, HALF], F32)) for i in range(8)]

        raw_full = [sem(f"raw_full{s}") for s in range(3)]
        hi_done, lo_done, block_used = sem("hi_done"), sem("lo_done"), sem("block_used")
        d_full = [sem(f"d_full{s}") for s in range(3)]
        d_hi, d_lo, down_done = sem("d_hi"), sem("d_lo"), sem("down_done")
        tanh_done, gated, prod_done = sem("tanh_done"), sem("gated"), sem("prod_done")
        h_hi, h_ready = sem("h_hi"), sem("h_ready")
        conv_in, conv_tap = sem("conv_in"), sem("conv_tap")
        x_loaded, con_loaded, band_loaded = sem("x_loaded"), sem("con_loaded"), sem("band_loaded")
        mem_loaded, rows_loaded, pscale_loaded = sem("mem_loaded"), sem("rows_loaded"), sem("pscale_loaded")
        late_rows_loaded = sem("late_rows_loaded")
        gain_loaded, pos_loaded = sem("gain_loaded"), sem("pos_loaded")
        last_gain_loaded = sem("last_gain_loaded")
        zero_set = sem("zero_set")
        tapped_done = sem("tapped_done")
        cols_t, cols_done, taps_halved = sem("cols_t"), sem("cols_done"), sem("taps_halved")
        pool_scaled = sem("pool_scaled")
        sq_done, rstd_done = sem("sq_done"), sem("rstd_done")
        res_done, xn_done = sem("res_done"), sem("xn_done")
        t_done, t_hi, t_lo = sem("t_done"), sem("t_hi"), sem("t_lo")
        bank_sum = sem("bank_sum")
        gained = sem("gained")
        mem_out = sem("mem_out")
        region_free = sem("region_free")
        scaled = sem("scaled")
        rope_a, rope_s = sem("rope_a"), sem("rope_s")
        ds_out, mla_sq, mla_rs, mla_scaled = sem("ds_out"), sem("mla_sq"), sem("mla_rs"), sem("mla_scaled")
        cq_t, cq_hi, cq_lo = sem("cq_t"), sem("cq_hi"), sem("cq_lo")
        kr_done, kr_t, kr_out = sem("kr_done"), sem("kr_t"), sem("kr_out")
        qk_mm, qk_out = sem("qk_mm"), sem("qk_out")
        v_mm, v_out = sem("v_mm"), sem("v_out")
        qr_done, qr_t, qr_out = sem("qr_done"), sem("qr_t"), sem("qr_out")
        s_mm, s_max, s_exp, s_norm = sem("s_mm"), sem("s_max"), sem("s_exp"), sem("s_norm")
        p_t, p_out, o_mm, o_hi, o_lo = sem("p_t"), sem("p_out"), sem("o_mm"), sem("o_hi"), sem("o_lo")
        z_out = sem("z_out")
        z_params = sem("z_params")
        z_ws, ws_loaded, ws_cut = sem("z_ws"), sem("ws_loaded"), sem("ws_cut")
        hc_done, cv_tap, cv_tap_pool = sem("hc_done"), sem("cv_tap"), sem("cv_tap_pool")
        shifted, fl_done, cmp_mm, cmp_a, cmp_d, cmp_out = (sem("shifted"), sem("fl_done"), sem("cmp_mm"),
                                                         sem("cmp_a"), sem("cmp_d"), sem("cmp_out"))
        vbd_zero, vbd_set = sem("vbd_zero"), sem("vbd_set")
        gl_a, gl_t, gl_done = sem("gl_a"), sem("gl_t"), sem("gl_done")
        gz_a, gz_d = sem("gz_a"), sem("gz_d")
        ws_t, ws_out, ln_rs, vn_done, mix_mm, gy_done = (sem("ws_t"), sem("ws_out"), sem("ln_rs"),
                                                        sem("vn_done"), sem("mix_mm"), sem("gy_done"))
        ycs_t, cvln_done, cv_a, cy_done = sem("ycs_t"), sem("cvln_done"), sem("cv_a"), sem("cy_done")
        sc_mm, cm_e, pc_done, pc_t, pc_out = (sem("sc_mm"), sem("cm_e"), sem("pc_done"), sem("pc_t"),
                                             sem("pc_out"))
        n_rec = sem("n_rec")
        n_mm, n_max, n_exp, n_norm, n_t, n_out = (sem("n_mm"), sem("n_max"), sem("n_exp"), sem("n_norm"),
                                                  sem("n_t"), sem("n_out"))
        o_all, y_sq, y_rs, y_scaled = sem("o_all"), sem("y_sq"), sem("y_rs"), sem("y_scaled")
        q_out = sem("q_out")
        a_mm, a_max, a_exp, a_norm, a_t, a_out, ao_mm, ao_hi, ao_lo = (
            sem("a_mm"), sem("a_max"), sem("a_exp"), sem("a_norm"), sem("a_t"), sem("a_out"),
            sem("ao_mm"), sem("ao_hi"), sem("ao_lo"))
        dve_order, pool_order = sem("dve_order"), sem("pool_order")
        stored = sem("stored")

        ident = con[:, K_ID:K_ID + P]
        mask = con[:, K_MASK:K_MASK + 3 * P]

        def split_views(n, *slots):
            if names[n] not in ("z_q0", "z_q1"):
                return [[t[:, 0:used_cols[n]] for t in slots]]
            by_head = [t[:, :].rearrange("p (k j g d) -> p k j g d", k=KD, j=2, g=GROUPS) for t in slots[1:]]
            by_group = slots[0][:, :].rearrange("p (k g j d) -> p k g j d", k=KD, j=2, g=GROUPS)
            return [[by_group[:, :, g, :, :]] + [v[:, :, :, g, :] for v in by_head] for g in range(GROUPS)]

        def k_view(t, k, c):
            return t[:, 0:k * c].rearrange("p (k c) -> p k c", k=k)

        block = ctx.enter_context(nc.Block())

        @block.sync
        def _(sp):
            def load(n):
                _, _, parts = blocks[n]
                if n >= 3:
                    sp.wait_ge(hi_done, n - 2)
                    sp.wait_ge(lo_done, n - 2)
                for v, (ks, cs_), src in parts:
                    sp.dma_start(v(raw[n % 3])[:, ks, cs_], src).then_inc(raw_full[n % 3], 32 // len(parts))

            def ffn(layer):
                n0, m0 = at[f"ffn{layer}"], STEPS * layer
                gu = gate_up(layer)
                dn = down_rows(layer)

                def load_gu(s, j, n):
                    slot = raw[s][:, :].rearrange("p (k h c) -> p k h c", k=KD, h=2)
                    sp.wait_ge(hi_done, n - 2)
                    sp.wait_ge(lo_done, n - 2)
                    for half in range(2):
                        src = gu[half].rearrange("(k p) n -> p k n", p=P)[:, :, bass.ds(j * P, P)]
                        sp.dma_start(slot[:, :, half, :], src).then_inc(raw_full[s], 16)

                def load_d(s, j, m):
                    if not isinstance(m, int) or m >= 3:
                        sp.wait_ge(d_lo, m - 2)
                    sp.dma_start(draw[s][:, :], dn[bass.ds(j * P, P), :]).then_inc(d_full[s], 16)

                for j in range(3):
                    load_gu((n0 + j) % 3, j, n0 + j)
                sp.wait_ge(region_free, layer + 1)
                for j in range(3):
                    load_d((m0 + j) % 3, j, m0 + j)
                with sp.Fori(0, LOOPED // 3) as i:
                    for s in range(3, 6):
                        load_gu((n0 + s) % 3, 3 * i + s, 3 * i + n0 + s)
                        load_d((m0 + s) % 3, 3 * i + s, 3 * i + m0 + s)
                for j in range(LOOPED + 3, STEPS):
                    load_gu((n0 + j) % 3, j, n0 + j)
                    load_d((m0 + j) % 3, j, m0 + j)

            for t in range(NT):
                sp.dma_start(xt[:, t, :], x_dram[:, t, :]).then_inc(x_loaded, 16)
            load(0)
            rows = [(0, 0, w["norm_mix"].rearrange("l (k p) -> (l k) p", p=P)),
                    (0, C_FFN, w["norm_ffn"].rearrange("l (k p) -> (l k) p", p=P)),
                    (0, C_QN, w["mla_q_norm"].rearrange("l (k p) -> (l k) p", p=P)),
                    (0, C_KVN, w["mla_kv_norm"].rearrange("l (k p) -> (l k) p", p=P)),
                    (0, C_MIXN, w["mix_norm_g_2"].rearrange("l (k p) -> (l k) p", p=P)),
                    (0, C_MOUT, w["mix_out_g_2"].rearrange("l (k p) -> (l k) p", p=P)),
                    (0, C_XN, w["xattn_norm_g_2"].rearrange("l (k p) -> (l k) p", p=P)),
                    (0, C_MEMN, w["mem_norm_g_2"].rearrange("l (k p) -> (l k) p", p=P)),
                    (0, C_FN2, w["ffn_norm_g_2"].rearrange("l (k p) -> (l k) p", p=P)),
                    (0, C_CDB, w["conv_dw_b_2"].rearrange("l (k p) -> (l k) p", p=P)),
                    (1, 0, w["conv_dw_w_2"][0].rearrange("t (a p) -> (t a) p", p=P)),
                    (1, 2 * TAPS, w["cmp_pe_2"][0].rearrange("a (k e) d -> (a k) (e d)", e=2)),
                    (2, 0, w["ffn_dw_w_2"][0, 0:2, :].rearrange("t (j p) -> (t j) p", p=P)),
                    (3, 0, w["ffn_dw_w_2"][0, 2:3, :].rearrange("t (j p) -> (t j) p", p=P)),
                    (3, NF2, w["ffn_dw_b_2"].rearrange("t (j p) -> (t j) p", p=P))]

            def load_rows(part, signal):
                for i, r, src in part:
                    sp.dma_start(prow[i][r:r + src.shape[0], :], src).then_inc(signal, 16)

            load_rows(rows[:EARLY_ROWS], rows_loaded)
            sp.dma_start(memt[:, :, :], mem_dram).then_inc(mem_loaded, 16)
            load_rows(rows[EARLY_ROWS:], late_rows_loaded)
            n = 1
            while n < NB:
                if names[n].startswith("ffn"):
                    ffn(int(names[n][3:]))
                    n += STEPS
                else:
                    load(n)
                    n += 1
            for t in range(NT):
                for c in range(2):
                    cs_ = slice(c * HALF, (c + 1) * HALF)
                    sp.wait_ge(scaled, NT + 2 * t + c + 1)
                    sp.dma_start(out_dram[:, t, cs_], xn[:, t, cs_]).then_inc(stored, 16)
            sp.wait_ge(stored, 16 * 2 * NT)

        @block.scalar
        def _(act):
            junk_writer = [None]

            def junk_for(signal, count, width):
                if junk_writer[0] is not None:
                    act.wait_ge(*junk_writer[0])
                junk_writer[0] = (signal, count)
                return junk[:, 0:width]

            def hi(n):
                if n >= NB:
                    return
                act.wait_ge(raw_full[n % 3], 32 * (n // 3 + 1))
                if n >= 3:
                    act.wait_ge(block_used, n - 2)
                if n == 0:
                    act.wait_ge(pool_scaled, 3)
                for r, h in split_views(n, raw[n % 3], wh[n % 3]):
                    ins = act.activation(h, r, ACT.Copy)
                ins.then_inc(hi_done, 1)

            def squares(q, src, ready, first):
                for t in range(NT):
                    for c in range(2):
                        if ready is not None:
                            act.wait_ge(ready, first + 2 * t + c)
                        act.activation(junk_for(sq_done, 4 * q + 2 * t + c + 1, HALF),
                                       src[:, t, c * HALF:(c + 1) * HALF], ACT.Square, scale=ROOT_D,
                                       accum_out=ss[:, q, t, c:c + 1]).then_inc(sq_done, 1)

            def split_t(e, dst, c0, banks, ks=range(KD), done=0):
                for i, k in enumerate(ks):
                    if k % 2 == 0:
                        act.wait_ge(t_done, (KD * e + done + i) // 2 + 1)
                    src = bank[banks + k // 2][:, (k % 2) * SEQ:(k % 2 + 1) * SEQ]
                    act.activation(dst[:, k, :], src, ACT.Copy, scale=col[:, c0 + k:c0 + k + 1]) \
                       .then_inc(t_hi, 1)

            def mem_block(i):
                n = at[f"mem{i}"]
                act.wait_ge(block_used, n + 1)
                src = bank[7][:, :].rearrange("p (a s) -> p a s", a=2)
                if i < 4:
                    dst = km[:, 2 * i:2 * i + 2, :]
                else:
                    dst = vm[:, :, (i - 4) * 256:(i - 3) * 256]
                act.activation(dst, src, ACT.Copy).then_inc(mem_out, 1)

            def after(name):
                hi(at[name] + 3)

            def ffn(layer, before):
                n0, m0 = at[f"ffn{layer}"], STEPS * layer

                def dhi(s, m, q):
                    act.wait_ge(d_full[s], q)
                    act.wait_ge(down_done, m + 1)
                    act.activation(dh[s][:, :], draw[s][:, :], ACT.Copy).then_inc(d_hi, 1)

                def step(j, i, jj):
                    s = (m0 + jj) % 3
                    n, m = n0 + j, m0 + j
                    act.wait_ge(block_used, n + 1)
                    b = bank[4 + s]
                    if layer < 2:
                        act.activation(th[s][:, :], b[:, 0:SEQ], ACT.Tanh, scale=0.5).then_inc(tanh_done, 1)
                    else:
                        for half, dst in ((0, cg[s]), (1, cu[s])):
                            c2 = C_DW + 2 * NF2 + half * STEPS
                            cb = C_DW + 3 * NF2 + half * STEPS
                            act.activation(dst[:, :], b[:, half * SEQ:(half + 1) * SEQ], ACT.Identity,
                                           scale=col[:, bass.ds(j + c2, 1)],
                                           bias=col[:, bass.ds(j + cb, 1)]).then_inc(conv_in, 1)

                    def next_weights():
                        if i is not None or jj + 3 < STEPS:
                            ns = (n0 + jj) % 3
                            act.wait_ge(raw_full[ns], 32 * ((n0 + jj) // 3 + 2) + (0 if i is None else 32 * i))
                            act.activation(wh[ns][:, :], raw[ns][:, :], ACT.Copy).then_inc(hi_done, 1)
                        else:
                            hi(n0 + jj + 3)

                    if jj > 0:
                        next_weights()
                    if layer == 2:
                        act.wait_ge(conv_tap, 4 * (j + 1) - 2)
                        act.activation(th[s][:, :], cg[s][:, :], ACT.Tanh, scale=0.5).then_inc(tanh_done, 1)
                    act.wait_ge(prod_done, m + 4)
                    act.wait_ge(down_done, m + 1)
                    act.activation(hh[s][:, :], pr[s][:, :], ACT.Copy).then_inc(h_hi, 1)
                    if jj == 0:
                        after(before)
                        dhi((m0 + 1) % 3, m0 + 1, 16 * ((m0 + 1) // 3 + 1))
                        next_weights()
                    if i is not None or jj + 2 < STEPS:
                        s2_ = (m0 + jj + 2) % 3
                        q = 16 * ((m0 + jj + 2) // 3 + 1) + (0 if i is None else 16 * i)
                        dhi(s2_, m + 2, q)

                dhi(m0 % 3, m0, 16 * (m0 // 3 + 1))
                step(0, None, 0)
                with act.Fori(0, LOOPED // 3) as i:
                    for s in range(1, 4):
                        step(3 * i + s, i, s)
                for j in range(LOOPED + 1, STEPS):
                    step(j, None, j)

            act.dma_start(con[:, :], consts).then_inc(con_loaded, 16)
            act.dma_start(posi[:, :], w["positions"].rearrange("a (t p) -> p (a t)", p=P),
                          allow_slow_non_contiguous=True).then_inc(pos_loaded, 16)
            act.dma_start(band[:, :], bands).then_inc(band_loaded, 16)
            act.dma_start(pscale[:, :], w["pool_scale"][0:1, :].to_broadcast([P, D])).then_inc(pscale_loaded, 16)
            act.dma_start(gain[:, :], w["norm_final"].rearrange("(a d) -> a d", a=1).to_broadcast([P, D])) \
               .then_inc(gain_loaded, 16)
            act.wait_ge(x_loaded, 16 * NT)
            squares(0, xt, None, 0)
            act.wait_ge(rope_a, 1)
            act.activation(sn[:, :, 32:64], r0[:, :, :], ACT.Sin).then_inc(rope_s, 1)
            act.activation(cs[:, :, 0:32], r1[:, :, :], ACT.Sin).then_inc(rope_s, 1)
            hi(0)
            act.wait_ge(cols_t, 1)
            act.activation(col[:, 0:EARLY], bank[7][:, 0:EARLY], ACT.Copy).then_inc(cols_done, 1)
            act.wait_ge(cols_done, 1)
            act.wait_ge(mem_loaded, 16)
            squares(1, memt, None, 0)
            split_t(0, xh, C_MIX0, 0)
            hi(1)
            split_t(1, mh, C_MEMN, 4)
            hi(2)
            squares(2, xt, res_done, 1)
            hi(3)
            act.wait_ge(cols_t, 2)
            act.activation(col[:, EARLY:NCOLS], bank[6][:, 0:NCOLS - EARLY], ACT.Copy).then_inc(cols_done, 1)
            mem_block(0)
            split_t(2, xh, C_FFN, 0)
            ffn(0, "mem0")
            squares(3, xt, res_done, 5)
            mem_block(1)
            split_t(3, xh, C_MIX1, 0)
            after("mem1")
            after("down0")
            act.wait_ge(block_used, at["down1"] + 1)
            for t in range(NT):
                act.activation(ds[:, t, 0:QLR], bank[4 + t][:, 0:QLR], ACT.Copy).then_inc(ds_out, 1)
            act.wait_ge(ds_out, 2)
            for t in range(NT):
                act.activation(junk_for(mla_sq, t + 1, QLR), ds[:, t, 0:QLR], ACT.Square,
                               accum_out=mst[:, 0, 0, t:t + 1]).then_inc(mla_sq, 1)
            after("down1")
            act.wait_ge(block_used, at["down2"] + 1)
            for t in range(NT):
                act.activation(ds[:, t, QLR:MLA_DOWN], bank[2 + t][:, 0:KVR + ROPE], ACT.Copy).then_inc(ds_out, 1)
            act.wait_ge(ds_out, 4)
            for t in range(NT):
                act.activation(junk_for(mla_sq, t + 3, KVR), ds[:, t, QLR:QLR + KVR], ACT.Square,
                               accum_out=mst[:, 0, 1, t:t + 1]).then_inc(mla_sq, 1)
            after("down2")
            for f in range(4):
                act.wait_ge(cq_t, f // 2 + 1)
                act.activation(xh[:, f, :], bank[4 + f // 2][:, (f % 2) * SEQ:(f % 2 + 1) * SEQ], ACT.Copy,
                               scale=col[:, C_QN + f:C_QN + f + 1]).then_inc(cq_hi, 1)
            mem_block(2)
            after("mem2")

            def heads_out(dst, i, first):
                act.wait_ge(qk_mm, first + i + 1)
                act.activation(dst[:, 2 * i:2 * i + 2, :].rearrange("p a s -> p (a s)"), bank[4 + i % 2][:, :],
                               ACT.Copy).then_inc(qk_out, 1)

            heads_out(qn, 0, 0)
            act.wait_ge(kr_t, 1)
            act.activation(krt[:, :], bank[6][:, 0:SEQ], ACT.Copy).then_inc(kr_out, 1)
            after("uq0")
            heads_out(qn, 1, 0)
            heads_out(qn, 2, 0)
            after("uq1")
            heads_out(qn, 3, 0)
            for i in range(4):
                heads_out(kn, i, 4)
            for i in range(2):
                act.wait_ge(v_mm, i + 1)
                act.activation(vv[:, 0, i * HALF:(i + 1) * HALF], bank[VALUE_BANK[i]][:, :], ACT.Copy).then_inc(v_out, 1)
            for i in range(2):
                act.wait_ge(qr_t, i + 1)
                act.activation(qrt[:, 2 * i:2 * i + 2, :].rearrange("p a s -> p (a s)"), bank[i][:, :], ACT.Copy) \
                   .then_inc(qr_out, 1)

            def mla_exp(h):
                act.wait_ge(s_max, h + 1)
                for t, (a, b) in enumerate(((0, P), (P, 3 * P))):
                    act.activation(sc[h % 2][:, a:b], sc[h % 2][:, a:b], ACT.Exp,
                                   bias=stat[:, h, 1, t:t + 1], accum_out=stat[:, h, 2, t:t + 1]) \
                       .then_inc(s_exp, 1)

            def mla_pt(h):
                act.wait_ge(p_t, h + 1)
                if h >= 2:
                    act.wait_ge(o_mm, h - 1)
                act.activation(pt[h % 2][:, :], bank[6][:, 0:3 * P], ACT.Copy).then_inc(p_out, 1)

            def mla_o(h):
                act.wait_ge(o_mm, h + 1)
                act.activation(xh[:, h, :], bank[7][:, (h % 2) * SEQ:(h % 2 + 1) * SEQ], ACT.Copy).then_inc(o_hi, 1)

            mla_exp(0)
            mla_exp(1)
            for h in range(HEADS):
                mla_pt(h)
                if h + 2 < HEADS:
                    mla_exp(h + 2)
                mla_o(h)
                if h in (2, 4, 6):
                    after(("uq2", "ukv", "wo0")[h // 2 - 1])
            after("wo1")
            after("wo2")
            squares(4, xt, res_done, 9)
            mem_block(3)
            split_t(4, xh, C_FFN + 8, 0)
            after("wo3")
            ffn(1, "mem3")
            squares(5, xt, res_done, 13)
            squares(6, xt, gained, 1)
            mem_block(4)
            after("mem4")
            split_t(5, xh, C_MIXN, 0)
            mem_block(5)
            after("mem5")
            act.wait_ge(block_used, at["z_gt"] + 1)
            act.activation(e1[:, :], bank[1][:, :], ACT.Tanh, scale=0.5).then_inc(z_out, 1)
            hi(at["z_a"] + 3)
            after("z_gt")
            for i, name in enumerate(("z_v", "z_u")):
                act.wait_ge(block_used, at[name] + 1)
                b = bank[2 + i]
                act.wait_ge(*((hc_done, 1) if i == 0 else (gz_d, 3)))
                act.activation(e1[:, :], b[:, :], ACT.Square).then_inc(gz_a, 1)
                act.wait_ge(gz_d, 3 * i + 2)
                act.activation(e1[:, :], e2[:, :], ACT.Tanh, scale=GELU_S).then_inc(gz_a, 1)
                after(name)
            act.wait_ge(block_used, at["z_kcvc"] + 1)
            act.activation(kvc[:, :, :].rearrange("p a s -> p (a s)"), bank[0][:, :], ACT.Copy).then_inc(z_out, 1)
            act.wait_ge(z_out, 2)
            for g in range(GROUPS):
                act.dma_start(x4[0:DH, :, g, :], kvc[g * DH:(g + 1) * DH, :, :]).then_inc(shifted, 16)
                act.dma_start(x4[DH:P, :, g, 0:SEQ - 1], kvc[g * DH:(g + 1) * DH, :, 1:SEQ]).then_inc(shifted, 16)
            after("z_kcvc")
            for i in range(2):
                act.wait_ge(block_used, at[f"z_q{i}"] + 1)
                act.activation(qt[:, 2 * i:2 * i + 2, :].rearrange("p a s -> p (a s)"), bank[1 + i][:, :],
                               ACT.Copy).then_inc(z_out, 1)
                after(f"z_q{i}")
            act.wait_ge(cmp_mm, 1)
            hs = bank[7][0:DH, 0:60]
            act.activation(hg[:, 0, :], hs, ACT.Square).then_inc(cmp_a, 1)
            act.wait_ge(cmp_d, 2)
            act.activation(hg[:, 1, :], hg[:, 2, :], ACT.Tanh, scale=GELU_S).then_inc(cmp_a, 1)
            act.wait_ge(block_used, at["z_ksw"] + 1)
            act.activation(ksw[:, :, :].rearrange("p a s -> p (a s)"), bank[3][:, :], ACT.Copy).then_inc(z_out, 1)
            after("z_ksw")
            act.wait_ge(cmp_mm, 2)
            act.activation(kcm[:, :], bank[7][:, 64:64 + NCMP], ACT.Copy, scale=0.5).then_inc(cmp_out, 1)
            act.activation(vcs[:, :, :], bank[7][0:NCMP, 128:256].rearrange("n (g d) -> n g d", g=GROUPS), ACT.Copy,
                           scale=0.5).then_inc(cmp_out, 1)
            act.wait_ge(cmp_out, 2)
            act.wait_ge(vbd_zero, 1)
            for h in range(NSA_HEADS):
                act.dma_start(vbd[h * NCMP:(h + 1) * NCMP, h * DH:(h + 1) * DH], vcs[:, h // REP, :]) \
                   .then_inc(vbd_set, 16)
            act.wait_ge(block_used, at["z_vsw"] + 1)
            act.activation(vsw[:, :, :].rearrange("p a s -> p (a s)"), bank[6][:, :], ACT.Copy).then_inc(z_out, 1)
            after("z_vsw")
            act.wait_ge(block_used, at["z_gl"] + 1)
            act.activation(glf[:, :], bank[2][0:24, 0:SEQ], ACT.Tanh, scale=0.5).then_inc(gl_a, 1)
            after("z_gl")
            act.wait_ge(cm_e, 1)
            act.activation(cm[1], cm[0], ACT.Exp, scale=NSA_SCALE).then_inc(cm_e, 1)
            act.wait_ge(ws_t, 1)
            act.activation(wst[:, :, :].rearrange("p g t -> p (g t)"), bank[3][:, :], ACT.Copy).then_inc(ws_out, 1)
            act.wait_ge(pc_t, NT)
            act.activation(e1[0:120, 0:SEQ], bank[6][0:120, 0:SEQ], ACT.Copy).then_inc(pc_out, 1)

            def nsa_exp(u):
                act.wait_ge(n_max, u + 1)
                for t, (a, b) in enumerate(((0, P), (P, 3 * P))):
                    act.activation(s2[u % 2][:, a:b], s2[u % 2][:, a:b], ACT.Exp,
                                   bias=nst[:, 1, u, t:t + 1], accum_out=nst[:, 2, u, t:t + 1]) \
                       .then_inc(n_exp, 1)

            def nsa_pt(u):
                act.wait_ge(n_t, u + 1)
                if u >= 2:
                    act.wait_ge(o_all, u - 1)
                act.activation(p2[u % 2][:, :], bank[6][:, 0:3 * P], ACT.Copy).then_inc(n_out, 1)

            def nsa_scale(u):
                act.wait_ge(n_rec, u + 1)
                for t, (a, b) in enumerate(((0, P), (P, 3 * P))):
                    act.activation(s2[u % 2][:, a:b], s2[u % 2][:, a:b], ACT.Copy, scale=nst[:, 3, u, t:t + 1]) \
                       .then_inc(n_norm, 1)

            nsa_exp(0)
            nsa_exp(1)
            nsa_scale(0)
            for u in range(2 * NSA_HEADS):
                for i in (6, 7):
                    if u == U_MEM[i] + MEM_STEPS:
                        mem_block(i)
                nsa_pt(u)
                if u + 1 < 2 * NSA_HEADS:
                    nsa_scale(u + 1)
                if u + 2 < 2 * NSA_HEADS:
                    nsa_exp(u + 2)
                if u == U_SILU:
                    act.wait_ge(cvln_done, 1)
                    act.activation(e1[:, :], e2[:, :], ACT.Tanh, scale=0.5).then_inc(cv_a, 1)
                if u == U_SQUARES:
                    act.wait_ge(gy_done, 2)
                    act.wait_ge(cy_done, 1)
                    for s, (a, b) in ((1, (512, 768)), (2, (768, 1024))):
                        for t in range(NT):
                            act.activation(junk_for(y_sq, 2 * s + t - 1, b - a), yn[:, t, a:b], ACT.Square,
                                           accum_out=lst[:, 32 + 2 * s + t:33 + 2 * s + t]).then_inc(y_sq, 1)
                if u == U_SPLIT:
                    split_t(6, xh, C_MOUT, 0, range(4, KD))
                for i in (6, 7):
                    if u == U_MEM[i] + MEM_STEPS:
                        after(f"mem{i}")
            act.wait_ge(o_all, 2 * NSA_HEADS)
            for t in range(NT):
                act.activation(junk_for(y_sq, 5 + t, HALF), bank[t][:, :], ACT.Square,
                               accum_out=lst[:, 32 + t:33 + t]).then_inc(y_sq, 1)
            split_t(6, xh, C_MOUT, 4, range(4), 4)
            for i in WOUT_ORDER[:3]:
                after(f"wout{i}")
            squares(7, xt, res_done, 17)
            split_t(7, xh, C_XN, 0)
            after(f"wout{WOUT_ORDER[3]}")
            def x_q(h):
                act.wait_ge(block_used, at[f"xq{h}"] + 1)
                act.activation(qx[:, 2 * h:2 * h + 2, :].rearrange("p a s -> p (a s)"), bank[QUERY_BANK[h]][:, :], ACT.Copy) \
                   .then_inc(q_out, 1)
                if h < 2:
                    after(f"xq{h}")

            def x_exp(h):
                act.wait_ge(a_max, h + 1)
                for t in range(NT):
                    act.activation(sx[h % 2][:, t, :], bank[4 + h % 2][:, t * SEQ:(t + 1) * SEQ], ACT.Exp, scale=XSCALE,
                                   bias=xst[:, h, 1, t:t + 1], accum_out=xst[:, h, 2, t:t + 1]) \
                       .then_inc(a_exp, 1)

            def x_pt(h):
                act.wait_ge(a_t, h + 1)
                if h >= 2:
                    act.wait_ge(ao_mm, h - 1)
                act.activation(px[h % 2][:, :, :].rearrange("p a s -> p (a s)"), bank[6][:, :], ACT.Copy) \
                   .then_inc(a_out, 1)

            def x_o(h):
                act.wait_ge(ao_mm, h + 1)
                act.activation(mh[:, 2 * h:2 * h + 2, :].rearrange("p a s -> p (a s)"), bank[7][:, :], ACT.Copy) \
                   .then_inc(ao_hi, 1)

            x_q(0)
            x_q(1)
            x_exp(0)
            for h in range(1, XHEADS + 1):
                if h >= 2:
                    after(("xq2", "xq3", "xo0")[h - 2])
                if h + 1 < XHEADS:
                    x_q(h + 1)
                x_pt(h - 1)
                if h < XHEADS:
                    x_exp(h)
                x_o(h - 1)
            after("xo1")
            after("xo2")
            squares(8, xt, res_done, 21)
            split_t(8, xh, C_FN2, 0)
            ffn(2, "xo3")
            squares(9, xt, res_done, 25)

        @block.vector
        def _(dve):
            order = [0]

            def then(ins):
                order[0] += 1
                ins.then_inc(dve_order, 1)
                dve.wait_ge(dve_order, order[0])

            def lo(n):
                if n >= NB:
                    return
                dve.wait_ge(hi_done, n + 1)
                for r, h, l in split_views(n, raw[n % 3], wh[n % 3], wl[n % 3]):
                    ins = dve.tensor_tensor(l, r, h.bitcast(F32), ALU.subtract)
                ins.then_inc(lo_done, 1)

            def split_t(e, hi_, lo_, c0, banks, ks=range(KD), done=0):
                for i, k in enumerate(ks):
                    if k % 2 == 0:
                        dve.wait_ge(t_hi, KD * e + done + i + 2)
                    src = bank[banks + k // 2][:, (k % 2) * SEQ:(k % 2 + 1) * SEQ]
                    dve.scalar_tensor_tensor(out=lo_[:, k, :], in0=src, scalar=col[:, c0 + k:c0 + k + 1],
                                             in1=hi_[:, k, :].bitcast(F32), op0=ALU.mult, op1=ALU.subtract) \
                       .then_inc(t_lo, 1)

            def normalise(q, src=xt, dst=xn):
                for t in range(NT):
                    dve.wait_ge(rstd_done, NT * q + t + 1)
                    for c in range(2):
                        cs_ = slice(c * HALF, (c + 1) * HALF)
                        dve.tensor_scalar(dst[:, t, cs_], src[:, t, cs_], rstd[:, q, t:t + 1], None, ALU.mult) \
                           .then_inc(xn_done, 1)

            def residual(r, last, count):
                for t in range(NT):
                    for c in range(2):
                        part = xt[:, t, c * HALF:(c + 1) * HALF]
                        if (t, c) == (NT - 1, 1):
                            dve.wait_ge(last, count)
                        else:
                            dve.wait_ge(bank_sum, 3 * r + 2 * t + c + 1)
                        dve.tensor_tensor(part, bank[2 * t + c][:, :], part, ALU.add).then_inc(res_done, 1)

            def times_gain():
                for t in range(NT):
                    for c in range(2):
                        part = xt[:, t, c * HALF:(c + 1) * HALF]
                        dve.wait_ge(sq_done, 4 * 5 + 2 * t + c + 1)
                        dve.tensor_tensor(part, part, gain[:, c * HALF:(c + 1) * HALF], ALU.mult).then_inc(gained, 1)

            def times_rstd():
                for t in range(NT):
                    dve.tensor_scalar(xt[:, t, :], xt[:, t, :], rstd[:, 5, t:t + 1], None, ALU.mult) \
                       .then_inc(scaled, 1)

            def last_norm(q):
                for t in range(NT):
                    for c in range(2):
                        cs_ = slice(c * HALF, (c + 1) * HALF)
                        dve.wait_ge(res_done, 4 * 6 + 2 * t + c + 1)
                        dve.tensor_tensor(xn[:, t, cs_], xt[:, t, cs_], gain[:, cs_], ALU.mult).then_inc(gained, 1)
                for t in range(NT):
                    dve.wait_ge(rstd_done, NT * q + t + 1)
                    for c in range(2):
                        cs_ = slice(c * HALF, (c + 1) * HALF)
                        dve.wait_ge(gained, 4 + 2 * t + c + 1)
                        dve.tensor_scalar(xn[:, t, cs_], xn[:, t, cs_], rstd[:, q, t:t + 1], None, ALU.mult) \
                           .then_inc(scaled, 1)

            def norm(q, e, c0):
                normalise(q)
                split_t(e, xh, xl, c0, 0)

            def ffn(layer, before):
                n0, m0 = at[f"ffn{layer}"], STEPS * layer

                def step(j, i, jj):
                    s = (m0 + jj) % 3
                    n, m = n0 + j, m0 + j
                    g, u = bank[4 + s][:, 0:SEQ], bank[4 + s][:, SEQ:2 * SEQ]
                    if layer == 2:
                        dve.wait_ge(conv_in, 2 * j + 2)
                        for half, (src, dst) in enumerate(((g, cg[s]), (u, cu[s]))):
                            for back in (1, 2):
                                if back == 2:
                                    dve.wait_ge(conv_tap, 4 * j + 2 * half + 1)
                                c = C_DW + (2 - back) * NF2 + half * STEPS
                                dve.scalar_tensor_tensor(
                                    out=dst[:, back:SEQ], in0=src[:, 0:SEQ - back],
                                    scalar=col[:, bass.ds(j + c, 1)], in1=dst[:, back:SEQ],
                                    op0=ALU.mult, op1=ALU.add).then_inc(conv_tap, 1)
                        dve.wait_ge(conv_tap, 4 * j + 4)
                        g, u = cg[s][:, :], cu[s][:, :]
                    dve.wait_ge(tanh_done, m + 1)
                    dve.scalar_tensor_tensor(out=ga[:, :], in0=th[s][:, :], scalar=1.0, in1=g,
                                             op0=ALU.add, op1=ALU.mult).then_inc(gated, 1)
                    dve.wait_ge(gated, m + 1)
                    dve.scalar_tensor_tensor(out=pr[s][:, :], in0=ga[:, :], scalar=0.5, in1=u,
                                             op0=ALU.mult, op1=ALU.mult).then_inc(prod_done, 1)

                    def next_weights():
                        if i is not None or jj + 3 < STEPS:
                            ns = (n0 + jj) % 3
                            dve.wait_ge(hi_done, n + 4)
                            dve.tensor_tensor(wl[ns][:, :], raw[ns][:, :], wh[ns][:, :].bitcast(F32),
                                              ALU.subtract).then_inc(lo_done, 1)
                        else:
                            lo(n0 + jj + 3)

                    dve.wait_ge(h_hi, m + 1)
                    dve.tensor_tensor(hl[s][:, :], pr[s][:, :], hh[s][:, :].bitcast(F32), ALU.subtract) \
                       .then_inc(h_ready, 1)
                    if jj == 0:
                        after(before)
                    next_weights()

                step(0, None, 0)
                with dve.Fori(0, LOOPED // 3) as i:
                    for s in range(1, 4):
                        step(3 * i + s, i, s)
                for j in range(LOOPED + 1, STEPS):
                    step(j, None, j)

            def after(name):
                lo(at[name] + 3)

            dve.memset(zero[:, :].bitcast(F32), 0.0).then_inc(zero_set, 1)
            dve.sem_inc(prod_done, 3)
            dve.wait_ge(pos_loaded, 16)
            dve.wait_ge(con_loaded, 16)
            then(dve.tensor_copy(posf[:, :], posi[:, :]))
            inv = con[:, K_INV:K_INV + ROPE // 2]
            for t in range(NT):
                then(dve.tensor_scalar(ang[:, t, :], inv, posf[:, t:t + 1], None, ALU.mult))
            magic = 1.5 * 2.0 ** 23
            then(dve.tensor_scalar(kk[:, :, :], ang[:, :, :], float(1.0 / (2 * np.pi)), magic, ALU.mult, ALU.add))
            then(dve.tensor_scalar(kk[:, :, :], kk[:, :, :], -magic, None, ALU.add))
            rest = 2 * np.pi
            src = ang
            for bits in (2 ** 5, 2 ** 14, 2 ** 23, None):
                part = float(np.float32(rest)) if bits is None else float(np.floor(rest * bits) / bits)
                rest -= part
                then(dve.scalar_tensor_tensor(out=r0[:, :, :], in0=kk[:, :, :], scalar=-part, in1=src[:, :, :],
                                              op0=ALU.mult, op1=ALU.add))
                src = r0
            pi32 = 3.1415925
            then(dve.tensor_scalar(r0[:, :, :], r0[:, :, :], pi32, -pi32, ALU.min, ALU.max))
            then(dve.tensor_scalar(r1[:, :, :], r0[:, :, :], -1.0, None, ALU.mult))
            then(dve.tensor_tensor(r1[:, :, :], r1[:, :, :], r0[:, :, :], ALU.min))
            dve.tensor_scalar(r1[:, :, :], r1[:, :, :], float(np.pi / 2), None, ALU.add).then_inc(rope_a, 1)
            dve.wait_ge(rstd_done, NT)
            dve.wait_ge(band_loaded, 16)
            edge = NG * P + NG * EDGE
            dve.tensor_scalar(bandr[:, 0:edge], band[:, 0:edge], rstd[:, 0, 0:1], None, ALU.mult) \
               .then_inc(pool_scaled, 1)
            dve.tensor_scalar(bandr[:, edge:NPOOL], band[:, edge:NPOOL], rstd[:, 0, 1:2], None, ALU.mult) \
               .then_inc(pool_scaled, 1)
            dve.wait_ge(raw_full[0], 32)
            dve.wait_ge(pscale_loaded, 16)
            rv = raw[0][:, :].rearrange("p (g c d) -> p g c d", g=NG, c=2)
            pv_ = pscale[:, :].rearrange("p (g a d) -> p g a d", g=NG, a=1).to_broadcast([P, NG, 2, 256])
            dve.tensor_tensor(rv, rv, pv_, ALU.mult).then_inc(pool_scaled, 1)
            lo(0)
            dve.wait_ge(rope_s, 2)
            dve.tensor_copy(cs[:, :, 32:64], cs[:, :, 0:32]).then_inc(rope_s, 1)
            dve.tensor_scalar(sn[:, :, 0:32], sn[:, :, 32:64], -1.0, None, ALU.mult).then_inc(rope_s, 1)
            normalise(1, memt, memt)
            split_t(0, xh, xl, C_MIX0, 0)
            lo(1)
            split_t(1, mh, ml, C_MEMN, 4)
            residual(0, block_used, at["pool"] + 1)
            lo(2)
            dve.wait_ge(cols_t, 2)
            dve.sem_inc(region_free, 1)
            norm(2, 2, C_FFN)
            lo(3)
            dve.wait_ge(cols_done, 2)
            taps = col[:, C_CDW:C_CDW + 2 * TAPS]
            dve.tensor_scalar(taps, taps, 0.5, None, ALU.mult).then_inc(taps_halved, 1)
            ffn(0, "mem0")
            residual(1, down_done, 3 + STEPS)
            norm(3, 3, C_MIX1)
            after("mem1")
            after("down0")
            after("down1")
            for part in range(2):
                dve.wait_ge(mla_rs, part + 1)
                for t in range(NT):
                    lat = ds[:, t, 0:QLR] if part == 0 else ds[:, t, QLR:QLR + KVR]
                    dve.tensor_scalar(lat, lat, mst[:, 3, part, t:t + 1], None, ALU.mult).then_inc(mla_scaled, 1)
                if part == 0:
                    after("down2")

            def rope(src, dst, nh, t):
                n = nh * ROPE
                c = cs[:, t:t + 1, :].to_broadcast([P, nh, ROPE])
                s = src.rearrange("p (h d) -> p h d", h=nh)
                a3 = ra[:, 0:n].rearrange("p (h d) -> p h d", h=nh)
                b3 = rb[:, 0:n].rearrange("p (h d) -> p h d", h=nh)
                dve.tensor_tensor(a3, s, c, ALU.mult)
                dve.tensor_tensor(b3[:, :, 0:32], s[:, :, 32:64], sn[:, t:t + 1, 0:32].to_broadcast([P, nh, 32]),
                                  ALU.mult)
                then(dve.tensor_tensor(b3[:, :, 32:64], s[:, :, 0:32],
                                       sn[:, t:t + 1, 32:64].to_broadcast([P, nh, 32]), ALU.mult))
                return dve.tensor_tensor(dst, ra[:, 0:n], rb[:, 0:n], ALU.add)

            def turn_keys():
                for t in range(NT):
                    dve.wait_ge(ds_out, 4)
                    then(rope(ds[:, t, QLR + KVR:MLA_DOWN], kr[:, t, 0:ROPE], 1, t))
                    dve.tensor_copy(kr[:, t, ROPE:P], kr[:, t, 0:ROPE]).then_inc(kr_done, 1)

            for f in range(4):
                dve.wait_ge(cq_hi, f // 2 * 2 + 2)
                dve.scalar_tensor_tensor(out=xl[:, f, :], in0=bank[4 + f // 2][:, (f % 2) * SEQ:(f % 2 + 1) * SEQ],
                                         scalar=col[:, C_QN + f:C_QN + f + 1], in1=xh[:, f, :].bitcast(F32),
                                         op0=ALU.mult, op1=ALU.subtract).then_inc(cq_lo, 1)
            turn_keys()
            after("mem2")
            after("uq0")
            after("uq1")
            dve.wait_ge(block_used, at["uq2"] + 1)
            for t in range(NT):
                if t:
                    dve.wait_ge(qr_done, t)
                rope(bank[t][:, :], qr[:, t, :], HEADS, t).then_inc(qr_done, 1)
            for i in range(2, 4):
                if i == 2:
                    dve.wait_ge(v_mm, 3)
                else:
                    dve.wait_ge(block_used, at["ukv"] + 1)
                dve.tensor_copy(vv[:, 1, (i - 2) * HALF:(i - 1) * HALF], bank[VALUE_BANK[i]][:, :]).then_inc(v_out, 1)

            def mla_max(h):
                dve.wait_ge(s_mm, h + 1)
                if h >= 2:
                    dve.wait_ge(p_t, h - 1)
                for t, (a, b) in enumerate(((0, P), (P, 3 * P))):
                    ins = dve.tensor_tensor_reduce(sc[h % 2][:, a:b], bank[4 + h % 2][:, a:b], mask[:, a:b], MLA_SCALE,
                                                   3.0 * NEG, ALU.add, ALU.max, stat[:, h, 0, t:t + 1])
                then(ins)
                dve.tensor_scalar(stat[:, h, 1, :], stat[:, h, 0, :], -1.0, None, ALU.mult).then_inc(s_max, 1)

            def mla_norm(h):
                dve.wait_ge(s_exp, 2 * h + 2)
                then(dve.reciprocal(stat[:, h, 3, :], stat[:, h, 2, :]))
                for t, (a, b) in enumerate(((0, P), (P, 3 * P))):
                    ins = dve.tensor_scalar(sc[h % 2][:, a:b], sc[h % 2][:, a:b], stat[:, h, 3, t:t + 1], None,
                                            ALU.mult)
                    ins.then_inc(s_norm, 1)

            def mla_o(h):
                dve.wait_ge(o_hi, h + 1)
                dve.tensor_tensor(xl[:, h, :], bank[7][:, (h % 2) * SEQ:(h % 2 + 1) * SEQ], xh[:, h, :].bitcast(F32),
                                  ALU.subtract).then_inc(o_lo, 1)

            for h in range(2):
                mla_max(h)
                mla_norm(h)
            for h in range(HEADS):
                if h + 2 < HEADS:
                    mla_max(h + 2)
                mla_o(h)
                if h + 2 < HEADS:
                    mla_norm(h + 2)
                if h in (2, 4, 6):
                    after(("uq2", "ukv", "wo0")[h // 2 - 1])
            after("wo1")
            after("wo2")
            residual(2, block_used, at["wo3"] + 1)
            dve.sem_inc(region_free, 1)
            norm(4, 4, C_FFN + 8)
            after("wo3")
            ffn(1, "mem3")
            residual(3, down_done, 3 + 2 * STEPS)
            dve.wait_ge(gain_loaded, 16)
            times_gain()
            dve.memset(vbd[:, :], 0.0).then_inc(vbd_zero, 1)
            dve.memset(hc[:, :, 0:PAD], 0.0)
            normalise(6)
            after("mem4")
            split_t(5, xh, xl, C_MIXN, 0)
            after("mem5")
            times_rstd()
            after("z_a")
            after("z_gt")
            dve.wait_ge(z_out, 1)
            then(dve.scalar_tensor_tensor(out=hc[:, :, PAD:PAD + SEQ], in0=e1[:, :].rearrange("p (a s) -> p a s", a=2),
                                          scalar=1.0, in1=bank[0][:, :].rearrange("p (a s) -> p a s", a=2),
                                          op0=ALU.add, op1=ALU.mult))
            dve.sem_inc(hc_done, 1)

            def conv(which):
                for k, c in which:
                    tap = col[:, C_CDW + 2 * k + c:C_CDW + 2 * k + c + 1]
                    if k == 0:
                        ins = dve.tensor_scalar(yc[:, 0, :], hc[:, 0, 0:SEQ], tap, col[:, C_CDB:C_CDB + 1],
                                                ALU.mult, ALU.add)
                    else:
                        if (k - 1, c) in VECTOR_TAPS:
                            dve.wait_ge(cv_tap, VECTOR_TAPS.index((k - 1, c)) + 1)
                        else:
                            dve.wait_ge(cv_tap_pool, k)
                        ins = dve.scalar_tensor_tensor(out=yc[:, c, :], in0=hc[:, c, k:k + SEQ], scalar=tap,
                                                       in1=yc[:, c, :], op0=ALU.mult, op1=ALU.add)
                    ins.then_inc(cv_tap, 1)

            conv(VECTOR_TAPS[0:1])
            for i, name in enumerate(("z_v", "z_u")):
                b = bank[2 + i]
                dve.wait_ge(gz_a, 2 * i + 1)
                dve.tensor_scalar(e3[:, :], e1[:, :], GELU_C, 1.0, ALU.mult, ALU.add).then_inc(gz_d, 1)
                dve.wait_ge(gz_d, 3 * i + 1)
                dve.tensor_tensor(e2[:, :], e3[:, :], b[:, :], ALU.mult).then_inc(gz_d, 1)
                conv(VECTOR_TAPS[1 + 2 * i:3 + 2 * i])
                dve.wait_ge(gz_a, 2 * i + 2)
                dve.scalar_tensor_tensor(out=(vg, uu)[i], in0=e1[:, :].rearrange("p (t c) -> p t c", t=NT), scalar=1.0,
                                         in1=b[:, :].rearrange("p (t c) -> p t c", t=NT), op0=ALU.add,
                                         op1=ALU.mult).then_inc(gz_d, 1)
                dve.wait_ge(gz_d, 3 * i + 3)
                if i == 0:
                    for t in range(NT):
                        dve.bn_stats(lst[:, 6 * t:6 * t + 6], vg[:, t, :])
                    then(dve.memset(lst[:, 60:61], 0.0))
                    for t in range(NT):
                        dve.bn_aggr(lst[:, 12 + 2 * t:14 + 2 * t], lst[:, 6 * t:6 * t + 6]).then_inc(vn_done, 1)
                after(name)
            dve.wait_ge(ln_rs, 1)
            dve.wait_ge(z_params, 64)
            for t in range(NT):
                then(dve.tensor_scalar(vg[:, t, :], vg[:, t, :], lst[:, 12 + 2 * t:13 + 2 * t], lst[:, 20 + t:21 + t],
                                       ALU.subtract, ALU.mult))
            then(dve.tensor_tensor(vg, vg, lng[:, 0, 0:1, :].to_broadcast([P, NT, GW]), ALU.mult))
            dve.tensor_tensor(vg, vg, lng[:, 0, 1:2, :].to_broadcast([P, NT, GW]), ALU.add).then_inc(vn_done, 1)
            dve.wait_ge(shifted, 64)
            for a in range(2):
                src = bass.AP(x4[:, a, :, :].tensor, x4[:, a, :, :].offset,
                              [list(x4[:, a, :, :].ap[0]), [2, CMP_KT], [SEQ, GROUPS], [CMP_STRIDE, NCMP]])
                pe_ = col[:, C_PE + a * CMP_KT:C_PE + (a + 1) * CMP_KT]
                pe_ = bass.AP(pe_.tensor, pe_.offset, [list(pe_.ap[0]), [1, CMP_KT], [0, GROUPS], [0, NCMP]])
                dve.tensor_tensor(fl[:, a, :, :, :], src, pe_, ALU.add).then_inc(fl_done, 1)
            after("z_kcvc")
            conv(VECTOR_TAPS[5:7])
            after("z_q0")
            conv(VECTOR_TAPS[7:9])
            dve.wait_ge(cmp_a, 1)
            hs = bank[7][0:DH, 0:60]
            dve.tensor_scalar(hg[:, 3, :], hg[:, 0, :], GELU_C, 1.0, ALU.mult, ALU.add).then_inc(cmp_d, 1)
            dve.wait_ge(cmp_d, 1)
            dve.tensor_tensor(hg[:, 2, :], hg[:, 3, :], hs, ALU.mult).then_inc(cmp_d, 1)
            dve.wait_ge(cmp_a, 2)
            dve.scalar_tensor_tensor(out=hg[:, 3, :], in0=hg[:, 1, :], scalar=1.0, in1=hs, op0=ALU.add,
                                     op1=ALU.mult).then_inc(cmp_d, 1)
            after("z_q1")
            conv(VECTOR_TAPS[9:11])
            after("z_ksw")
            conv(VECTOR_TAPS[11:TAPS_BEFORE])
            n240 = NT * NSA_HEADS * NCMP
            dve.wait_ge(sc_mm, GROUPS)

            def m3(ap):
                return ap.rearrange("p (t h n) -> p t h n", t=NT, h=NSA_HEADS)

            def m2(ap):
                return ap.rearrange("p (a n) -> p a n", n=NCMP)

            def over_heads(c0):
                return con[:, c0:c0 + NT * NCMP].rearrange("p (t a n) -> p t a n", t=NT, a=1) \
                    .to_broadcast([P, NT, NSA_HEADS, NCMP])

            def per_row(ap):
                return ap.rearrange("p (a b) -> p a b", b=1).to_broadcast([P, NT * NSA_HEADS, NCMP])

            mx = lst[:, 24:24 + 16]
            for g in range(GROUPS):
                bias = con[:, K_CB:K_CB + NT * NCMP].rearrange("p (t a n) -> p t a n", t=NT, a=1) \
                    .to_broadcast([P, NT, REP, NCMP])
                sc_g = bank[g][:, 0:n240 // GROUPS].rearrange("p (t h n) -> p t h n", t=NT, h=REP)
                then(dve.tensor_tensor(m3(cm[2])[:, :, g * REP:(g + 1) * REP, :], sc_g, bias, ALU.add))
            then(dve.tensor_reduce(mx, m2(cm[2]), AX.X, ALU.max))
            dve.tensor_tensor(m2(cm[0]), m2(cm[2]), per_row(mx), ALU.subtract).then_inc(cm_e, 1)
            after("z_vsw")
            dve.wait_ge(cm_e, 2)
            then(dve.tensor_tensor(m3(cm[2]), m3(cm[1]), over_heads(K_C01), ALU.mult))
            then(dve.tensor_reduce(mx, m2(cm[2]), AX.X, ALU.add))
            then(dve.tensor_scalar(mx, mx, TINY, None, ALU.max))
            then(dve.reciprocal(mx, mx))
            dve.wait_ge(gl_t, 1)
            dve.tensor_scalar(gate[:, :, :], bank[2][:, SEQ:SEQ + NT * 24].rearrange("p (t c) -> p t c", t=NT), 1.0, 0.5, ALU.add, ALU.mult).then_inc(gl_done, 1)
            dve.wait_ge(gl_done, 1)
            gv = gate[:, :, :].rearrange("p t (h b) -> p t h b", b=3)
            then(dve.tensor_tensor(mx.rearrange("p (t h) -> p t h", t=NT), mx.rearrange("p (t h) -> p t h", t=NT),
                                   gv[:, :, :, 0], ALU.mult))
            dve.tensor_tensor(m2(cm[3]), m2(cm[2]), per_row(mx), ALU.mult).then_inc(pc_done, 1)
            after("z_gl")

            def nsa_max(u):
                dve.wait_ge(n_mm, u + 1)
                if u >= 2:
                    dve.wait_ge(n_t, u - 1)
                for t, (a, b) in enumerate(((0, P), (P, 3 * P))):
                    ins = dve.tensor_tensor_reduce(s2[u % 2][:, a:b], bank[4 + u % 2][:, a:b], mask[:, a:b], NSA_SCALE,
                                                   3.0 * NEG, ALU.add, ALU.max, nst[:, 0, u, t:t + 1])
                then(ins)
                dve.tensor_scalar(nst[:, 1, u, :], nst[:, 0, u, :], -1.0, None, ALU.mult).then_inc(n_max, 1)

            def nsa_norm(u):
                h, br = u // 2, u % 2
                dve.wait_ge(n_exp, 2 * u + 2)
                then(dve.reciprocal(nst[:, 3, u, :], nst[:, 2, u, :]))
                dve.tensor_tensor(nst[:, 3, u, :], nst[:, 3, u, :], gv[:, :, h, 1 + br], ALU.mult).then_inc(n_rec, 1)

            e3v = e3[:, :].rearrange("p (t c) -> p t c", t=NT)
            e2v = e2[:, :].rearrange("p (t c) -> p t c", t=NT)

            def normalise_y():
                for t in range(NT):
                    for s, a, b in ((1, 512, 768), (2, 768, 1024)):
                        dve.tensor_scalar(yn[:, t, a:b], yn[:, t, a:b], lst[:, 48 + 2 * s + t:49 + 2 * s + t], None,
                                          ALU.mult).then_inc(y_scaled, 1)

            for u in range(2):
                nsa_max(u)
                nsa_norm(u)
            for u in range(2 * NSA_HEADS):
                if u + 2 < 2 * NSA_HEADS:
                    nsa_max(u + 2)
                conv(VECTOR_TAPS[TAPS_BEFORE + TAPS_PER_STEP * u:TAPS_BEFORE + TAPS_PER_STEP * (u + 1)])
                if u + 2 < 2 * NSA_HEADS:
                    nsa_norm(u + 2)
                if u == 0:
                    dve.wait_ge(mix_mm, 1)
                    for t in range(NT):
                        dve.tensor_tensor(yn[:, t, 512:768], bank[7][:, t * GW:(t + 1) * GW], uu[:, t, :],
                                          ALU.mult).then_inc(gy_done, 1)
                if u == U_STATS:
                    dve.wait_ge(ycs_t, 1)
                    for t in range(NT):
                        dve.bn_stats(lst[:, 6 * t:6 * t + 6], bank[3][:, t * CW_:(t + 1) * CW_])
                    then(dve.memset(lst[:, 60:61], 0.0))
                    for t in range(NT):
                        dve.bn_aggr(lst[:, 40 + 2 * t:42 + 2 * t], lst[:, 6 * t:6 * t + 6]).then_inc(vn_done, 1)
                if u == U_LN:
                    dve.wait_ge(ln_rs, 2)
                    for t in range(NT):
                        then(dve.tensor_scalar(e3[:, t * GW:(t + 1) * GW], bank[3][:, t * GW:(t + 1) * GW],
                                               lst[:, 40 + 2 * t:41 + 2 * t], lst[:, 44 + t:45 + t], ALU.subtract,
                                               ALU.mult))
                    then(dve.tensor_tensor(e3v, e3v, lng[:, 1, 0:1, :].to_broadcast([P, NT, GW]), ALU.mult))
                    dve.tensor_tensor(e2v, e3v, lng[:, 1, 1:2, :].to_broadcast([P, NT, GW]), ALU.add) \
                       .then_inc(cvln_done, 1)
                if u == U_SILU + 1:
                    dve.wait_ge(cv_a, 1)
                    dve.wait_ge(gy_done, 2)
                    dve.scalar_tensor_tensor(out=yn[:, :, 768:1024], in0=e1[:, :].rearrange("p (t c) -> p t c", t=NT),
                                             scalar=1.0, in1=e2v, op0=ALU.add, op1=ALU.mult).then_inc(cy_done, 1)
                if u == U_SQUARES + 1:
                    dve.wait_ge(y_rs, 1)
                    normalise_y()
                if u == U_SPLIT:
                    split_t(6, xh, xl, C_MOUT, 0, range(4, KD))
                for i in (6, 7):
                    if u == U_MEM[i] + MEM_STEPS:
                        after(f"mem{i}")
            for t in range(NT):
                dve.wait_ge(y_rs, 2 + t)
                dve.tensor_scalar(yn[:, t, 0:HALF], bank[t][:, :], lst[:, 48 + t:49 + t], None, ALU.mult) \
                   .then_inc(y_scaled, 1)
            split_t(6, xh, xl, C_MOUT, 4, range(4), 4)
            for i in WOUT_ORDER[:2]:
                after(f"wout{i}")
            residual(4, block_used, at[f"wout{WOUT_ORDER[3]}"] + 1)
            normalise(7)
            split_t(7, xh, xl, C_XN, 0)
            for i in WOUT_ORDER[2:]:
                after(f"wout{i}")
            def x_max(h):
                dve.wait_ge(a_mm, h + 1)
                then(dve.tensor_reduce(xst[:, h, 0, :], bank[4 + h % 2][:, :].rearrange("p (t s) -> p t s", t=NT), AX.X,
                                       ALU.max))
                dve.tensor_scalar(xst[:, h, 1, :], xst[:, h, 0, :], -XSCALE, None, ALU.mult).then_inc(a_max, 1)

            def x_norm(h):
                dve.wait_ge(a_exp, 2 * h + 2)
                then(dve.reciprocal(xst[:, h, 3, :], xst[:, h, 2, :]))
                for t in range(NT):
                    dve.tensor_scalar(sx[h % 2][:, t, :], sx[h % 2][:, t, :], xst[:, h, 3, t:t + 1], None, ALU.mult) \
                       .then_inc(a_norm, 1)

            def x_o(h):
                dve.wait_ge(ao_hi, h + 1)
                dve.tensor_tensor(ml[:, 2 * h:2 * h + 2, :].rearrange("p a s -> p (a s)"), bank[7][:, :],
                                  mh[:, 2 * h:2 * h + 2, :].rearrange("p a s -> p (a s)").bitcast(F32),
                                  ALU.subtract).then_inc(ao_lo, 1)

            after("xq0")
            after("xq1")
            x_max(0)
            x_norm(0)
            for h in range(1, XHEADS + 1):
                if h >= 2:
                    after(("xq2", "xq3", "xo0")[h - 2])
                if h < XHEADS:
                    x_max(h)
                    x_norm(h)
                x_o(h - 1)
            after("xo1")
            residual(5, block_used, at["xo3"] + 1)
            dve.sem_inc(region_free, 1)
            norm(8, 8, C_FN2)
            after("xo2")
            ffn(2, "xo3")
            residual(6, down_done, 3 + 3 * STEPS)
            dve.wait_ge(last_gain_loaded, 16)
            last_norm(9)

        @block.gpsimd
        def _(pool):
            order = [0]

            def then(ins):
                order[0] += 1
                ins.then_inc(pool_order, 1)
                pool.wait_ge(pool_order, order[0])

            def inverse_rms(q):
                for t in range(NT):
                    one = slice(t, t + 1)
                    pool.wait_ge(sq_done, 4 * q + 2 * t + 2)
                    then(pool.tensor_scalar(st1[:, q, one], ss[:, q, t, 0:1], ss[:, q, t, 1:2], EPS, ALU.add, ALU.add))
                    pool.tensor_tensor(rstd[:, q, one], st1[:, q, one], mhalf[:, 0:1], ALU.pow).then_inc(rstd_done, 1)

            def inverse_rms_after_norm():
                for t in range(NT):
                    one = slice(t, t + 1)
                    r = rstd[:, 5, one]
                    pool.wait_ge(sq_done, 4 * 6 + 2 * t + 2)
                    then(pool.tensor_scalar(st1[:, 6, one], ss[:, 6, t, 0:1], ss[:, 6, t, 1:2], r, ALU.add, ALU.mult))
                    then(pool.tensor_scalar(st1[:, 6, one], st1[:, 6, one], r, EPS, ALU.mult, ALU.add))
                    then(pool.tensor_tensor(st2[:, 6, one], st1[:, 6, one], mhalf[:, 0:1], ALU.pow))
                    pool.tensor_tensor(rstd[:, 6, one], st2[:, 6, one], r, ALU.mult).then_inc(rstd_done, 1)

            def down_lo(layer):
                m0 = STEPS * layer

                def one(s, m):
                    pool.wait_ge(d_hi, m + 1)
                    pool.tensor_tensor(dl[s][:, :], draw[s][:, :], dh[s][:, :].bitcast(F32), ALU.subtract) \
                        .then_inc(d_lo, 1)

                one(m0 % 3, m0)
                with pool.Fori(0, (STEPS - 1) // 3) as i:
                    for jj in range(1, 4):
                        one((m0 + jj) % 3, 3 * i + m0 + jj)

            then(pool.memset(mhalf[:, :], -0.5))
            for q in range(3):
                inverse_rms(q)
            down_lo(0)
            inverse_rms(3)
            for part, width in ((0, QLR), (1, KVR)):
                pool.wait_ge(mla_sq, 2 * part + 2)
                then(pool.tensor_scalar(mst[:, 1, part, :], mst[:, 0, part, :], 1.0 / width, EPS, ALU.mult, ALU.add))
                pool.tensor_tensor(mst[:, 3, part, :], mst[:, 1, part, :], mhalf[:, 0:NT], ALU.pow).then_inc(mla_rs, 1)
            inverse_rms(4)
            down_lo(1)
            inverse_rms(5)
            inverse_rms_after_norm()
            pool.wait_ge(down_done, 3 + 2 * STEPS)
            pool.dma_start(cw1[:, :, :, :], w["cmp_w1_2"][0].rearrange("a (k p) d -> p a k d", p=P)).then_inc(z_ws, 16)
            pool.dma_start(cw2[:, :, :], w["cmp_w2_2"][0].rearrange("a p d -> p a d")).then_inc(z_ws, 16)
            pool.dma_start(bsr[:, :], w["gmlp_bs_2"][0]).then_inc(z_ws, 16)
            for i, name in enumerate(("gmlp_ln_g_2", "gmlp_ln_b_2", "conv_ln_g_2", "conv_ln_b_2")):
                pool.dma_start(lng[:, i // 2, i % 2, :], w[name][0:1, :].to_broadcast([P, GW])).then_inc(z_params, 16)
            pool.wait_ge(gained, 4)
            pool.dma_start(gain[:, :], w["final_norm_g_2"].rearrange("(a d) -> a d", a=1).to_broadcast([P, D])) \
                .then_inc(last_gain_loaded, 16)
            def conv(k0, k1):
                for k in range(k0, k1):
                    tap = col[:, C_CDW + 2 * k + 1:C_CDW + 2 * k + 2]
                    if k == 0:
                        ins = pool.tensor_scalar(yc[:, 1, :], hc[:, 1, 0:SEQ], tap, col[:, C_CDB + 1:C_CDB + 2],
                                                 ALU.mult, ALU.add)
                    else:
                        pool.wait_ge(cv_tap_pool, k)
                        pool.tensor_scalar(tapped[:, :], hc[:, 1, k:k + SEQ], tap, None, ALU.mult) \
                            .then_inc(tapped_done, 1)
                        pool.wait_ge(tapped_done, k)
                        ins = pool.tensor_tensor(yc[:, 1, :], yc[:, 1, :], tapped[:, :], ALU.add)
                    ins.then_inc(cv_tap_pool, 1)

            def layer_norm_rstd(i, src, dst):
                pool.wait_ge(vn_done, 2 if i == 0 else 5)
                var = lst[:, src:src + 4].rearrange("p (t b) -> p t b", b=2)[:, :, 1]
                then(pool.tensor_scalar(lst[:, 16 + 2 * i:18 + 2 * i], var, 1.0, 4.0 * EPS if i == 0 else EPS,
                                        ALU.mult, ALU.add))
                pool.tensor_tensor(lst[:, dst:dst + 2], lst[:, 16 + 2 * i:18 + 2 * i], mhalf[:, 0:NT], ALU.pow) \
                    .then_inc(ln_rs, 1)

            pool.wait_ge(hc_done, 1)
            conv(0, 2)
            layer_norm_rstd(0, 12, 20)
            conv(2, 11)
            pool.wait_ge(cmp_mm, 1)
            pool.dma_start(ws.rearrange("p (g s) -> p g s", g=GG), w["gmlp_ws_2"][0].rearrange("g t s -> t g s")) \
                .then_inc(ws_loaded, 16)
            conv(11, 16)
            pool.wait_ge(ws_loaded, 16)
            w3 = ws.rearrange("p (g s) -> p g s", g=GG)
            pool.affine_select(out=w3, in_=w3, compare_op=ALU.is_ge, fill=0.0, base=0,
                               pattern=[[0, GG], [-1, P]], channel_multiplier=1).then_inc(ws_cut, 1)
            conv(16, POOL_TAPS)
            layer_norm_rstd(1, 40, 44)
            pool.wait_ge(y_sq, 4)
            then(pool.tensor_scalar(lst[:, 56:60], lst[:, 34:38], 1.0 / 256, 4.0 * EPS, ALU.mult, ALU.add))
            pool.tensor_tensor(lst[:, 50:54], lst[:, 56:60], mhalf[:, 0:4], ALU.pow).then_inc(y_rs, 1)
            for t in range(NT):
                pool.wait_ge(y_sq, 5 + t)
                then(pool.tensor_scalar(lst[:, 54 + t:55 + t], lst[:, 32 + t:33 + t], 1.0 / 512, EPS, ALU.mult, ALU.add))
                pool.tensor_tensor(lst[:, 48 + t:49 + t], lst[:, 54 + t:55 + t], mhalf[:, 0:1], ALU.pow) \
                    .then_inc(y_rs, 1)
            inverse_rms(7)
            inverse_rms(8)
            down_lo(2)
            inverse_rms(9)

        @block.tensor
        def _(pe):
            def three(outp, a_hi, a_lo, b_hi, b_lo, start, stop, **kw):
                pe.matmul(outp, a_hi, b_hi, start=start, stop=False, **kw)
                pe.matmul(outp, a_hi, b_lo, start=False, stop=False, **kw)
                return pe.matmul(outp, a_lo, b_hi, start=False, stop=stop, **kw)

            def weights(name, k, c):
                n = at[name]
                pe.wait_ge(lo_done, n + 1)
                return k_view(wh[n % 3], k, c), k_view(wl[n % 3], k, c)

            zero4 = zero[:, :].rearrange("p (a b) -> p a b", a=1).to_broadcast([P, HALF // P, P])

            def turn(src, banks, ks=range(KD), ready=None):
                for t in range(NT):
                    for k in ks:
                        if ready is not None and k % 4 == 0:
                            ready(2 * t + k // 4)
                        o = bank[banks + k // 2][:, (k % 2) * SEQ + t * P:(k % 2) * SEQ + (t + 1) * P]
                        ins = pe.transpose(o, src[:, t, k * P:(k + 1) * P], ident)
                        if k % 2 and t == NT - 1:
                            ins.then_inc(t_done, 1)

            def normalised(i):
                return lambda half: pe.wait_ge(xn_done, 4 * i + half + 1)

            def split_wait(e):
                return lambda k: pe.wait_ge(t_lo, KD * e + max(k + 1, 2))

            def columns(name, b, a_hi, a_lo, between=None):
                h_, l_ = weights(name, KD, 2 * P)
                for f in range(2):
                    if f == 1 and between is not None:
                        between()
                    for k in range(KD):
                        fs = slice(f * P, (f + 1) * P)
                        ins = three(bank[b][:, f * SEQ:(f + 1) * SEQ], h_[:, k, fs], l_[:, k, fs], a_hi[:, k, :],
                                    a_lo[:, k, :], k == 0, k == KD - 1)
                ins.then_inc(block_used, 1)

            def tokens(name, b, width, a_hi, a_lo, at_col=None):
                h_, l_ = weights(name, KD, width)
                for t in range(NT):
                    for k in range(KD):
                        c = width * t if at_col is None else at_col
                        bb = b if at_col is None else b + t
                        ins = three(bank[bb][:, c:c + width], a_hi[:, k, t * P:(t + 1) * P],
                                    a_lo[:, k, t * P:(t + 1) * P], h_[:, k, :], l_[:, k, :], k == 0, k == KD - 1)
                ins.then_inc(block_used, 1)

            def row_block(name, i, a_hi, a_lo, first, last, tiles=range(NT), through=True):
                h_, l_ = weights(name, 2, D)
                for t in tiles:
                    for c in range(2):
                        for kk_ in range(2):
                            ins = three(bank[2 * t + c][:, :], a_hi[:, 2 * i + kk_, t * P:(t + 1) * P],
                                        a_lo[:, 2 * i + kk_, t * P:(t + 1) * P], h_[:, kk_, c * HALF:(c + 1) * HALF],
                                        l_[:, kk_, c * HALF:(c + 1) * HALF], first and kk_ == 0, last and kk_ == 1)
                        if last and (t, c) != (NT - 1, 1):
                            ins.then_inc(bank_sum, 1)
                if through:
                    ins.then_inc(block_used, 1)

            def mem_block(i, between=None):
                if i > 0:
                    pe.wait_ge(mem_out, i)
                if i < 4:
                    columns(f"mem{i}", 7, mh, ml, between)
                else:
                    tokens(f"mem{i}", 7, 2 * P, mh, ml)

            def norm(i, rs):
                pe.wait_ge(res_done, rs)
                turn(xn, 0, ready=normalised(i))

            def seed(b):
                pe.matmul(bank[b][:, :], zero[:, :], zero4, start=True, stop=True)

            def first_product(n, b, e):
                pe.wait_ge(lo_done, n + 1)
                seed(b)
                for of_lo in (False, True):
                    for k in range(KD):
                        pe.wait_ge(t_lo if of_lo else t_hi, KD * e + k + 1)
                        for half in range(2):
                            o = bank[b][:, half * SEQ:(half + 1) * SEQ]
                            a = (2 * k + half) * P
                            for w_ in ((wh,) if of_lo else (wh, wl)):
                                ins = pe.matmul(o, w_[n % 3][:, a:a + P], (xl if of_lo else xh)[:, k, :], start=False,
                                                stop=True, skip_group_check=True)
                ins.then_inc(block_used, 1)

            def ffn(layer, e):
                n0, m0 = at[f"ffn{layer}"], STEPS * layer
                if layer == 0:
                    pe.wait_ge(cols_done, 2)

                def up(j, jj):
                    n, m = n0 + j, m0 + j
                    ns, s = (n0 + jj) % 3, (m0 + jj) % 3
                    pe.wait_ge(lo_done, n + 1)
                    pe.wait_ge(prod_done, m + 1)
                    for half in range(2):
                        for k in range(KD):
                            a = (2 * k + half) * P
                            ins = three(bank[4 + s][:, half * SEQ:(half + 1) * SEQ], wh[ns][:, a:a + P],
                                        wl[ns][:, a:a + P], xh[:, k, :], xl[:, k, :], k == 0, k == KD - 1)
                    ins.then_inc(block_used, 1)

                def down(j, jj, last=False):
                    m = m0 + j
                    s = (m0 + jj) % 3
                    pe.wait_ge(d_lo, m + 1)
                    pe.wait_ge(h_ready, m + 1)
                    for t in range(NT):
                        for c in range(2):
                            ins = three(bank[2 * t + c][:, :], hh[s][:, t * P:(t + 1) * P], hl[s][:, t * P:(t + 1) * P],
                                        dh[s][:, c * HALF:(c + 1) * HALF], dl[s][:, c * HALF:(c + 1) * HALF],
                                        False, last, skip_group_check=True)
                            if last and (t, c) != (NT - 1, 1):
                                ins.then_inc(bank_sum, 1)
                    ins.then_inc(down_done, 1)

                pe.wait_ge(prod_done, m0 + 1)
                first_product(n0, 4 + m0 % 3, e)
                for b in range(4):
                    seed(b)
                with pe.Fori(0, LOOPED // 3) as i:
                    for s in range(1, 4):
                        up(3 * i + s, s)
                        down(3 * i + s - 1, s - 1)
                up(LOOPED + 1, LOOPED + 1)
                down(LOOPED, LOOPED)
                for j in range(LOOPED + 2, STEPS):
                    up(j, j)
                for j in range(LOOPED + 1, STEPS):
                    down(j, j, j == STEPS - 1)

            pe.sem_inc(down_done, 3)
            pe.wait_ge(con_loaded, 16)
            pe.wait_ge(zero_set, 1)
            pe.wait_ge(x_loaded, 16 * NT)
            pe.wait_ge(pool_scaled, 2)
            for k in range(KD):
                g = k // 2
                o = (k % 2) * SEQ
                b = bank[k // 2]
                ks = slice(k * P, (k + 1) * P)
                e0, d1 = NG * P + g * EDGE, NG * P + NG * EDGE + g * P
                pe.matmul(b[:, o:o + P], xt[:, 0, ks], bandr[:, g * P:(g + 1) * P], start=True, stop=True)
                pe.matmul(b[:, o + P:o + SEQ], xt[:, 1, ks], bandr[:, d1:d1 + P], start=True, stop=True)
                ins = pe.matmul(b[:, o + P:o + P + EDGE], xt[:, 0, ks], bandr[:, e0:e0 + EDGE], start=False, stop=True,
                                skip_group_check=True)
                if k % 2:
                    ins.then_inc(t_done, 1)
                if k == 1:
                    pe.wait_ge(rows_loaded, 16 * EARLY_ROWS)
                    pe.transpose(bank[7][:, 0:EARLY], prow[0][0:EARLY, :], con[0:EARLY, K_ID:K_ID + EARLY]).then_inc(cols_t, 1)
            pe.wait_ge(cols_done, 1)
            turn(memt, 4, ready=normalised(0))
            h_, l_ = weights("pool", 2 * NG, 256)
            split = split_wait(0)
            for t in range(NT):
                for g in range(NG):
                    for c in range(2):
                        k = 2 * g + c
                        if t == 0:
                            split(k)
                        ins = three(bank[2 * t + g // 2][:, (g % 2) * 256:(g % 2 + 1) * 256],
                                    xh[:, k, t * P:(t + 1) * P], xl[:, k, t * P:(t + 1) * P],
                                    h_[:, k, :], l_[:, k, :], c == 0, c == 1)
                    if g % 2 and (t, g) != (NT - 1, NG - 1):
                        ins.then_inc(bank_sum, 1)
            ins.then_inc(block_used, 1)
            pe.wait_ge(t_lo, KD * 2)
            pe.wait_ge(late_rows_loaded, 16 * LATE_ROWS)
            c = 0
            for i, n in ((1, 2 * TAPS + 2 * CMP_KT), (2, 2 * NF2), (3, 2 * NF2)):
                ins = pe.transpose(bank[6][:, c:c + n], prow[i][0:n, :], con[0:n, K_ID:K_ID + n])
                c += n
            ins.then_inc(cols_t, 1)
            mem_block(0)
            norm(1, 4)
            ffn(0, 2)
            mem_block(1)
            norm(2, 8)
            third = MLA_DOWN // 3
            h_, l_ = weights("down0", KD, third)
            for k in range(KD):
                pe.wait_ge(t_hi, KD * 3 + k + 1)
                for t in range(NT):
                    tok = slice(t * P, (t + 1) * P)
                    pe.matmul(bank[4 + t][:, 0:third], xh[:, k, tok], h_[:, k, :], start=k == 0, stop=False)
                    pe.matmul(bank[4 + t][:, 0:third], xh[:, k, tok], l_[:, k, :], start=False, stop=False)
            for k in range(KD):
                pe.wait_ge(t_lo, KD * 3 + k + 1)
                for t in range(NT):
                    ins = pe.matmul(bank[4 + t][:, 0:third], xl[:, k, t * P:(t + 1) * P], h_[:, k, :], start=False,
                                    stop=k == KD - 1)
            ins.then_inc(block_used, 1)
            tokens("down1", 4, third, xh, xl, at_col=third)
            tokens("down2", 2, third, xh, xl, at_col=0)

            def turn_latents(half):
                for f in (2 * half, 2 * half + 1):
                    pe.wait_ge(mla_scaled, 2 if f < 3 else 4)
                    for t in range(NT):
                        ins = pe.transpose(bank[4 + f // 2][:, (f % 2) * SEQ + t * P:(f % 2) * SEQ + (t + 1) * P],
                                           ds[:, t, f * P:(f + 1) * P], ident)
                ins.then_inc(cq_t, 1)

            mem_block(2, lambda: turn_latents(0))
            turn_latents(1)
            hw = NOPE + ROPE
            for b, nh in enumerate((3, 3, 2)):
                h_, l_ = weights(f"uq{b}", 3, nh * hw)
                for i in range(nh):
                    h = 3 * b + i
                    if h >= 4 and h % 2 == 0:
                        pe.wait_ge(qk_out, h // 2 - 1)
                    for k in range(3):
                        if h in (0, 2):
                            pe.wait_ge(cq_lo, max(k + 1, 2) if h == 0 else 4)
                        ins = three(bank[4 + (h % 4) // 2][:, (h % 2) * SEQ:(h % 2 + 1) * SEQ],
                                    h_[:, k, i * hw:i * hw + NOPE], l_[:, k, i * hw:i * hw + NOPE],
                                    xh[:, k, :], xl[:, k, :], k == 0, k == 2)
                    if h % 2:
                        ins.then_inc(qk_mm, 1)
                for t in range(NT):
                    for k in range(3):
                        def rp(v):
                            return v[:, k, :].rearrange("p (h c) -> p h c", c=hw)[:, :, NOPE:hw]
                        ins = three(bank[t][:, 3 * b * ROPE:(3 * b + nh) * ROPE], xh[:, k, t * P:(t + 1) * P],
                                    xl[:, k, t * P:(t + 1) * P], rp(h_), rp(l_), k == 0, k == 2)
                ins.then_inc(block_used, 1)
                if b == 0:
                    pe.wait_ge(kr_done, 2)
                    for t in range(NT):
                        ins = pe.transpose(bank[6][:, t * P:(t + 1) * P], kr[:, t, :], ident)
                    ins.then_inc(kr_t, 1)
            h_, l_ = weights("ukv", 1, 2048)
            pe.wait_ge(kr_out, 1)
            for h in range(HEADS):
                if h % 2 == 0:
                    pe.wait_ge(qk_out, 3 + h // 2)
                a = 2 * P * h
                ins = three(bank[4 + (h % 4) // 2][:, (h % 2) * SEQ:(h % 2 + 1) * SEQ], h_[:, 0, a:a + P], l_[:, 0, a:a + P],
                            xh[:, 3, :], xl[:, 3, :], True, True)
                if h % 2:
                    ins.then_inc(qk_mm, 1)
            for i in range(4):
                t, hv = i // 2, i % 2
                if i == 3:
                    pe.wait_ge(mem_out, 3)

                def vp(v):
                    return v[:, 0, :].rearrange("p (h c) -> p h c", c=2 * P)[:, 4 * hv:4 * hv + 4, P:2 * P]
                ins = three(bank[VALUE_BANK[i]][:, :], xh[:, 3, t * P:(t + 1) * P], xl[:, 3, t * P:(t + 1) * P],
                            vp(h_), vp(l_), True, True)
                if i < 3:
                    ins.then_inc(v_mm, 1)
            ins.then_inc(block_used, 1)
            pe.wait_ge(qr_done, 2)
            for i in range(4):
                for t in range(NT):
                    ins = pe.transpose(bank[i // 2][:, (i % 2) * SEQ + t * P:(i % 2) * SEQ + (t + 1) * P],
                                       qr[:, t, i * P:(i + 1) * P], ident)
                if i % 2:
                    ins.then_inc(qr_t, 1)
            pe.wait_ge(qr_out, 2)
            pe.wait_ge(qk_out, HEADS)

            def mla_scores(h):
                if h >= 2:
                    pe.wait_ge(s_max, h - 1)
                half = slice((h % 2) * ROPE, (h % 2 + 1) * ROPE)
                for t, (a, b, keys) in enumerate(((0, P, P), (P, 3 * P, SEQ))):
                    o = bank[4 + h % 2][:, a:b]
                    tok = slice(t * P, (t + 1) * P)
                    pe.matmul(o, qn[:, h, tok], kn[:, h, 0:keys], start=True, stop=False)
                    ins = pe.matmul(o, qrt[half, h // 2, tok], krt[half, 0:keys], start=False, stop=True)
                ins.then_inc(s_mm, 1)

            def mla_pt(h):
                pe.wait_ge(s_norm, 2 * h + 2)
                if h >= 1:
                    pe.wait_ge(p_out, h)
                for i, a in enumerate((0, P, 2 * P)):
                    ins = pe.transpose(bank[6][:, i * P:(i + 1) * P], sc[h % 2][:, a:a + P], ident)
                ins.then_inc(p_t, 1)

            def mla_pv(h):
                pe.wait_ge(p_out, h + 1)
                if h >= 1:
                    pe.wait_ge(o_lo, h)
                o = (h % 2) * SEQ
                pe.matmul(bank[7][:, o:o + SEQ], vv[:, 0, h * P:(h + 1) * P], pt[h % 2][:, 0:SEQ], start=True, stop=True)
                pe.matmul(bank[7][:, o + P:o + SEQ], vv[:, 1, h * P:(h + 1) * P], pt[h % 2][:, SEQ:SEQ + P], start=False,
                          stop=True, skip_group_check=True).then_inc(o_mm, 1)

            pe.wait_ge(mem_out, 3)
            mla_scores(0)
            mla_scores(1)
            pe.wait_ge(v_out, 4)
            for h in range(HEADS):
                mla_pt(h)
                if h + 2 < HEADS:
                    mla_scores(h + 2)
                mla_pv(h)
                if h >= 2:
                    i = h // 2 - 1
                    pe.wait_ge(o_lo, 2 * i + 2)
                    row_block(f"wo{i}", i, xh, xl, i == 0, False, (h % 2,), h % 2 == 1)
            pe.wait_ge(o_lo, HEADS)
            row_block("wo3", 3, xh, xl, False, True)
            mem_block(3)
            norm(3, 12)
            ffn(1, 4)
            mem_block(4)
            norm(4, 16)
            mem_block(5)
            pe.wait_ge(t_lo, KD * 6)
            columns("z_a", 0, xh, xl)
            columns("z_gt", 1, xh, xl)
            tokens("z_v", 2, GW, xh, xl)
            tokens("z_u", 3, GW, xh, xl)
            pe.wait_ge(hc_done, 1)
            columns("z_kcvc", 0, xh, xl)
            columns("z_q0", 1, xh, xl)
            pe.wait_ge(gz_d, 3)
            columns("z_q1", 2, xh, xl)
            pe.wait_ge(fl_done, 2)
            pe.wait_ge(z_ws, 48)
            pe.wait_ge(mem_out, 6)
            for a in range(2):
                for k in range(CMP_KT):
                    ins = pe.matmul(bank[7][0:DH, 30 * a:30 * a + 30], cw1[:, a, k, :],
                                    fl[:, a, k, :, :].rearrange("p g n -> p (g n)"), start=k == 0, stop=k == CMP_KT - 1)
            ins.then_inc(cmp_mm, 1)
            pe.wait_ge(gz_d, 6)
            columns("z_ksw", 3, xh, xl)
            pe.wait_ge(cmp_d, 3)
            for g in range(GROUPS):
                pe.matmul(bank[7][g * DH:(g + 1) * DH, 64:64 + NCMP], cw2[:, 0, :], hg[:, 3, g * NCMP:(g + 1) * NCMP],
                          start=True, stop=True)
            for g in range(GROUPS):
                ins = pe.matmul(bank[7][0:NCMP, 128 + g * DH:128 + (g + 1) * DH],
                                hg[:, 3, 30 + g * NCMP:30 + (g + 1) * NCMP], cw2[:, 1, :], start=True, stop=True)
            ins.then_inc(cmp_mm, 1)
            tokens("z_vsw", 6, 2 * P, xh, xl)
            pe.wait_ge(z_out, 4)
            pe.wait_ge(cmp_out, 2)
            for g in range(GROUPS):
                rows_ = slice(g * DH, (g + 1) * DH)
                for t, j in ((t, j) for t in range(NT) for j in range(REP)):
                    c = (t * REP + j) * NCMP
                    ins = pe.matmul(bank[g][:, c:c + NCMP], qt[rows_, j, t * P:(t + 1) * P], kcm[rows_, :], start=True,
                                    stop=True)
                ins.then_inc(sc_mm, 1)
            h_, l_ = weights("z_gl", KD, 24)
            for k in range(KD):
                ins = three(bank[2][0:24, 0:SEQ], h_[:, k, :], l_[:, k, :], xh[:, k, :], xl[:, k, :], k == 0,
                            k == KD - 1)
            ins.then_inc(block_used, 1)
            pe.wait_ge(ws_cut, 1)
            pe.wait_ge(z_out, 5)
            for g in range(GG):
                ins = pe.transpose(bank[3][:, g * P:(g + 1) * P], ws[:, g * P:(g + 1) * P], ident)
            ins.then_inc(ws_t, 1)

            def nsa_scores(u):
                if u >= 2:
                    pe.wait_ge(n_max, u - 1)
                h, br = u // 2, u % 2
                g, j = h // REP, h % REP
                rows_ = slice(g * DH, (g + 1) * DH)
                for t, (a, b, keys) in enumerate(((0, P, P), (P, 3 * P, SEQ))):
                    ins = pe.matmul(bank[4 + u % 2][:, a:b], qt[rows_, j, t * P:(t + 1) * P], ksw[rows_, br, 0:keys],
                                    start=True, stop=True)
                ins.then_inc(n_mm, 1)

            nsa_scores(0)
            pe.wait_ge(gl_a, 1)
            for t in range(NT):
                ins = pe.transpose(bank[2][:, SEQ + t * 24:SEQ + (t + 1) * 24], glf[:, t * P:(t + 1) * P],
                                   con[0:24, K_ID:K_ID + 24])
            ins.then_inc(gl_t, 1)
            nsa_scores(1)
            pe.wait_ge(z_out, 6)
            pe.wait_ge(ws_out, 1)
            pe.wait_ge(vn_done, 3)
            for t in range(NT):
                pe.matmul(bank[7][:, t * GW:(t + 1) * GW], bsr[:, :], con[0:GG, K_SEL:K_SEL + GW], start=True, stop=False,
                          skip_group_check=True)
                for g in range(GG):
                    o = t * GW + g * GW // GG
                    ins = pe.matmul(bank[7][:, o:o + GW // GG], wst[:, g, :], vg[:, t, g * GW // GG:(g + 1) * GW // GG], start=False,
                                    stop=g == GG - 1, skip_group_check=True)
            ins.then_inc(mix_mm, 1)
            pe.wait_ge(pc_done, 1)
            for t in range(NT):
                pe.transpose(bank[6][0:120, t * P:(t + 1) * P], cm[3][:, t * 120:(t + 1) * 120], ident).then_inc(pc_t, 1)
            pe.wait_ge(pc_out, 1)
            pe.wait_ge(vbd_set, 16 * NSA_HEADS)
            pe.wait_ge(gz_d, 6)
            for t in range(NT):
                pe.matmul(bank[t][:, :], e1[0:120, t * P:(t + 1) * P], vbd[0:120, :], start=True, stop=False,
                          skip_group_check=True)

            def nsa_pt(u):
                pe.wait_ge(n_norm, 2 * u + 2)
                if u >= 1:
                    pe.wait_ge(n_out, u)
                for i, a in enumerate((0, P, 2 * P)):
                    ins = pe.transpose(bank[6][:, i * P:(i + 1) * P], s2[u % 2][:, a:a + P], ident)
                ins.then_inc(n_t, 1)

            def nsa_pv(u):
                h, br = u // 2, u % 2
                g = h // REP
                pe.wait_ge(n_out, u + 1)
                p_ = p2[u % 2]
                v0 = vsw[:, 0, br * P + g * DH:br * P + (g + 1) * DH]
                v1 = vsw[:, 1, br * P + g * DH:br * P + (g + 1) * DH]
                hs = slice(h * DH, (h + 1) * DH)
                last = u == 2 * NSA_HEADS - 1
                pe.matmul(bank[0][:, hs], p_[:, 0:P], v0, start=False, stop=last, skip_group_check=True)
                pe.matmul(bank[1][:, hs], p_[:, P:2 * P], v0, start=False, stop=False, skip_group_check=True)
                pe.matmul(bank[1][:, hs], p_[:, 2 * P:3 * P], v1, start=False, stop=last, skip_group_check=True) \
                  .then_inc(o_all, 1)

            def mem_part(i, first):
                if first == 0:
                    pe.wait_ge(*((gy_done, 2) if i == 6 else (mem_out, i)))
                h_, l_ = weights(f"mem{i}", KD, 2 * P)
                groups = [(t, k) for t in range(NT) for k in range(KD)]
                for t, k in groups[first:first + MEM_PER_STEP]:
                    ins = three(bank[7][:, t * 2 * P:(t + 1) * 2 * P], mh[:, k, t * P:(t + 1) * P],
                                ml[:, k, t * P:(t + 1) * P], h_[:, k, :], l_[:, k, :], k == 0, k == KD - 1)
                if first + MEM_PER_STEP >= len(groups):
                    ins.then_inc(block_used, 1)

            for u in range(2 * NSA_HEADS):
                nsa_pt(u)
                if u + 2 < 2 * NSA_HEADS:
                    nsa_scores(u + 2)
                for i in (6, 7):
                    if U_MEM[i] <= u < U_MEM[i] + MEM_STEPS:
                        mem_part(i, MEM_PER_STEP * (u - U_MEM[i]))
                nsa_pv(u)
                if u == U_TURN:
                    pe.wait_ge(cv_tap, len(VECTOR_TAPS))
                    for t in range(NT):
                        for c in range(2):
                            ins = pe.transpose(bank[3][:, t * CW_ + c * P:t * CW_ + (c + 1) * P],
                                               yc[:, c, t * P:(t + 1) * P], ident)
                    ins.then_inc(ycs_t, 1)
                if u == U_TURN_Y:
                    pe.wait_ge(y_scaled, 4)
                    turn(yn, 0, range(4, KD))
            pe.wait_ge(t_lo, KD * 6 + 4)

            row_block("wout2", 2, xh, xl, True, False, (1,), False)
            row_block("wout3", 3, xh, xl, False, False, (1,), False)
            pe.wait_ge(y_scaled, 6)
            turn(yn, 4, range(4))
            row_block("wout2", 2, xh, xl, True, False, (0,))
            row_block("wout3", 3, xh, xl, False, False, (0,))
            pe.wait_ge(t_lo, KD * 7)
            row_block("wout0", 0, xh, xl, False, False)
            row_block("wout1", 1, xh, xl, False, True)
            norm(5, 20)
            pe.wait_ge(mem_out, 8)

            def x_q(h):
                if h == 3:
                    pe.wait_ge(q_out, 2)
                columns(f"xq{h}", QUERY_BANK[h], xh, xl)

            def x_scores(h):
                pe.wait_ge(q_out, h + 1)
                if h >= 2:
                    pe.wait_ge(a_exp, 2 * h - 2)
                for t in range(NT):
                    for f in range(2):
                        ins = pe.matmul(bank[4 + h % 2][:, t * SEQ:(t + 1) * SEQ], qx[:, 2 * h + f, t * P:(t + 1) * P],
                                        km[:, 2 * h + f, :], start=f == 0, stop=f == 1)
                ins.then_inc(a_mm, 1)

            def x_pt(h):
                pe.wait_ge(a_norm, 2 * h + 2)
                if h >= 1:
                    pe.wait_ge(a_out, h)
                for kt in range(NT):
                    for t in range(NT):
                        ins = pe.transpose(bank[6][:, kt * SEQ + t * P:kt * SEQ + (t + 1) * P],
                                           sx[h % 2][:, t, kt * P:(kt + 1) * P], ident)
                ins.then_inc(a_t, 1)

            def x_pv(h):
                pe.wait_ge(a_out, h + 1)
                if h >= 1:
                    pe.wait_ge(ao_lo, h)
                for f in range(2):
                    for kt in range(NT):
                        c = h * XHD + f * P
                        ins = pe.matmul(bank[7][:, f * SEQ:(f + 1) * SEQ], vm[:, kt, c:c + P], px[h % 2][:, kt, :],
                                        start=kt == 0, stop=kt == NT - 1)
                ins.then_inc(ao_mm, 1)

            first_product(at["xq0"], QUERY_BANK[0], 7)
            x_q(1)
            x_scores(0)
            for h in range(XHEADS):
                if h + 2 < XHEADS:
                    x_q(h + 2)
                else:
                    pe.wait_ge(q_out, XHEADS)
                    pe.wait_ge(ao_lo, h - 1)
                    row_block(f"xo{h - 2}", h - 2, mh, ml, h == 2, False)
                x_pt(h)
                if h + 1 < XHEADS:
                    x_scores(h + 1)
                else:
                    pe.wait_ge(ao_lo, h)
                    row_block("xo2", 2, mh, ml, False, False, (0,), False)
                x_pv(h)
            row_block("xo2", 2, mh, ml, False, False, (1,))
            pe.wait_ge(ao_lo, XHEADS)
            row_block("xo3", 3, mh, ml, False, True)
            norm(6, 24)
            ffn(2, 8)


INPUTS = (
    "x", "positions", "norm_mix", "norm_ffn", "norm_final", "pool_w", "pool_scale", "mla_w_down", "mla_q_norm",
    "mla_w_uq", "mla_kv_norm", "mla_w_ukv", "mla_w_o", "ffn_w_gate", "ffn_w_up", "ffn_w_down", "mem_2",
    "mix_norm_g_2", "w_in_2", "cmp_pe_2", "cmp_w1_2", "cmp_w2_2", "gmlp_ln_g_2", "gmlp_ln_b_2", "gmlp_ws_2",
    "gmlp_bs_2", "conv_dw_w_2", "conv_dw_b_2", "conv_ln_g_2", "conv_ln_b_2", "mix_out_g_2", "w_out_2",
    "xattn_norm_g_2", "mem_norm_g_2", "xattn_wq_2", "xattn_wk_2", "xattn_wv_2", "xattn_wo_2", "ffn_norm_g_2",
    "ffn_w_up_2", "ffn_dw_w_2", "ffn_dw_b_2", "ffn_w_down_2", "final_norm_g_2",
)


def kernel(**inputs):
    import numpy as _np
    import concourse.bacc as _bacc
    from concourse import mybir as _mybir
    from concourse.bass_utils import run_bass_kernel_spmd as _run

    nc = _bacc.Bacc("TRN2", target_bir_lowering=False, num_devices=1)
    arrays, w = {}, {}
    for name in INPUTS:
        a = _np.ascontiguousarray(inputs[name])
        arrays[f"in_{name}"] = a
        w[name] = nc.dram_tensor(f"in_{name}", a.shape, _mybir.dt.from_np(a.dtype), kind="ExternalInput").ap()
    extra = []
    for name, a in zip(("consts", "bands"), constants()):
        arrays[f"in_{name}"] = a
        extra.append(nc.dram_tensor(f"in_{name}", a.shape, _mybir.dt.from_np(a.dtype), kind="ExternalInput").ap())
    out = nc.dram_tensor("out_x", (1, SEQ, D), F32, kind="ExternalOutput").ap()
    build(nc, w, *extra, out)
    r = _run(nc, [arrays], core_ids=[0])
    return r.results[0]["out_x"]
```
